# Optimizing a Trainium2 kernel written in Bass

```python
import jax, jax.numpy as jnp
from jax import lax
import numpy as np

D_MODEL = 1024
BATCH = 1
SEQ = 512
DEPTH = 2

CHUNK = 64
N_MIXERS = 2
GLA_HEADS = 4
GLA_DK = D_MODEL // 2
GLA_DV = D_MODEL
GLA_DK_HEAD = GLA_DK // GLA_HEADS
GLA_DV_HEAD = GLA_DV // GLA_HEADS
GLA_GATE_RANK = 16
GLA_GATE_TAU = 16.0
GLA_IN_WIDTH = 2 * GLA_DK + 2 * GLA_DV + GLA_GATE_RANK
ATT_HEADS = 16
ATT_HEAD_DIM = D_MODEL // ATT_HEADS
LEFT_CHUNKS = 8
BAND = (LEFT_CHUNKS + 1) * CHUNK
MAX_REL = 128
N_REL = 2 * MAX_REL + 1
D_FF = 4 * D_MODEL
DEEPNORM_ALPHA = (2.0 * DEPTH) ** 0.25
DEEPNORM_BETA = (8.0 * DEPTH) ** -0.25
LN_EPS = 1e-5
RMS_EPS = 1e-6
NEG_INF = -1e30
N_GLA_LAYERS = (DEPTH + 1) // 2
N_ATT_LAYERS = DEPTH // 2


def layer_norm(x, g, b):
    xf = x.astype(jnp.float32)
    mu = jnp.mean(xf, -1, keepdims=True)
    var = jnp.mean(jnp.square(xf - mu), -1, keepdims=True)
    return ((xf - mu) * lax.rsqrt(var + LN_EPS)).astype(x.dtype) * g + b

def gla_mixer(u, w_in, w_gk2, b_gk, g_norm, w_out):
    B_, S_, _ = u.shape
    nC = S_ // CHUNK
    proj = u @ w_in
    q, k, v, g, gk_lr = jnp.split(
        proj, [GLA_DK, 2 * GLA_DK, 2 * GLA_DK + GLA_DV, 2 * GLA_DK + 2 * GLA_DV], axis=-1)
    log_a = jax.nn.log_sigmoid((gk_lr @ w_gk2 + b_gk).astype(jnp.float32)) / GLA_GATE_TAU

    def to_chunks(t, hd):
        return t.reshape(B_, nC, CHUNK, GLA_HEADS, hd).transpose(0, 3, 1, 2, 4)

    qc = to_chunks(q.astype(jnp.float32), GLA_DK_HEAD) * (GLA_DK_HEAD ** -0.5)
    kc = to_chunks(k.astype(jnp.float32), GLA_DK_HEAD)
    vc = to_chunks(v.astype(jnp.float32), GLA_DV_HEAD)
    cum = jnp.cumsum(to_chunks(log_a, GLA_DK_HEAD), axis=3)
    e_pos = jnp.exp(cum)
    e_neg = jnp.exp(-cum)
    q_fwd = qc * e_pos
    a_fwd = jnp.einsum('bhntd,bhnsd->bhnts', q_fwd, kc * e_neg)
    a_bwd = jnp.einsum('bhntd,bhnsd->bhnts', qc * e_neg, kc * e_pos)
    lower = jnp.tril(jnp.ones((CHUNK, CHUNK), dtype=bool))
    o_intra = jnp.einsum('bhnts,bhnsv->bhntv', jnp.where(lower, a_fwd, a_bwd), vc)
    k_to_end = kc * jnp.exp(cum[:, :, :, -1:, :] - cum)
    chunk_decay = jnp.exp(cum[:, :, :, -1, :])

    def step(state, inp):
        qs, ke, vv, dec = inp
        o = jnp.einsum('bhtk,bhkv->bhtv', qs, state)
        state = state * dec[..., None] + jnp.einsum('bhtk,bhtv->bhkv', ke, vv)
        return state, o

    s0 = jnp.zeros((B_, GLA_HEADS, GLA_DK_HEAD, GLA_DV_HEAD), jnp.float32)
    _, o_inter = lax.scan(step, s0, (jnp.moveaxis(q_fwd, 2, 0), jnp.moveaxis(k_to_end, 2, 0),
                                     jnp.moveaxis(vc, 2, 0), jnp.moveaxis(chunk_decay, 2, 0)))
    o = o_intra + jnp.moveaxis(o_inter, 0, 2)
    o = o * lax.rsqrt(jnp.mean(jnp.square(o), -1, keepdims=True) + RMS_EPS)
    o = o * g_norm.astype(jnp.float32)[None, :, None, None, :]
    o = o.transpose(0, 2, 3, 1, 4).reshape(B_, S_, GLA_DV).astype(u.dtype)
    return (o * jax.nn.silu(g)) @ w_out

def chunk_attention(u, w_in, b_in, rel_bias, w_out):
    B_, S_, _ = u.shape
    nC = S_ // CHUNK
    q, k, v = jnp.split(u @ w_in + b_in, 3, axis=-1)

    def heads(t):
        return t.reshape(B_, S_, ATT_HEADS, ATT_HEAD_DIM).transpose(0, 2, 1, 3)

    pad = LEFT_CHUNKS * CHUNK
    qc = (heads(q) * (ATT_HEAD_DIM ** -0.5)).reshape(B_, ATT_HEADS, nC, CHUNK, ATT_HEAD_DIM)
    kp = jnp.pad(heads(k), ((0, 0), (0, 0), (pad, 0), (0, 0)))
    vp = jnp.pad(heads(v), ((0, 0), (0, 0), (pad, 0), (0, 0)))
    key_valid = jnp.arange(S_ + pad) >= pad
    rel = jnp.clip(pad + jnp.arange(CHUNK)[:, None] - jnp.arange(BAND)[None, :], -MAX_REL, MAX_REL) + MAX_REL
    bias = rel_bias.astype(jnp.float32)[:, rel]

    def one_chunk(inp):
        qi, start = inp
        kb = lax.dynamic_slice_in_dim(kp, start, BAND, axis=2)
        vb = lax.dynamic_slice_in_dim(vp, start, BAND, axis=2)
        mb = lax.dynamic_slice_in_dim(key_valid, start, BAND)
        s = jnp.einsum('bhtd,bhjd->bhtj', qi, kb).astype(jnp.float32) + bias
        p = jax.nn.softmax(jnp.where(mb, s, NEG_INF), axis=-1).astype(vb.dtype)
        return jnp.einsum('bhtj,bhjd->bhtd', p, vb)

    o = lax.map(one_chunk, (jnp.moveaxis(qc, 2, 0), jnp.arange(nC) * CHUNK))
    o = o.transpose(1, 0, 3, 2, 4).reshape(B_, S_, D_MODEL)
    return o @ w_out

def squared_relu_mlp(u, w1, w2):
    return jnp.square(jax.nn.relu(u @ w1)) @ w2

def first_inputs(seed: int = 0) -> dict:
    key = jax.random.key(seed)
    ks = jax.random.split(key, 16)
    nrm = lambda k, shape, s: jax.random.normal(k, shape, jnp.float32) * s
    D = D_MODEL
    return {
        "x": nrm(ks[0], (BATCH, SEQ, D), 1.0),
        "c": nrm(ks[1], (BATCH, D), 1.0),
        "w_ada": nrm(ks[2], (DEPTH, D, 6 * D), 0.1 * D ** -0.5),
        "b_ada": nrm(ks[3], (DEPTH, 6 * D), 0.02),
        "ln_g": 1.0 + nrm(ks[4], (DEPTH, 2, D), 0.02),
        "ln_b": nrm(ks[5], (DEPTH, 2, D), 0.02),
        "gla_w_in": nrm(ks[6], (N_GLA_LAYERS, D, GLA_IN_WIDTH), D ** -0.5),
        "gla_w_gk2": nrm(ks[7], (N_GLA_LAYERS, GLA_GATE_RANK, GLA_DK), GLA_GATE_RANK ** -0.5),
        "gla_b_gk": nrm(ks[8], (N_GLA_LAYERS, GLA_DK), 0.1),
        "gla_g_norm": 1.0 + nrm(ks[9], (N_GLA_LAYERS, GLA_HEADS, GLA_DV_HEAD), 0.02),
        "gla_w_out": nrm(ks[10], (N_GLA_LAYERS, GLA_DV, D), DEEPNORM_BETA * GLA_DV ** -0.5),
        "att_w_in": nrm(ks[11], (N_ATT_LAYERS, D, 3 * D), D ** -0.5),
        "att_b_in": nrm(ks[12], (N_ATT_LAYERS, 3 * D), 0.02),
        "att_rel_bias": nrm(ks[13], (N_ATT_LAYERS, ATT_HEADS, N_REL), 0.2),
        "att_w_out": nrm(ks[14], (N_ATT_LAYERS, D, D), DEEPNORM_BETA * D ** -0.5),
        "ff_w1": nrm(jax.random.fold_in(ks[15], 0), (DEPTH, D, D_FF), D ** -0.5),
        "ff_w2": nrm(jax.random.fold_in(ks[15], 1), (DEPTH, D_FF, D), DEEPNORM_BETA * D_FF ** -0.5),
    }

def first_block(x, c, w_ada, b_ada, ln_g, ln_b, gla_w_in, gla_w_gk2, gla_b_gk, gla_g_norm, gla_w_out,
              att_w_in, att_b_in, att_rel_bias, att_w_out, ff_w1, ff_w2):
    c_act = jax.nn.silu(c)
    for i in range(DEPTH):
        mods = jnp.split(c_act @ w_ada[i] + b_ada[i], 6, axis=-1)
        sh1, sc1, g1, sh2, sc2, g2 = [m[:, None, :] for m in mods]
        u = x * (1.0 + sc1) + sh1
        j = i // N_MIXERS
        if i % N_MIXERS == 0:
            y = gla_mixer(u, gla_w_in[j], gla_w_gk2[j], gla_b_gk[j], gla_g_norm[j], gla_w_out[j])
        else:
            y = chunk_attention(u, att_w_in[j], att_b_in[j], att_rel_bias[j], att_w_out[j])
        x = layer_norm(DEEPNORM_ALPHA * x + (1.0 + g1) * y, ln_g[i, 0], ln_b[i, 0])
        u = x * (1.0 + sc2) + sh2
        y = squared_relu_mlp(u, ff_w1[i], ff_w2[i])
        x = layer_norm(DEEPNORM_ALPHA * x + (1.0 + g2) * y, ln_g[i, 1], ln_b[i, 1])
    return x


HGRN_HEADS = 4
HGRN_KEY = 128
HGRN_VAL = 128
HGRN_KW = HGRN_HEADS * HGRN_KEY
HGRN_VW = HGRN_HEADS * HGRN_VAL
HGRN_CHUNK = 64
POOL_WINDOWS = (2, 4, 8, 16)
POOL_GROUP = 128
POOL_WIDTH = POOL_GROUP * len(POOL_WINDOWS)
FOX_HEADS = 16
FOX_HEAD_DIM = 64
FOX_WIDTH = FOX_HEADS * FOX_HEAD_DIM
FOX_BLOCK = 128
EVEN_IN = 2 * HGRN_KW + 2 * HGRN_VW + 2 * POOL_WIDTH
EVEN_MIX = HGRN_VW + POOL_WIDTH
ODD_IN = 4 * FOX_WIDTH + FOX_HEADS
N_EVEN = (DEPTH + 1) // 2
N_ODD = DEPTH // 2
EPS = 1e-6


def rms_norm(x, g):
    xf = x.astype(jnp.float32)
    y = xf * lax.rsqrt(jnp.mean(xf * xf, axis=-1, keepdims=True) + EPS)
    return (y * g.astype(jnp.float32)).astype(x.dtype)

def hgrn2_chunked(q, k, v, logf):
    b_, s_, h_, kd = q.shape
    vd = v.shape[-1]
    nc = s_ // HGRN_CHUNK

    def to_chunks(t):
        return t.reshape(b_, nc, HGRN_CHUNK, h_, t.shape[-1]).transpose(1, 0, 3, 2, 4)

    causal = jnp.tril(jnp.ones((HGRN_CHUNK, HGRN_CHUNK), dtype=bool))

    def step(state, inp):
        qc, kc, vc, gc = inp
        cum = jnp.cumsum(gc, axis=2)
        diff = cum[:, :, :, None, :] - cum[:, :, None, :, :]
        decay = jnp.where(causal[:, :, None], jnp.exp(jnp.minimum(diff, 0.0)), 0.0)
        scores = jnp.einsum('bhtk,bhsk,bhtsk->bhts', qc, kc, decay)
        out = (jnp.einsum('bhts,bhsv->bhtv', scores, vc)
               + jnp.einsum('bhtk,bhkv->bhtv', qc * jnp.exp(cum), state))
        last = cum[:, :, -1:, :]
        state = (jnp.exp(last[:, :, 0, :])[..., None] * state
                 + jnp.einsum('bhsk,bhsv->bhkv', kc * jnp.exp(last - cum), vc))
        return state, out

    s0 = jnp.zeros((b_, h_, kd, vd), jnp.float32)
    _, out = lax.scan(step, s0, (to_chunks(q), to_chunks(k), to_chunks(v), to_chunks(logf)))
    return out.transpose(1, 0, 3, 2, 4).reshape(b_, s_, h_, vd)

def multiscale_pool(u):
    b_, s_, _ = u.shape
    groups = u.reshape(b_, s_, len(POOL_WINDOWS), POOL_GROUP)
    csum = jnp.cumsum(groups, axis=1)
    csum = jnp.concatenate([jnp.zeros_like(csum[:, :1]), csum], axis=1)
    pos = jnp.arange(s_)
    outs = []
    for gi, w in enumerate(POOL_WINDOWS):
        cg = csum[:, :, gi]
        lagged = jnp.concatenate([jnp.zeros((b_, w - 1, POOL_GROUP), cg.dtype), cg[:, :s_ - w + 1]], axis=1)
        count = jnp.minimum(pos + 1, w).astype(cg.dtype)[None, :, None]
        outs.append((cg[:, 1:] - lagged) / count - groups[:, :, gi])
    return jnp.stack(outs, axis=2)

def even_mixer(h, w_in, lower, onorm_g, pool_w, pool_scale, w_out):
    b_, s_, _ = h.shape
    proj = (h @ w_in).astype(jnp.float32)
    cuts = [HGRN_KW, 2 * HGRN_KW, 2 * HGRN_KW + HGRN_VW, 2 * HGRN_KW + 2 * HGRN_VW,
            2 * HGRN_KW + 2 * HGRN_VW + POOL_WIDTH]
    q, f, i, g_a, u, g_b = jnp.split(proj, cuts, axis=-1)
    lb = lower.astype(jnp.float32)
    forget = lb + (1.0 - lb) * jax.nn.sigmoid(f)
    logf = jnp.log(forget)
    key = 1.0 - forget
    kh = lambda t: t.reshape(b_, s_, HGRN_HEADS, HGRN_KEY)
    o_a = hgrn2_chunked(kh(q), kh(key), i.reshape(b_, s_, HGRN_HEADS, HGRN_VAL), kh(logf))
    o_a = rms_norm(o_a, onorm_g.reshape(HGRN_HEADS, HGRN_VAL)).reshape(b_, s_, HGRN_VW) * jax.nn.silu(g_a)
    pooled = multiscale_pool(u)
    o_b = jnp.einsum('bsgc,gcd->bsgd', pooled, pool_w.astype(jnp.float32)).reshape(b_, s_, POOL_WIDTH)
    o_b = o_b * pool_scale.astype(jnp.float32) * jax.nn.silu(g_b)
    mixed = jnp.concatenate([o_a, o_b], axis=-1).astype(h.dtype)
    return mixed @ w_out

def odd_mixer(h, w_in, b_f, qnorm_g, knorm_g, w_out):
    b_, s_, _ = h.shape
    proj = (h @ w_in).astype(jnp.float32)
    q, k, v, g, fl = jnp.split(proj, [FOX_WIDTH, 2 * FOX_WIDTH, 3 * FOX_WIDTH, 4 * FOX_WIDTH], axis=-1)
    hd = lambda t: t.reshape(b_, s_, FOX_HEADS, FOX_HEAD_DIM)
    q = rms_norm(hd(q), qnorm_g).transpose(0, 2, 1, 3)
    k = rms_norm(hd(k), knorm_g).transpose(0, 2, 1, 3)
    v = hd(v).transpose(0, 2, 1, 3)
    logf = jax.nn.log_sigmoid(fl + b_f.astype(jnp.float32))
    cumf = jnp.cumsum(logf, axis=1).transpose(0, 2, 1)
    scale = FOX_HEAD_DIM ** -0.5
    outs = []
    for blk in range(s_ // FOX_BLOCK):
        q0 = blk * FOX_BLOCK
        q1 = q0 + FOX_BLOCK
        logits = (jnp.einsum('bhqd,bhkd->bhqk', q[:, :, q0:q1], k[:, :, :q1]) * scale
                  + cumf[:, :, q0:q1, None] - cumf[:, :, None, :q1])
        mask = jnp.arange(q0, q1)[:, None] >= jnp.arange(q1)[None, :]
        probs = jax.nn.softmax(jnp.where(mask, logits, -jnp.inf), axis=-1)
        outs.append(jnp.einsum('bhqk,bhkd->bhqd', probs, v[:, :, :q1]))
    o = jnp.concatenate(outs, axis=2).transpose(0, 2, 1, 3).reshape(b_, s_, FOX_WIDTH)
    o = o * jax.nn.silu(g)
    return o.astype(h.dtype) @ w_out

def second_inputs(seed: int = 0) -> dict:
    key = jax.random.key(seed)
    ks = jax.random.split(key, 16)
    nrm = jax.random.normal
    f32 = jnp.float32
    return {
        'x': nrm(ks[0], (BATCH, SEQ, D_MODEL), f32),
        'c': nrm(ks[1], (BATCH, D_MODEL), f32),
        'norm_g': 1.0 + 0.05 * nrm(ks[2], (DEPTH, D_MODEL), f32),
        'ada_w': 0.5 * D_MODEL ** -0.5 * nrm(ks[3], (DEPTH, D_MODEL, 3 * D_MODEL), f32),
        'ada_b': 0.02 * nrm(ks[4], (DEPTH, 3 * D_MODEL), f32),
        'hgrn_lb': 0.1 * nrm(ks[5], (DEPTH + 1, HGRN_KW), f32),
        'even_w_in': D_MODEL ** -0.5 * nrm(ks[6], (N_EVEN, D_MODEL, EVEN_IN), f32),
        'hgrn_onorm_g': 1.0 + 0.05 * nrm(ks[7], (N_EVEN, HGRN_VW), f32),
        'pool_w': POOL_GROUP ** -0.5 * nrm(ks[8], (N_EVEN, len(POOL_WINDOWS), POOL_GROUP, POOL_GROUP), f32),
        'pool_scale': 1.0 + 0.05 * nrm(ks[9], (N_EVEN, POOL_WIDTH), f32),
        'even_w_out': EVEN_MIX ** -0.5 * nrm(ks[10], (N_EVEN, EVEN_MIX, D_MODEL), f32),
        'odd_w_in': D_MODEL ** -0.5 * nrm(ks[11], (N_ODD, D_MODEL, ODD_IN), f32),
        'fox_b_f': jax.random.uniform(ks[12], (N_ODD, FOX_HEADS), f32, 1.0, 4.0),
        'fox_qnorm_g': 1.0 + 0.05 * nrm(ks[13], (N_ODD, FOX_HEAD_DIM), f32),
        'fox_knorm_g': 1.0 + 0.05 * nrm(ks[14], (N_ODD, FOX_HEAD_DIM), f32),
        'odd_w_out': FOX_WIDTH ** -0.5 * nrm(ks[15], (N_ODD, FOX_WIDTH, D_MODEL), f32),
    }

def second_block(x, c, norm_g, ada_w, ada_b, hgrn_lb, even_w_in, hgrn_onorm_g, pool_w, pool_scale,
              even_w_out, odd_w_in, fox_b_f, fox_qnorm_g, fox_knorm_g, odd_w_out):
    lower = jnp.cumsum(jax.nn.softmax(hgrn_lb.astype(jnp.float32), axis=0), axis=0)
    cond = jax.nn.silu(c)
    for l in range(DEPTH):
        mod = cond @ ada_w[l] + ada_b[l]
        shift, scale, gate = jnp.split(mod, 3, axis=-1)
        h = rms_norm(x, norm_g[l]) * (1.0 + scale[:, None, :]) + shift[:, None, :]
        j = l // 2
        if l % 2 == 0:
            y = even_mixer(h, even_w_in[j], lower[l], hgrn_onorm_g[j], pool_w[j], pool_scale[j], even_w_out[j])
        else:
            y = odd_mixer(h, odd_w_in[j], fox_b_f[j], fox_qnorm_g[j], fox_knorm_g[j], odd_w_out[j])
        x = x + gate[:, None, :] * y
    return x


def setup_inputs(seed=0):
    out = dict(first_inputs(seed))
    for name, value in second_inputs(seed + 1).items():
        if name != "x":
            out[name + "_2"] = value
    return out


def reference(
    x, c, w_ada, b_ada, ln_g, ln_b, gla_w_in, gla_w_gk2, gla_b_gk, gla_g_norm, gla_w_out,
    att_w_in, att_b_in, att_rel_bias, att_w_out, ff_w1, ff_w2, c_2, norm_g_2, ada_w_2, ada_b_2,
    hgrn_lb_2, even_w_in_2, hgrn_onorm_g_2, pool_w_2, pool_scale_2, even_w_out_2, odd_w_in_2,
    fox_b_f_2, fox_qnorm_g_2, fox_knorm_g_2, odd_w_out_2,
):
    x = first_block(
        x, c, w_ada, b_ada, ln_g, ln_b, gla_w_in, gla_w_gk2, gla_b_gk, gla_g_norm, gla_w_out,
        att_w_in, att_b_in, att_rel_bias, att_w_out, ff_w1, ff_w2,
    )
    return second_block(
        x, c_2, norm_g_2, ada_w_2, ada_b_2, hgrn_lb_2, even_w_in_2, hgrn_onorm_g_2, pool_w_2,
        pool_scale_2, even_w_out_2, odd_w_in_2, fox_b_f_2, fox_qnorm_g_2, fox_knorm_g_2,
        odd_w_out_2,
    )


_drawn_inputs = setup_inputs


def setup_inputs(seed=0):
    import zlib

    import numpy as np

    out = dict(_drawn_inputs(seed))
    spreads = {}
    factors = {'gla_b_gk': 6.422,
     'gla_g_norm': 8.0,
     'att_b_in': 7.44,
     'att_rel_bias': 7.17,
     'norm_g_2': 2.943,
     'ada_b_2': 2.992,
     'hgrn_lb_2': 7.488,
     'hgrn_onorm_g_2': 7.82,
     'pool_scale_2': 8.0,
     'fox_qnorm_g_2': 8.0,
     'fox_knorm_g_2': 8.0}
    for name, (base, spread) in spreads.items():
        noise = np.random.default_rng([zlib.crc32(name.encode()), seed]).standard_normal(out[name].shape)
        drawn = base * np.exp(spread * noise) if base else spread * noise
        out[name] = __import__('jax').numpy.asarray(drawn.astype(out[name].dtype))
    for name, factor in factors.items():
        out[name] = (out[name] * factor).astype(out[name].dtype)
    return out
```

```python
from contextlib import ExitStack

import concourse.bass as bass
from concourse import mybir

F32 = mybir.dt.float32
F32R = mybir.dt.float32r
U32 = mybir.dt.uint32
ALU = mybir.AluOpType
ACT = mybir.ActivationFunctionType
AX = mybir.AxisListType.X

P = 128
SEQ = 512
D = 1024
ST = SEQ // P
KT = D // P
COLS = 512
HK = 4
FF = 4 * D
FB = FF // COLS
CH = 64
NC = SEQ // CH
DEPTH = 2
ALPHA = (2.0 * DEPTH) ** 0.25
LN_EPS = 1e-5
RMS_EPS = 1e-6
GLA_H, GLA_DK, GLA_DV, GLA_R, GLA_TAU = 4, 128, 256, 16, 16.0
HEADS, HD = 16, 64
POOLS = (2, 4, 8, 16)
LEVELS = (32, 16, 8, 4, 2, 1)
REL = SEQ + P - 1
MAX_REL = 128
NEG = -1e30
AW = 6 * D // FB
RING = 4

ROWS = {}
_n = 0
for _name, _rows in [("b_ada", DEPTH * 48), ("ln_g", 32), ("ln_b", 32), ("gla_b_gk", 4), ("gla_g_norm", 8),
                     ("att_b_in", 24), ("norm_g_2", 16), ("ada_b_2", 48), ("hgrn_lb_2", 12), ("hgrn_onorm_g_2", 4),
                     ("pool_scale_2", 4), ("fox_qnorm_g_2", 1), ("fox_knorm_g_2", 1), ("c", 8), ("c_2", 8)]:
    ROWS[_name] = _n
    _n += _rows
NV = (_n + P - 1) // P


def build(nc, T, out):
    ctx = ExitStack()

    def sb(name, shape, dt=F32, where=None):
        return (where or ctx).enter_context(nc.sbuf_tensor(name, shape, dt))

    def sem(name):
        return ctx.enter_context(nc.semaphore(name))

    with ctx:
        bank = [ctx.enter_context(nc.psum_tensor(f"bank{i}", [P, COLS], F32)) for i in range(8)]

        raw = sb("raw", [P, 2, HK, COLS])
        wsp = sb("wsp", [P, 2, 2, HK, COLS], F32R)
        xT = sb("xT", [P, 2, KT, SEQ], F32R)
        x = sb("x", [P, ST, D])
        tok = sb("tok", [P, ST, D])
        u32 = sb("u32", [P, 2, SEQ])
        vrow = u32[:, :, :].rearrange("p a b -> p (a b)")[:, 0:NV * P].rearrange("p (t n) -> p t n", n=P)
        cols = sb("cols", [P, NV * P])
        ident = sb("ident", [P, P])
        ones = sb("ones", [P, P])
        gmask = sb("gmask", [P, P])
        cmask = sb("cmask", [P, P])
        lmask = sb("lmask", [P, len(LEVELS), P])
        rcnt = sb("rcnt", [P, max(POOLS)])
        rev = sb("rev", [P, P])
        bones = sb("bones", [P, P])
        csil = sb("csil", [P, 16])
        ctmp = sb("ctmp", [P, 16])
        modcol = sb("modcol", [P, 48])
        scol = sb("scol", [P, KT])
        bcol = sb("bcol", [P, KT])
        stats = sb("stats", [P, ST, 2, 6])
        mv = sb("mv", [P, ST, 2])
        rstd = sb("rstd", [P, ST])
        sd = sb("sd", [P, ST])
        ssq = sb("ssq", [P, ST])
        rms = sb("rms", [P, ST])
        w16 = sb("w16", [P, KT, GLA_R])

        first = ctx.enter_context(ExitStack())
        gate1 = sb("gate1", [P, D], where=first)
        gate2 = sb("gate2", [P, D], where=first)
        vec_ld = sem("vec_ld")

        def col(name, k=0, n=1):
            return cols[:, ROWS[name] + k:ROWS[name] + k + n]

        base, J = {}, 0
        PANELS = [("gla_in", 6), ("gla_out", 2), ("ff0", None), ("att_in", 6), ("att_out", 2), ("ff1", None),
                  ("even_in", 6), ("even_out", 2), ("odd_in", 8), ("odd_out", 2)]
        PANELS_N = dict(PANELS)
        for n, c in PANELS:
            base[n] = J
            J += 2 * c if c else 4 * FB
        kview = lambda w: w.rearrange("(k p) n -> p k n", p=P)
        W = {"gla_in": kview(T["gla_w_in"][0]), "gla_out": kview(T["gla_w_out"][0]),
             "att_in": kview(T["att_w_in"][0]), "att_out": kview(T["att_w_out"][0]),
             "even_in": kview(T["even_w_in_2"][0]), "even_out": kview(T["even_w_out_2"][0]),
             "odd_in": kview(T["odd_w_in_2"][0]), "odd_out": kview(T["odd_w_out_2"][0])}
        W1 = [kview(T["ff_w1"][l]) for l in range(DEPTH)]
        W2 = [kview(T["ff_w2"][l]) for l in range(DEPTH)]
        ADA = [kview(T["w_ada"][l]) for l in range(DEPTH)]

        raw_ld = [sem("raw_ld0"), sem("raw_ld1")]
        hi_made = sem("hi_made")
        lo_made = sem("lo_made")
        w_used = sem("w_used")
        dve_step = sem("dve_step")
        act_step = sem("act_step")
        const_made = sem("const_made")

        def sems(stage, *names):
            return [sem(f"{n}_{stage}") for n in names]

        shared = {n: sem(n) for n in ("tr_done", "u_made", "xT_ready")}
        TS = {}
        for n, _ in PANELS:
            s = {"in": "in_", "out": "mid_"}.get(n.split("_")[-1], "hid_") + n
            TS[s] = {"k0": KT * len(TS), "tok_ready": sem("tok_ready_" + s), "bank_free": sem("bank_free_" + s), **shared}
        tile_done, tile0, var_made, sd_made = sem("tile_done"), {}, sem("var_made"), sem("sd_made")
        for n, c in PANELS:
            if c:
                tile0[n] = 3 * sum(PANELS_N[m] for m in tile0)
        norm0 = {n: ST * i for i, n in enumerate(("gla_out", "ff0", "att_out", "ff1"))}
        FS = {}
        for n in ("ff0", "ff1"):
            names = ("ff1_tile", "relu_done", "sq_done", "hhi_done", "hT_ready", "ff2_tile", "acc_done", "ada_used")
            FS[n] = dict(zip(names, sems(n, *names)))
            FS[n]["ada_ld"] = sems(n, *[f"ada_ld{i}" for i in range(RING)])

        def sp_half(sp, j, slot, src, peel=False):
            if not peel:
                sp.wait_ge(lo_made, j - 1)
            sp.dma_start(raw[:, slot], src).then_inc(raw_ld[slot], 16)

        def sp_panels(sp, name, n, extra=None):
            w = W[name]
            b = base[name]
            peel = 1 if b == 0 else 0
            if peel:
                for h in range(2):
                    sp_half(sp, h, h, w[:, HK * h:HK * h + HK, 0:COLS], peel=True)
            with sp.Fori(peel, n) as i:
                for h in range(2):
                    sp_half(sp, b + 2 * i + h, h, w[:, HK * h:HK * h + HK, bass.ds(i * COLS, COLS)])

        def act_high(act, q, slot, peel=False):
            act.wait_ge(raw_ld[slot], 16 * q + 16)
            if not peel:
                act.wait_ge(w_used, 2 * q + slot - 1)
            act.activation(wsp[:, slot, 0], raw[:, slot], ACT.Copy).then_inc(hi_made, 1)

        def act_ahead(act, name, panel, half):
            q = base[name] // 2 + panel + 1
            if not isinstance(q, int) or q < J // 2:
                act_high(act, q, half)

        def pe_tile(pe, out_ap, slot, k, kk, t, kind, start, stop):
            for n, (a, b) in enumerate([(0, 0), (0, 1), (1, 0)]):
                w = wsp[:, slot, b, k, :]
                if kind == "T":
                    l, r = wsp[:, slot, b, k, t * P:t * P + P], xT[:, a, kk, :]
                else:
                    l, r = xT[:, a, kk, t * P:t * P + P], w
                mm = pe.matmul(out_ap, l, r, start=(start and n == 0), stop=(stop and n == 2))
            return mm

        def pe_panel(pe, j, bk, kind, free, free_at):
            for h in range(2):
                pe.wait_ge(lo_made, j + h + 1)
                if h == 0:
                    for t in range(4):
                        pe.wait_ge(free, free_at + t + 1)
                        for k in range(HK):
                            mm = pe_tile(pe, bank[bk + t][:, :], 0, k, k, t, kind, k == 0, False)
                    mm.then_inc(w_used, 1)
                else:
                    for t in range(4):
                        for k in range(HK):
                            mm = pe_tile(pe, bank[bk + t][:, :], 1, k, HK + k, t, kind, False, k == HK - 1)
                        mm.then_inc(tile_done if t < 3 else w_used, 1)

        def pe_panels(pe, name, ts, runs):
            s = TS[ts]
            pe.wait_ge(s["xT_ready"], s["k0"] + KT)
            i0 = 0
            for kind, pairs in runs:
                def pair(i):
                    for b in range(2):
                        pe_panel(pe, base[name] + 4 * i + 2 * b, 4 * b, kind[b], s["bank_free"], 8 * i + 4 * b)
                if pairs > 1:
                    with pe.Fori(i0, i0 + pairs) as i:
                        pair(i)
                else:
                    pair(i0)
                i0 += pairs

        def wait_tile(eng, name, panel, t):
            if t < 3:
                eng.wait_ge(tile_done, tile0[name] + 3 * panel + t + 1)
            else:
                eng.wait_ge(w_used, base[name] + 2 * panel + 2)

        def act_evac(act, name, ts, i, fn):
            for b in range(2):
                act_ahead(act, name, 2 * i + b, 0)
                for t in range(4):
                    if t == 3:
                        act_ahead(act, name, 2 * i + b, 1)
                    wait_tile(act, name, 2 * i + b, t)
                    fn(b, t, bank[4 * b + t]).then_inc(TS[ts]["bank_free"], 1)

        def pe_transposes(pe, ts, src, need, before_last=None):
            s = TS[ts]
            if need:
                pe.wait_ge(s["tok_ready"], need)
            for k in range(KT):
                if before_last and k == KT - 1:
                    before_last()
                for t in range(ST):
                    mm = pe.transpose(bank[k][:, t * P:t * P + P], src[:, t, k * P:k * P + P], ident[:, :])
                mm.then_inc(s["tr_done"], 1)

        def act_transposed(act, ts, scale, bias):
            s = TS[ts]
            for k in range(KT):
                act.wait_ge(s["tr_done"], s["k0"] + k + 1)
                if k >= 2:
                    act.wait_ge(s["xT_ready"], s["k0"] + k - 1)
                kw = {}
                if scale is not None:
                    kw["scale"] = scale(k)
                if bias is not None:
                    kw["bias"] = bias(k)
                act.activation(u32[:, k % 2], bank[k][:, :], ACT.Identity, **kw).then_inc(s["u_made"], 1)
                act.activation(xT[:, 0, k], bank[k][:, :], ACT.Identity, **kw).then_inc(s["bank_free"], 1)

        def dve_transposed(dve, ts):
            s = TS[ts]
            for k in range(KT):
                dve.wait_ge(s["u_made"], s["k0"] + k + 1)
                dve.wait_ge(s["bank_free"], k + 1)
                dve.tensor_tensor(xT[:, 1, k], u32[:, k % 2], xT[:, 0, k].bitcast(F32), ALU.subtract)\
                   .then_inc(s["xT_ready"], 1)

        dcount, acount = [0], [0]

        def dchain(dve, ins):
            ins.then_inc(dve_step, 1)
            dcount[0] += 1
            dve.wait_ge(dve_step, dcount[0])

        def achain(act, ins):
            ins.then_inc(act_step, 1)
            acount[0] += 1
            act.wait_ge(act_step, acount[0])

        def sp_ff(sp, l, ada, rows):
            s, hid = FS[f"ff{l}"], TS[f"hid_ff{l}"]
            b = base[f"ff{l}"]
            w = AW // ada.shape[2]

            def ada_tiles(m, ks, peel=False):
                for k in ks:
                    if not (peel and k < RING):
                        sp.wait_ge(s["ada_used"], KT * m + k - RING + 1)
                    if peel and k == RING - 1:
                        sp.wait_ge(hid["xT_ready"], hid["k0"] + KT)
                    sp.dma_start(ada_slot(l, k % RING).rearrange("p (l n) -> p l n", n=w), ada[:, k, :, bass.ds(m * w, w)])\
                      .then_inc(s["ada_ld"][k % RING], 16)

            for h in range(2):
                sp_half(sp, b + h, h, W1[l][:, HK * h:HK * h + HK, 0:COLS])
            for r, row in enumerate(rows):
                sp.dma_start(brow[l][:, r], row.partition_broadcast(P)).then_inc(brow_ld, 16)
            ada_tiles(0, range(KT), True)
            with sp.Fori(0, FB - 1) as i:
                for h in range(2):
                    sp_half(sp, b + 2 + 4 * i + h, h, W1[l][:, HK * h:HK * h + HK, bass.ds((i + 1) * COLS, COLS)])
                    ada_tiles(i + 1, range(2 * h, 2 * h + 2))
                for n in range(2):
                    sp_half(sp, b + 4 + 4 * i + n, n, W2[l][:, bass.ds(i * HK, HK), n * COLS:n * COLS + COLS])
                    ada_tiles(i + 1, range(4 + 2 * n, 6 + 2 * n))
            for n in range(2):
                sp_half(sp, b + 4 * FB - 2 + n, n, W2[l][:, (FB - 1) * HK:FB * HK, n * COLS:n * COLS + COLS])

        def pe_ff(pe, l):
            s = FS[f"ff{l}"]
            b = base[f"ff{l}"]
            ts = TS[f"hid_ff{l}"]

            def up(m, peel=False):
                j = b if peel else b + 4 * m - 2
                for h in range(2):
                    pe.wait_ge(lo_made, j + h + 1)
                    for t in range(4):
                        if h == 0 and not peel:
                            pe.wait_ge(s["relu_done"], 4 * m - 4 + t + 1)
                        for k in range(HK):
                            mm = pe_tile(pe, bank[t][:, :], h, k, HK * h + k, t, "T", h == 0 and k == 0,
                                         h == 1 and k == HK - 1)
                        if h == 1 and t < 3:
                            mm.then_inc(s["ff1_tile"], 1)
                    mm.then_inc(w_used, 1)

            def down(i, peel=False, last=False):
                j = b + 4 * i + (4 if not last else 2)
                pe.wait_ge(s["hT_ready"], 4 * i + 4)
                for n in range(2):
                    pe.wait_ge(lo_made, j + n + 1)
                    for t in range(ST):
                        if not (peel and n == 0):
                            pe.wait_ge(s["acc_done"], 8 * i + 4 * n - 4 + t + 1)
                        for k in range(HK):
                            for q, (a, c) in enumerate([(0, 0), (0, 1), (1, 0)]):
                                mm = pe.matmul(bank[4 + t][:, :], hT[l][:, a, k, t * P:t * P + P], wsp[:, n, c, k, :],
                                               start=(k == 0 and q == 0), stop=(k == HK - 1 and q == 2))
                        mm.then_inc(s["ff2_tile"] if t < 3 else w_used, 1)

            pe.wait_ge(ts["xT_ready"], ts["k0"] + KT)
            up(0, peel=True)
            up(1)
            down(0, peel=True)
            with pe.Fori(1, FB - 1) as i:
                up(i + 1)
                down(i)
            acc = modacc[l]
            pe.wait_ge(s["ada_used"], KT * FB)
            pe.wait_ge(s["relu_done"], 4 * FB)
            pe_modcols(pe, acc, range(48), 0, mod_done)
            r1, r2 = mod_rows[l]
            pe_modrow(pe, acc, r1, 1, mod_done)
            pe.matmul(bank[3][:, :], ones[:, :], acc[:, r2:r2 + COLS], start=True, stop=True).then_inc(mod_done, 1)
            down(FB - 1, last=True)
            pe.wait_ge(mod_made, 4 + 4 * l + 2)
            pe.matmul(bank[1][:, :], ones[:, :], acc[:, r2 + COLS:r2 + D], start=True, stop=True).then_inc(mod_done, 1)

        def act_ff(act, l):
            s = FS[f"ff{l}"]
            b = base[f"ff{l}"]

            def relu(m, t, peel=False):
                if t < 3:
                    act.wait_ge(s["ff1_tile"], 3 * m + t + 1)
                else:
                    act.wait_ge(w_used, b + (2 if peel else 4 * m))
                if not peel:
                    act.wait_ge(s["hT_ready"], 4 * m - 4 + t + 1)
                act.activation(h32[l][:, t], bank[t][:, :], ACT.Relu).then_inc(s["relu_done"], 1)

            def high(m):
                for t in range(4):
                    act.wait_ge(s["sq_done"], 4 * m + t + 1)
                    act.activation(hT[l][:, 0, t], h32[l][:, t], ACT.Copy).then_inc(s["hhi_done"], 1)

            act_high(act, b // 2 + 1, 0)
            for t in range(3):
                relu(0, t, True)
            relu(0, 3, True)
            act_high(act, b // 2 + 1, 1)
            high(0)

            def step(m):
                q = b // 2 + 2 * m
                act_high(act, q, 0)
                for t in range(3):
                    relu(m, t)
                relu(m, 3)
                act_high(act, q, 1)
                act_high(act, q + 1, 0)
                act_high(act, q + 1, 1)
                high(m)
            with act.Fori(1, FB) as m:
                step(m)
            if b // 2 + 2 * FB < J // 2:
                for slot in range(2):
                    act_high(act, b // 2 + 2 * FB, slot)

        def ada_slot(l, i):
            return ada_ring[l][:, i] if i < RING - 1 else u32[:, :, :].rearrange("p a b -> p (a b)")[:, 0:AW]

        def dve_ff(dve, l, cb, layers, before_last, finish):
            s = FS[f"ff{l}"]
            w = AW // layers

            def square(m):
                for t in range(4):
                    dve.wait_ge(s["relu_done"], 4 * m + t + 1)
                    dve.tensor_tensor(h32[l][:, t], h32[l][:, t], h32[l][:, t], ALU.mult).then_inc(s["sq_done"], 1)

            def low(m):
                for t in range(4):
                    dve.wait_ge(s["hhi_done"], 4 * m + t + 1)
                    dve.tensor_tensor(hT[l][:, 1, t], h32[l][:, t], hT[l][:, 0, t].bitcast(F32), ALU.subtract)\
                       .then_inc(s["hT_ready"], 1)

            def add(i, n, peel=False, last=False):
                for t in range(ST):
                    y = tok[:, t, n * COLS:n * COLS + COLS]
                    if t < 3:
                        dve.wait_ge(s["ff2_tile"], 6 * i + 3 * n + t + 1)
                    else:
                        dve.wait_ge(w_used, base[f"ff{l}"] + 4 * i + (2 if last else 4) + n + 1)
                    if peel:
                        ins = dve.tensor_copy(y, bank[4 + t][:, :])
                    else:
                        dve.wait_ge(s["acc_done"], 8 * i - 8 + 4 * n + t + 1)
                        ins = dve.tensor_tensor(y, y, bank[4 + t][:, :], ALU.add)
                    ins.then_inc(s["acc_done"], 1)
                    if last and n == 1:
                        dve.wait_ge(s["acc_done"], 8 * i + 4 + t + 1)
                        finish(t)

            def ada(m, ks):
                acc = modacc[l][:, :].rearrange("p (l n) -> p l n", l=layers)[:, :, bass.ds(m * w, w)]
                for k in ks:
                    t = ada_slot(l, k % RING).rearrange("p (l n) -> p l n", n=w)
                    dve_mod_tile(dve, acc, t, k, csil[:, cb + k:cb + k + 1], s["ada_ld"][k % RING],
                                 16 * (KT // RING * m + k // RING + 1), s["ada_used"], KT * m + k)

            def step(i, peel=False):
                ada(i + 1, range(0, 4))
                square(i + 1)
                ada(i + 1, range(4, 6))
                add(i, 0, peel)
                ada(i + 1, range(6, 8))
                add(i, 1, peel)
                low(i + 1)

            ada(0, range(KT))
            square(0)
            low(0)
            step(0, True)
            with dve.Fori(1, FB - 1) as i:
                step(i)
            before_last()
            for n in range(2):
                add(FB - 1, n, last=True)

        def dve_mod_tile(dve, acc, w, k, c, ld, ld_at, used, done):
            dve.wait_ge(ld, ld_at)
            if k == 0:
                ins = dve.tensor_scalar(acc, w, c, None, ALU.mult)
            else:
                dve.wait_ge(used, done)
                ins = dve.scalar_tensor_tensor(acc, w, c, acc, ALU.mult, ALU.add)
            ins.then_inc(used, 1)

        def pe_modcols(pe, acc, blocks, bk, done, wrap=6 * KT):
            for b in blocks:
                a = b % wrap * P
                mm = pe.matmul(bank[bk][:, b:b + 1], acc[:, a:a + P], ones[:, 0:1], start=True, stop=True)
            mm.then_inc(done, 1)

        def pe_modrow(pe, acc, off, bk, done):
            for n in range(2):
                mm = pe.matmul(bank[bk + n][:, :], ones[:, :], acc[:, off + n * COLS:off + n * COLS + COLS],
                               start=True, stop=True)
            mm.then_inc(done, 1)

        def dve_modrow(dve, gate, bk):
            for n in range(2):
                g = gate[:, n * COLS:n * COLS + COLS]
                dchain(dve, dve.scalar_tensor_tensor(g, bank[bk + n][:, :], 1.0, g, ALU.add, ALU.add))

        def act_sd(act, name, t0=0, t1=ST):
            for t in range(t0, t1):
                act.wait_ge(var_made, norm0[name] + t + 1)
                act.activation(sd[:, t:t + 1], mv[:, t, 1:2], ACT.Sqrt, bias=LN_EPS).then_inc(sd_made, 1)

        def dve_norm(dve, t, gate, ready, name):
            z = tok[:, t]
            dchain(dve, dve.tensor_tensor(z, z, gate[:, :], ALU.mult))
            dchain(dve, dve.scalar_tensor_tensor(z, x[:, t], ALPHA, z, ALU.mult, ALU.add))
            for n in range(2):
                dchain(dve, dve.bn_stats(stats[:, t, n], tok[:, t, n * COLS:n * COLS + COLS]))
            dve.bn_aggr(mv[:, t], stats[:, t]).then_inc(var_made, 1)
            dve.wait_ge(var_made, norm0[name] + t + 1)
            dve.wait_ge(sd_made, norm0[name] + t + 1)
            dchain(dve, dve.reciprocal(rstd[:, t:t + 1], sd[:, t:t + 1]))
            ins = dve.tensor_scalar(z, z, mv[:, t, 0:1], rstd[:, t:t + 1], ALU.subtract, ALU.mult)
            ins.then_inc(ready, 1)

        def dve_fold(dve, l, i, sh, sc):
            g, b = col("ln_g", (2 * l + i) * 8, 8), col("ln_b", (2 * l + i) * 8, 8)
            dchain(dve, dve.tensor_scalar(ctmp[:, 0:8], modcol[:, sc:sc + 8], 1.0, None, ALU.add))
            dchain(dve, dve.tensor_tensor(scol[:, :], g, ctmp[:, 0:8], ALU.mult))
            dchain(dve, dve.tensor_tensor(ctmp[:, 8:16], b, ctmp[:, 0:8], ALU.mult))
            dchain(dve, dve.tensor_tensor(bcol[:, :], ctmp[:, 8:16], modcol[:, sh:sh + 8], ALU.add))

        def act_rms(act, name, t):
            act.wait_ge(RS[name]["x"], t + 1)
            achain(act, act.activation(u32[:, :, :].rearrange("p a b -> p (a b)"), x[:, t], ACT.Square, accum_out=ssq[:, t:t + 1]))
            act.activation(rms[:, t:t + 1], ssq[:, t:t + 1], ACT.Sqrt, scale=1.0 / D, bias=RMS_EPS).then_inc(RS[name]["rms"], 1)

        def act_out(act, name):
            for p in range(2):
                for h in range(2):
                    act_ahead(act, name, p, h)

        def dve_w16_split(dve, pad, done):
            dchain(dve, dve.memset(pad[:, :, :, :].bitcast(F32), 0.0))
            dchain(dve, dve.tensor_copy(pad[:, 0, :, 0:GLA_R], w16[:, :, :]))
            dve.sem_inc(done, 1)
            dve.tensor_tensor(pad[:, 1, :, 0:GLA_R], w16[:, :, :], pad[:, 0, :, 0:GLA_R].bitcast(F32), ALU.subtract)\
               .then_inc(done, 1)

        def dve_residual(dve, l, ready_done):
            for t in range(ST):
                dchain(dve, dve.tensor_tensor(x[:, t], tok[:, t], lnrow[l][:, 0], ALU.mult))
                ins = dve.tensor_tensor(x[:, t], x[:, t], lnrow[l][:, 1], ALU.add)
                dchain(dve, ins)
            dve.sem_inc(ready_done, 1)

        def sp_lnrow(sp, l, i):
            for r, n in enumerate(("ln_g", "ln_b")):
                sp.dma_start(lnrow[l][:, r], T[n][l, i, :].partition_broadcast(P)).then_inc(ln_ld, 16)

        ada_ring, modacc, hT, h32, lnrow, brow = {}, {}, {}, {}, {}, {}
        s_ctx = ExitStack()
        ring_s = sb("ring_s", [P, RING, 2 * D], where=s_ctx)
        s_ctx.close()
        g_ctx = ExitStack()
        gq = sb("gq", [P, GLA_H, SEQ], where=g_ctx)
        gk = sb("gk", [P, GLA_H, SEQ], where=g_ctx)
        gv = sb("gv", [P, ST, D], where=g_ctx)
        gg = sb("gg", [P, ST, D], where=g_ctx)
        gkT = sb("gkT", [P, SEQ], where=g_ctx)
        wgk2 = sb("wgk2", [GLA_R, GLA_H * GLA_DK], where=g_ctx)
        a_ctx = ExitStack()
        ring0 = sb("ring0", [P, RING, COLS], where=a_ctx)
        acc0 = tok[:, :, :].rearrange("p s d -> p (s d)")
        lohi = sb("lohi", [P, 2, KT, P], F32R, where=a_ctx)
        a_ctx.close()
        r_ctx = ExitStack()
        gbuf = {n: sb("g_" + n, [P, SEQ], where=r_ctx) for n in ("t0", "t1", "cum", "ep", "en")}
        gbuf.update(qb=gbuf["t0"], kb=gbuf["ep"], kf=gbuf["en"], ke=gbuf["t1"])
        gAT = sb("gAT", [P, ST, P], where=r_ctx)
        gkeT = sb("gkeT", [P, ST, P], where=r_ctx)
        gst = sb("gst", [P, NC, GLA_DV], where=r_ctx)
        gdec = sb("gdec", [P, NC], where=r_ctx)
        gss = sb("gss", [P, ST], where=r_ctx)
        grs = sb("grs", [P, ST], where=r_ctx)
        gjunk, greset = u32[:, 0, 0:GLA_DV], u32[:, 1]
        r_ctx.close()
        g_ctx.close()
        for l in range(DEPTH):
            f_ctx = ExitStack()
            lnrow[l] = sb(f"lnrow{l}", [P, 2, D], where=f_ctx)
            brow[l] = sb(f"brow{l}", [P, 2, D], where=f_ctx)
            ada_ring[l] = sb(f"ada_ring{l}", [P, RING - 1, AW], where=f_ctx)
            modacc[l] = sb(f"modacc{l}", [P, 6 * D], where=f_ctx)
            hT[l] = sb(f"hT{l}", [P, 2, 4, SEQ], F32R, where=f_ctx)
            h32[l] = sb(f"h32_{l}", [P, 4, SEQ], where=f_ctx)
            f_ctx.close()

        t_ctx = ExitStack()
        aq = sb("aq", [P, KT, SEQ], where=t_ctx)
        ak = sb("ak", [P, KT, SEQ], where=t_ctx)
        av = sb("av", [P, ST, D], where=t_ctx)
        aP = sb("aP", [P, 2, SEQ], where=t_ctx)
        aPT = sb("aPT", [P, 2, SEQ], where=t_ctx)
        abt = sb("abt", [P, 2, SEQ], where=t_ctx)
        bq8 = sb("bq8", [P, KT], where=t_ctx)
        a_max = sb("a_max", [P, HEADS * ST], where=t_ctx)
        a_sum = sb("a_sum", [P, HEADS * ST], where=t_ctx)
        a_rec = sb("a_rec", [P, HEADS * ST], where=t_ctx)
        t_ctx.close()
        e_ctx = ExitStack()
        hq = sb("hq", [P, 4, SEQ], where=e_ctx)
        hf = sb("hf", [P, 4, SEQ], where=e_ctx)
        hk = sb("hk", [P, 4, SEQ], where=e_ctx)
        hv = sb("hv", [P, ST, COLS], where=e_ctx)
        hu = sb("hu", [P, 4, SEQ], where=e_ctx)
        hc = sb("hc", [P, SEQ], where=e_ctx)
        hqe = sb("hqe", [P, 2, SEQ], where=e_ctx)
        hke = sb("hke", [P, 2, SEQ], where=e_ctx)
        hE = u32
        hAT = sb("hAT", [P, ST, P], where=e_ctx)
        htmp = sb("htmp", [P, ST, P], where=e_ctx)
        hkeT = sb("hkeT", [P, ST, P], where=e_ctx)
        hst = sb("hst", [P, NC, P], where=e_ctx)
        hreset = sb("hreset", [P, SEQ], where=e_ctx)
        hdec = sb("hdec", [P, NC], where=e_ctx)
        hss = sb("hss", [P, ST], where=e_ctx)
        hrs = sb("hrs", [P, ST], where=e_ctx)
        hjunk = sb("hjunk", [P, P], where=e_ctx)
        lb = sb("lb", [P, 4], where=e_ctx)
        omlb = sb("omlb", [P, 4], where=e_ctx)
        lbe = sb("lbe", [P, 3, 4], where=e_ctx)
        lbm = sb("lbm", [P, 4], where=e_ctx)
        pw = sb("pw", [P, 4, P], where=e_ctx)
        pc = hqe[:, 0]
        pp_ = hke
        e_ctx.close()
        o_ctx = ExitStack()
        fq = sb("fq", [P, KT, SEQ], where=o_ctx)
        fk = sb("fk", [P, KT, SEQ], where=o_ctx)
        fv = sb("fv", [P, ST, D], where=o_ctx)
        fP = sb("fP", [P, 2, SEQ], where=o_ctx)
        fPT = sb("fPT", [P, 2, SEQ], where=o_ctx)
        flohi = sb("flohi", [P, 2, KT, P], F32R, where=o_ctx)
        fcum = sb("fcum", [HEADS, SEQ], where=o_ctx)
        fncum = sb("fncum", [HEADS, 2, SEQ], F32R, where=o_ctx)
        eyer = sb("eyer", [P, P], F32R, where=o_ctx)
        cmaskr = sb("cmaskr", [P, P], F32R, where=o_ctx)
        ft = sb("ft", [HEADS, SEQ], where=o_ctx)
        fbf = sb("fbf", [HEADS, 1], where=o_ctx)
        f_max = sb("f_max", [P, HEADS * ST], where=o_ctx)
        f_sum = sb("f_sum", [P, HEADS * ST], where=o_ctx)
        f_rec = sb("f_rec", [P, HEADS * ST], where=o_ctx)
        qg8 = sb("qg8", [P, 1], where=o_ctx)
        o_ctx.close()

        x_ld, w16_ld, gk2_ld, gate_ld, ln_ld = (sem(n) for n in ("x_ld", "w16_ld", "gk2_ld", "gate_ld", "ln_ld"))
        vtr_done, cols_made, esil_done = (sem(n) for n in ("vtr_done", "cols_made", "esil_done"))
        ada0_ld = [sem(f"ada0_ld{i}") for i in range(RING)]
        ada0_used = sem("ada0_used")
        mod_done, mod_made, lohi_made, gkT_done = sem("mod_done"), sem("mod_made"), sem("lohi_made"), sem("gkT_done")
        x_new = sem("x_new")
        brow_ld = sem("brow_ld")
        normed = sem("normed")
        out_ready = sem("out_ready")
        RS = {n: {"x": sem(f"x_made_{n}"), "rms": sem(f"rms_made_{n}")} for n in ("even_in", "odd_in")}
        st_out = sem("st_out")
        g_sem = {n: sem("gla_" + n) for n in ("gkT", "pre", "la", "softplus", "cum", "exps", "dl", "edl", "qk", "ke", "a",
                                              "keT", "keTs", "at", "kv", "state", "o", "ss", "out", "reset")}
        N0 = 9 * KT

        mod_rows = [(2 * D, 5 * D), (2 * D, 5 * D)]
        NCONST = 13 + max(POOLS) + 3 * len(LEVELS)
        def gla_kv(n):
            at = n // 2 % 2 * GLA_DV
            return bank[4 + 2 * (n % 2) + n // 4][:, at:at + GLA_DV]

        def gla_pe(pe):
            s = g_sem
            pe.wait_ge(lohi_made, 2)
            pe.wait_ge(TS["in_gla_in"]["bank_free"], 8 + 24)
            for k in range(KT):
                for q, (a, b) in enumerate([(0, 0), (0, 1), (1, 0)]):
                    mm = pe.matmul(bank[0][:, :], lohi[:, b, k, :], xT[:, a, k, :], start=(k == 0 and q == 0),
                                   stop=(k == KT - 1 and q == 2))
            mm.then_inc(gkT_done, 1)
            pe.wait_ge(ada0_used, N0)
            pe_modcols(pe, acc0, range(24, 40), 1, mod_done, ST * KT)
            pe_modrow(pe, acc0, 2 * D, 2, mod_done)
            pe_modrow(pe, acc0, D, 4, mod_done)
            pe.wait_ge(gk2_ld, 16)
            pe.wait_ge(s["gkT"], 1)
            pe.wait_ge(mod_made, 4)
            for h in range(GLA_H):
                if h:
                    pe.wait_ge(s["la"], h)
                pe.matmul(bank[0][:, :], wgk2[:, h * P:h * P + P], gkT[0:GLA_R, :], start=True, stop=True)\
                  .then_inc(s["pre"], 1)
                pe.wait_ge(s["qk"], 2 * h + 2)
                if h:
                    pe.wait_ge(s["out"], 4 * h)
                for c in range(ST):
                    cc = slice(c * P, c * P + P)
                    pe.matmul(bank[1][:, cc], gbuf["kf"][:, cc], gq[:, h, cc], start=True, stop=True)
                    mm = pe.matmul(bank[2][:, cc], gbuf["kb"][:, cc], gbuf["qb"][:, cc], start=True, stop=True)
                mm.then_inc(s["a"], 1)
                pe.wait_ge(s["ke"], h + 1)
                for c in range(ST):
                    mm = pe.transpose(bank[3][:, c * P:c * P + P], gbuf["ke"][:, c * P:c * P + P], ident[:, :])
                mm.then_inc(s["keT"], 1)
                pe.wait_ge(s["keTs"], h + 1)
                if h:
                    pe.wait_ge(s["state"], h)
                for n in range(NC - 1):
                    pp = slice((n % 2) * CH, (n % 2) * CH + CH)
                    mm = pe.matmul(gla_kv(n), gkeT[pp, n // 2, :], gv[pp, n // 2, h * GLA_DV:h * GLA_DV + GLA_DV], start=True, stop=True)
                mm.then_inc(s["kv"], 1)
                pe.wait_ge(s["at"], h + 1)
                pe.wait_ge(s["state"], h + 1)
                for c in range(ST):
                    o = bank[1 + c // 2][:, (c % 2) * GLA_DV:(c % 2) * GLA_DV + GLA_DV]
                    mm = pe.matmul(o, gAT[:, c, :], gv[:, c, h * GLA_DV:h * GLA_DV + GLA_DV], start=True, stop=False,
                                   skip_group_check=True)
                    for n in (2 * c, 2 * c + 1):
                        if n == 0:
                            continue
                        r = slice((n % 2) * CH, (n % 2) * CH + CH)
                        mm = pe.matmul(o[r, :], gq[:, h, n * CH:n * CH + CH], gst[:, n, :], start=False,
                                       stop=True, skip_group_check=True)
                mm.then_inc(s["o"], 1)

        def gla_act(act):
            s = g_sem
            act.wait_ge(gkT_done, 1)
            act.activation(gkT[:, :], bank[0][:, :], ACT.Copy).then_inc(s["gkT"], 1)
            for h in range(GLA_H):
                b = gbuf
                act.wait_ge(s["pre"], h + 1)
                if h:
                    act.wait_ge(s["a"], h)
                    act.wait_ge(s["keT"], h)
                achain(act, act.activation(b["t0"][:, :], bank[0][:, :], ACT.Abs, bias=col("gla_b_gk", h)))
                achain(act, act.activation(b["t0"][:, :], b["t0"][:, :], ACT.Exp, scale=-1.0))
                act.activation(b["t1"][:, :], b["t0"][:, :], ACT.Ln, bias=1.0).then_inc(s["softplus"], 1)
                act.wait_ge(s["cum"], h + 1)
                act.activation(b["ep"][:, :], b["cum"][:, :], ACT.Exp, scale=1 / GLA_TAU).then_inc(s["exps"], 1)
                act.activation(b["en"][:, :], b["cum"][:, :], ACT.Exp, scale=-1 / GLA_TAU).then_inc(s["exps"], 1)
                if h:
                    act.wait_ge(s["state"], h)
                act.activation(gdec[:, :], b["cum"][:, CH - 1::CH], ACT.Exp, scale=1 / GLA_TAU).then_inc(s["exps"], 1)
                act.wait_ge(s["dl"], h + 1)
                act.activation(b["t1"][:, :], b["t1"][:, :], ACT.Exp, scale=1 / GLA_TAU).then_inc(s["edl"], 1)
                act.wait_ge(s["keT"], h + 1)
                if h:
                    act.wait_ge(s["kv"], h)
                act.activation(gkeT[:, :, :], bank[3][:, :].rearrange("p (c k) -> p c k", c=ST), ACT.Copy)\
                   .then_inc(s["keTs"], 1)
                act.wait_ge(s["o"], h + 1)
                for c in range(ST):
                    o = bank[1 + c // 2][:, (c % 2) * GLA_DV:(c % 2) * GLA_DV + GLA_DV]
                    if h:
                        act.wait_ge(s["out"], 4 * h)
                    achain(act, act.activation(gjunk, o, ACT.Square, accum_out=gss[:, c:c + 1]))
                act.activation(grs[:, :], gss[:, :], ACT.Sqrt, scale=1.0 / GLA_DV, bias=RMS_EPS).then_inc(s["ss"], 1)

        def gla_dve(dve):
            s = g_sem
            b = gbuf
            dve.wait_ge(const_made, NCONST)
            dve.memset(greset, 1.0).then_inc(s["reset"], 1)
            dve.wait_ge(s["reset"], 1)
            dchain(dve, dve.memset(greset[:, 0::CH], 0.0))
            dchain(dve, dve.memset(gAT[:, :, :], 0.0))
            for h in range(GLA_H):
                dve.wait_ge(s["softplus"], h + 1)
                dchain(dve, dve.tensor_scalar(b["cum"][:, :], bank[0][:, :], col("gla_b_gk", h), 0.0, ALU.add, ALU.min))
                ins = dve.tensor_tensor(b["t1"][:, :], b["cum"][:, :], b["t1"][:, :], ALU.subtract)
                ins.then_inc(s["la"], 1)
                dve.wait_ge(s["la"], h + 1)
                dve.tensor_tensor_scan(b["cum"][:, :], greset, b["t1"][:, :], 0.0, ALU.mult, ALU.add)\
                   .then_inc(s["cum"], 1)
                dve.wait_ge(s["cum"], h + 1)
                c3 = b["cum"][:, :].rearrange("p (n c) -> p n c", c=CH)
                dve.tensor_tensor(b["t1"][:, :].rearrange("p (n c) -> p n c", c=CH),
                                  c3[:, :, CH - 1:CH].broadcast_to([P, NC, CH]), c3, ALU.subtract).then_inc(s["dl"], 1)
                dve.wait_ge(s["exps"], 3 * h + 3)
                sc = GLA_DK ** -0.5
                q, k = gq[:, h], gk[:, h]
                dchain(dve, dve.scalar_tensor_tensor(b["qb"][:, :], q, sc, b["en"][:, :], ALU.mult, ALU.mult))
                dchain(dve, dve.scalar_tensor_tensor(q, q, sc, b["ep"][:, :], ALU.mult, ALU.mult))
                dve.tensor_tensor(b["kf"][:, :], k, b["en"][:, :], ALU.mult).then_inc(s["qk"], 1)
                dve.tensor_tensor(b["kb"][:, :], k, b["ep"][:, :], ALU.mult).then_inc(s["qk"], 1)
                dve.wait_ge(s["edl"], h + 1)
                dve.tensor_tensor(b["ke"][:, :], k, b["t1"][:, :], ALU.mult).then_inc(s["ke"], 1)
                dve.wait_ge(s["a"], h + 1)
                for r in range(2):
                    pp = slice(r * CH, r * CH + CH)
                    fw = bank[1][pp, :].rearrange("p (c t) -> p c t", c=ST)[:, :, pp]
                    dchain(dve, dve.tensor_copy(gAT[pp, :, pp], fw))
                for r in range(2):
                    pp = slice(r * CH, r * CH + CH)
                    bw = bank[2][pp, :].rearrange("p (c t) -> p c t", c=ST)[:, :, pp]
                    dchain(dve, dve.copy_predicated(gAT[pp, :, pp], gmask[pp, pp].bitcast(U32).unsqueeze(1).broadcast_to([CH, ST, CH]), bw))
                dve.sem_inc(s["at"], 1)
                dve.wait_ge(s["kv"], h + 1)
                for n in range(1, NC):
                    kv = gla_kv(n - 1)
                    if n == 1:
                        dchain(dve, dve.tensor_copy(gst[:, 1], kv))
                    else:
                        dchain(dve, dve.scalar_tensor_tensor(gst[:, n], gst[:, n - 1], gdec[:, n - 1:n], kv, ALU.mult, ALU.add))
                dve.sem_inc(s["state"], 1)
                dve.wait_ge(s["ss"], h + 1)
                dchain(dve, dve.reciprocal(grs[:, :], grs[:, :]))
                for c in range(ST):
                    o = bank[1 + c // 2][:, (c % 2) * GLA_DV:(c % 2) * GLA_DV + GLA_DV]
                    hv = slice(h * GLA_DV, h * GLA_DV + GLA_DV)
                    dve.scalar_tensor_tensor(tok[:, c, hv], o, grs[:, c:c + 1], gg[:, c, hv], ALU.mult, ALU.mult)\
                       .then_inc(s["out"], 1)
                    dve.wait_ge(s["out"], 4 * h + c + 1)
            dve.sem_inc(TS["mid_gla_out"]["tok_ready"], 1)

        UNITS = [(h, qt) for h in range(HEADS) for qt in range(ST)]
        NU = len(UNITS)
        both = {n: sem("att_" + n) for n in ("s", "max", "exp", "tr", "pt", "pv", "out")}
        a_sem = {"bt": sem("att_bt"), "u0": 0, **both}
        bt_ld = [sem("bt_ld0"), sem("bt_ld1")]
        f_sem = {n: sem("fox_" + n) for n in ("sq", "ms", "rs", "qk", "fl", "z",
                                              "sp", "la", "cum", "lohi", "bf")}
        f_sem.update(both, u0=NU)

        def pe_attention(pe, s, q, k, v, pr, pt, add):
            for u in range(NU + 2):
                if u < NU:
                    h, qt = UNITS[u]
                    n = qt * P + P
                    hp = slice(h % 2 * HD, h % 2 * HD + HD)
                    if u >= 2:
                        pe.wait_ge(s["exp"], s["u0"] + u - 1)
                    S = bank[u % 2]
                    pe.matmul(S[:, 0:n], q[hp, h // 2, qt * P:qt * P + P], k[hp, h // 2, 0:n], start=True, stop=False,
                              skip_group_check=True)
                    add(h, qt, n, S).then_inc(s["s"], 1)
                if 1 <= u <= NU:
                    w = u - 1
                    pe.wait_ge(s["exp"], s["u0"] + w + 1)
                    if w >= 2:
                        pe.wait_ge(s["pt"], s["u0"] + w - 1)
                    for kt in range(UNITS[w][1] + 1):
                        mm = pe.transpose(bank[2 + w % 2][:, kt * P:kt * P + P], pr[:, w % 2, kt * P:kt * P + P], ident[:, :])
                    mm.then_inc(s["tr"], 1)
                if u >= 2:
                    w = u - 2
                    h, qt = UNITS[w]
                    pe.wait_ge(s["pt"], s["u0"] + w + 1)
                    if w >= 2:
                        pe.wait_ge(s["out"], s["u0"] + w - 1)
                    for kt in range(qt + 1):
                        mm = pe.matmul(bank[4 + w % 2][:, 0:HD], pt[:, w % 2, kt * P:kt * P + P], v[:, kt, h * HD:h * HD + HD],
                                       start=(kt == 0), stop=(kt == qt))
                    mm.then_inc(s["pv"], 1)

        def act_attention(act, s, pr, pt, mx, sm, after=None):
            for u in range(NU + 1):
                if u < NU:
                    n = UNITS[u][1] * P + P
                    act.wait_ge(s["max"], s["u0"] + u + 1)
                    if u >= 2:
                        act.wait_ge(s["tr"], s["u0"] + u - 1)
                    act.activation(pr[:, u % 2, 0:n], bank[u % 2][:, 0:n], ACT.Exp, bias=mx[:, u:u + 1],
                                   accum_out=sm[:, u:u + 1]).then_inc(s["exp"], 1)
                    if after:
                        after(u)
                if u >= 1:
                    w = u - 1
                    n = UNITS[w][1] * P + P
                    act.wait_ge(s["tr"], s["u0"] + w + 1)
                    if w >= 2:
                        act.wait_ge(s["pv"], s["u0"] + w - 1)
                    act.activation(pt[:, w % 2, 0:n], bank[2 + w % 2][:, 0:n], ACT.Copy).then_inc(s["pt"], 1)

        def dve_attention(dve, s, mx, sm, rec, write, before=None):
            for u in range(NU + 2):
                if u < NU:
                    n = UNITS[u][1] * P + P
                    if before:
                        before(u)
                    dve.wait_ge(s["s"], s["u0"] + u + 1)
                    dve.tensor_reduce(mx[:, u:u + 1], bank[u % 2][:, 0:n], AX, ALU.max, negate=True).then_inc(s["max"], 1)
                if u >= 2:
                    w = u - 2
                    h, qt = UNITS[w]
                    dve.wait_ge(s["pv"], s["u0"] + w + 1)
                    dchain(dve, dve.reciprocal(rec[:, w:w + 1], sm[:, w:w + 1]))
                    write(w, h, qt, bank[4 + w % 2][:, 0:HD], rec[:, w:w + 1]).then_inc(s["out"], 1)
            dve.wait_ge(s["out"], s["u0"] + NU)

        def att_bias_load(act, h):
            src = T["rel_rows"]
            ap = bass.AP(src.tensor, h * REL, [[1, P], [1, SEQ]])
            act.dma_start(abt[:, h % 2], ap).then_inc(bt_ld[h % 2], 16)

        def att_pe(pe):
            def add(h, qt, n, S):
                if qt == 0:
                    pe.wait_ge(a_sem["bt"], h + 1)
                return pe.matmul(S[:, 0:n], rev[:, :], abt[:, h % 2, SEQ - n:SEQ], start=False, stop=True, skip_group_check=True)
            pe_attention(pe, a_sem, aq, ak, av, aP, aPT, add)

        def att_act(act):
            def after(u):
                h, qt = UNITS[u]
                if qt == ST - 1 and h + 2 < HEADS:
                    att_bias_load(act, h + 2)
            act_attention(act, a_sem, aP, aPT, a_max, a_sum, after)

        def att_dve(dve):
            def bt(h):
                dve.wait_ge(bt_ld[h % 2], 16 * (h // 2) + 16)
                dve.memset(abt[CH:P, h % 2, SEQ - CH:SEQ], NEG).then_inc(a_sem["bt"], 1)

            def before(u):
                h, qt = UNITS[u]
                if u == 0:
                    bt(0)
                if qt == 2 and h + 1 < HEADS:
                    bt(h + 1)

            def write(w, h, qt, o, r):
                return dve.tensor_scalar(tok[:, qt, h * HD:h * HD + HD], o, r, None, ALU.mult)
            dve_attention(dve, a_sem, a_max, a_sum, a_rec, write, before)
            dve.sem_inc(TS["mid_att_out"]["tok_ready"], 1)

        def fox_gate_pe(pe):
            pe.wait_ge(f_sem["lohi"], 2)
            pe.wait_ge(TS["in_odd_in"]["bank_free"], 8 + 32)
            for k in range(KT):
                for q, (a, b) in enumerate([(0, 0), (0, 1), (1, 0)]):
                    mm = pe.matmul(bank[0][:, :], flohi[:, b, k, :], xT[:, a, k, :], start=(k == 0 and q == 0),
                                   stop=(k == KT - 1 and q == 2))
            mm.then_inc(f_sem["fl"], 1)

        def fox_pe(pe):
            s = f_sem
            fox_gate_pe(pe)
            for i in range(2 * KT):
                pe.wait_ge(s["sq"], i + 1)
                if i >= 2:
                    pe.wait_ge(s["rs"], i - 1)
                pe.matmul(bank[2 + i % 2][:, :], bones[:, :], fPT[:, i % 2], start=True, stop=True).then_inc(s["ms"], 1)
            pe.wait_ge(s["qk"], 2 * KT)
            pe.wait_ge(s["cum"], 2)
            def add(h, qt, n, S):
                e = eyer[0:HEADS, h:h + 1].broadcast_to([HEADS, P])
                for part in range(2):
                    pe.matmul(S[:, 0:n], e, fncum[:, part, 0:n], start=False, stop=False, skip_group_check=True)
                return pe.matmul(S[:, n - P:n], eyer[:, :], cmaskr[:, :], start=False, stop=True, skip_group_check=True)
            pe_attention(pe, s, fq, fk, fv, fP, fPT, add)

        def fox_act(act):
            s = f_sem
            act.wait_ge(s["fl"], 1)
            act.wait_ge(s["bf"], 16)
            z = bank[0][0:HEADS, :]
            act.activation(fcum[:, :], z, ACT.Identity, bias=fbf[:, 0:1]).then_inc(s["z"], 1)
            achain(act, act.activation(ft[:, :], z, ACT.Abs, bias=fbf[:, 0:1]))
            achain(act, act.activation(ft[:, :], ft[:, :], ACT.Exp, scale=-1.0))
            act.activation(ft[:, :], ft[:, :], ACT.Ln, bias=1.0).then_inc(s["sp"], 1)
            for i in range(2 * KT + 1):
                if i < 2 * KT:
                    src = (fq, fk)[i // KT][:, i % KT]
                    if i >= 2:
                        act.wait_ge(s["ms"], i - 1)
                    act.activation(fPT[:, i % 2], src, ACT.Square).then_inc(s["sq"], 1)
                if i >= 1:
                    w = i - 1
                    act.wait_ge(s["ms"], w + 1)
                    if w >= 2:
                        act.wait_ge(s["qk"], w - 1)
                    achain(act, act.activation(fP[:, w % 2], bank[2 + w % 2][:, :], ACT.Ln, scale=1.0 / HD, bias=RMS_EPS))
                    act.activation(fP[:, w % 2], fP[:, w % 2], ACT.Exp, scale=-0.5).then_inc(s["rs"], 1)
            act_attention(act, s, fP, fPT, f_max, f_sum)

        def fox_dve(dve):
            s = f_sem
            dve.wait_ge(s["z"], 1)
            dchain(dve, dve.tensor_scalar(fcum[:, :], fcum[:, :], 0.0, None, ALU.min))
            dve.wait_ge(s["sp"], 1)
            dve.tensor_tensor(ft[:, :], fcum[:, :], ft[:, :], ALU.subtract).then_inc(s["la"], 1)
            dve.wait_ge(s["la"], 1)
            dve.tensor_tensor_scan(fcum[:, :], ones[0:HEADS, 0:1].broadcast_to([HEADS, SEQ]), ft[:, :], 0.0, ALU.mult, ALU.add)\
               .then_inc(s["cum"], 1)
            dve.wait_ge(s["cum"], 1)
            dchain(dve, dve.tensor_scalar(fncum[:, 0], fcum[:, :], -1.0, None, ALU.mult))
            dchain(dve, dve.scalar_tensor_tensor(fncum[:, 1], fcum[:, :], -1.0, fncum[:, 0].bitcast(F32), ALU.mult, ALU.subtract))
            dchain(dve, dve.tensor_copy(eyer[:, :], ident[:, :]))
            dve.tensor_copy(cmaskr[:, :], cmask[:, :]).then_inc(s["cum"], 1)
            dchain(dve, dve.tensor_scalar(qg8[:, :], col("fox_qnorm_g_2"), HD ** -0.5, None, ALU.mult))
            for i in range(2 * KT):
                t = (fq, fk)[i // KT][:, i % KT]
                g = (qg8[:, 0:1], col("fox_knorm_g_2"))[i // KT]
                dve.wait_ge(s["rs"], i + 1)
                dve.scalar_tensor_tensor(t, t, g, fP[:, i % 2], ALU.mult, ALU.mult).then_inc(s["qk"], 1)

            def write(w, h, qt, o, r):
                t = tok[:, qt, h * HD:h * HD + HD]
                return dve.scalar_tensor_tensor(t, o, r, t, ALU.mult, ALU.mult)
            dve_attention(dve, s, f_max, f_sum, f_rec, write)
            dve.sem_inc(TS["mid_odd_out"]["tok_ready"], 1)

        h_sem = {n: sem("hgrn_" + n) for n in ("lb", "lbe", "f", "logf", "cum", "diff", "E", "qk", "s", "at", "ex", "keT", "keTs",
                                               "kv", "state", "o", "ss", "out", "pool", "po", "pout", "reset", "pw")}
        NL = len(LEVELS)

        def hgrn_kv(n):
            at = n // 2 * P
            return bank[4 + n % 2][:, at:at + P]

        def hgrn_pe(pe):
            s = h_sem
            for h in range(4):
                for lv in range(NL + 1):
                    it = h * (NL + 1) + lv
                    if lv == 0:
                        pe.wait_ge(s["cum"], h + 1)
                        kk, qq = hk[:, h], hq[:, h]
                    else:
                        pe.wait_ge(s["qk"], h * (NL + 1) + lv)
                        kk, qq = hke[:, lv % 2], hqe[:, lv % 2]
                    if it >= 2:
                        pe.wait_ge(s["at"], it - 1)
                    for c in range(ST):
                        cc = slice(c * P, c * P + P)
                        mm = pe.matmul(bank[it % 2][:, cc], kk[:, cc], qq[:, cc], start=True, stop=True)
                    mm.then_inc(s["s"], 1)
                pe.wait_ge(s["qk"], (h + 1) * (NL + 1))
                for c in range(ST):
                    mm = pe.transpose(bank[2][:, c * P:c * P + P], hke[:, 1, c * P:c * P + P], ident[:, :])
                mm.then_inc(s["keT"], 1)
                pe.wait_ge(s["keTs"], h + 1)
                if h:
                    pe.wait_ge(s["state"], h)
                for n in range(NC - 1):
                    r = slice((n % 2) * CH, (n % 2) * CH + CH)
                    mm = pe.matmul(hgrn_kv(n), hkeT[r, n // 2, :], hv[r, n // 2, h * P:h * P + P], start=True, stop=True)
                mm.then_inc(s["kv"], 1)
                pe.wait_ge(s["at"], (h + 1) * (NL + 1))
                pe.wait_ge(s["state"], h + 1)
                if h:
                    pe.wait_ge(s["out"], 4 * h)
                for c in range(ST):
                    o = bank[3][:, c * P:c * P + P]
                    mm = pe.matmul(o, hAT[:, c, :], hv[:, c, h * P:h * P + P], start=True, stop=False, skip_group_check=True)
                    for n in (2 * c, 2 * c + 1):
                        if n == 0:
                            continue
                        r = slice((n % 2) * CH, (n % 2) * CH + CH)
                        mm = pe.matmul(o[r, :], hqe[:, 1, n * CH:n * CH + CH], hst[:, n, :], start=False, stop=True,
                                       skip_group_check=True)
                mm.then_inc(s["o"], 1)
            for g in range(4):
                pe.wait_ge(s["pool"], g + 1)
                if g == 0:
                    pe.wait_ge(s["pw"], 16)
                if g >= 2:
                    pe.wait_ge(s["pout"], 4 * (g - 1))
                for t in range(ST):
                    mm = pe.matmul(bank[6 + g % 2][:, t * P:t * P + P], pp_[:, g % 2, t * P:t * P + P], pw[:, g, :],
                                   start=True, stop=True)
                mm.then_inc(s["po"], 1)

        def hgrn_act(act):
            s = h_sem
            act.wait_ge(s["lb"], 1)
            act.activation(lbe[:, :, :], lbe[:, :, :], ACT.Exp).then_inc(s["lbe"], 1)
            for h in range(4):
                act.wait_ge(s["f"], h + 1)
                act.activation(hf[:, h], hf[:, h], ACT.Ln).then_inc(s["logf"], 1)
            for h in range(4):
                for lv in range(1, NL + 1):
                    n = h * (NL + 1) + lv
                    act.wait_ge(s["diff"], n)
                    achain(act, act.activation(hE[:, lv % 2], hE[:, lv % 2], ACT.Abs))
                    act.activation(hE[:, lv % 2], hE[:, lv % 2], ACT.Exp, scale=-1.0).then_inc(s["E"], 1)
                act.wait_ge(s["diff"], (h + 1) * (NL + 1))
                if h:
                    act.wait_ge(s["state"], h)
                act.activation(hdec[:, :], hc[:, CH - 1::CH], ACT.Exp).then_inc(s["ex"], 1)
                act.activation(hE[:, 0], hc[:, :], ACT.Exp).then_inc(s["ex"], 1)
                act.activation(hE[:, 1], hE[:, 1], ACT.Exp).then_inc(s["ex"], 1)
                act.wait_ge(s["keT"], h + 1)
                if h:
                    act.wait_ge(s["kv"], h)
                act.activation(hkeT[:, :, :], bank[2][:, :].rearrange("p (c k) -> p c k", c=ST), ACT.Copy)\
                   .then_inc(s["keTs"], 1)
                act.wait_ge(s["o"], h + 1)
                if h:
                    act.wait_ge(s["out"], 4 * h)
                for c in range(ST):
                    achain(act, act.activation(hjunk[:, :], bank[3][:, c * P:c * P + P], ACT.Square, accum_out=hss[:, c:c + 1]))
                act.activation(hrs[:, :], hss[:, :], ACT.Sqrt, scale=1.0 / P, bias=RMS_EPS).then_inc(s["ss"], 1)

        def hgrn_dve(dve):
            s = h_sem
            r = [col("hgrn_lb_2", 4 * i, 4) for i in range(3)]
            dchain(dve, dve.tensor_tensor(lbm[:, :], r[0], r[1], ALU.max))
            dchain(dve, dve.tensor_tensor(lbm[:, :], lbm[:, :], r[2], ALU.max))
            for i in range(3):
                dchain(dve, dve.tensor_tensor(lbe[:, i], r[i], lbm[:, :], ALU.subtract))
            dve.sem_inc(s["lb"], 1)
            dve.wait_ge(s["lbe"], 1)
            dchain(dve, dve.tensor_tensor(lbm[:, :], lbe[:, 0], lbe[:, 1], ALU.add))
            dchain(dve, dve.tensor_tensor(lbm[:, :], lbm[:, :], lbe[:, 2], ALU.add))
            dchain(dve, dve.reciprocal(lbm[:, :], lbm[:, :]))
            dchain(dve, dve.tensor_tensor(lb[:, :], lbe[:, 0], lbm[:, :], ALU.mult))
            dchain(dve, dve.tensor_scalar(omlb[:, :], lb[:, :], -1.0, 1.0, ALU.mult, ALU.add))
            dve.wait_ge(TS["in_even_in"]["bank_free"], 8 + 24)
            for h in range(4):
                dchain(dve, dve.tensor_scalar(hf[:, h], hf[:, h], omlb[:, h:h + 1], lb[:, h:h + 1], ALU.mult, ALU.add))
                dve.tensor_scalar(hk[:, h], hf[:, h], -1.0, 1.0, ALU.mult, ALU.add).then_inc(s["f"], 1)
            dve.memset(hreset[:, :], 1.0).then_inc(s["reset"], 1)
            dve.wait_ge(s["reset"], 1)
            dchain(dve, dve.memset(hreset[:, 0::CH], 0.0))
            for h in range(4):
                q, k = hq[:, h], hk[:, h]
                dve.wait_ge(s["logf"], h + 1)
                if h:
                    dve.wait_ge(s["ex"], 3 * h)
                dve.tensor_tensor_scan(hc[:, :], hreset[:, :], hf[:, h], 0.0, ALU.mult, ALU.add).then_inc(s["cum"], 1)
                dve.wait_ge(s["cum"], h + 1)

                def diff(lv):
                    b = 2 * LEVELS[lv - 1] if lv <= NL else CH
                    m = LEVELS[lv - 1] - 1 if lv <= NL else CH - 1
                    c3 = hc[:, :].rearrange("p (n c) -> p n c", c=b)
                    e = hE[:, lv % 2 if lv <= NL else 1].rearrange("p (n c) -> p n c", c=b)
                    dve.tensor_tensor(e, c3[:, :, m:m + 1].broadcast_to([P, SEQ // b, b]), c3, ALU.subtract).then_inc(s["diff"], 1)

                def add(lv):
                    it = h * (NL + 1) + lv
                    dve.wait_ge(s["s"], it + 1)
                    b4 = bank[it % 2][:, :].rearrange("p (c t) -> p c t", c=ST)
                    m = ident[:, :] if lv == 0 else lmask[:, lv - 1, :]
                    m = m.unsqueeze(1).broadcast_to([P, ST, P])
                    if lv == 0:
                        if h:
                            dve.wait_ge(s["o"], h)
                        ins = dve.tensor_tensor(hAT[:, :, :], b4, m, ALU.mult)
                    else:
                        dchain(dve, dve.tensor_tensor(htmp[:, :, :], b4, m, ALU.mult))
                        dve.wait_ge(s["at"], it)
                        ins = dve.tensor_tensor(hAT[:, :, :], hAT[:, :, :], htmp[:, :, :], ALU.add)
                    ins.then_inc(s["at"], 1)

                diff(1)
                add(0)
                for lv in range(1, NL + 1):
                    if lv < NL:
                        diff(lv + 1)
                    dve.wait_ge(s["E"], h * NL + lv)
                    if lv >= 3:
                        dve.wait_ge(s["s"], h * (NL + 1) + lv - 1)
                    elif h:
                        dve.wait_ge(s["o"], h)
                    dchain(dve, dve.tensor_tensor(hqe[:, lv % 2], q, hE[:, lv % 2], ALU.mult))
                    dve.tensor_tensor(hke[:, lv % 2], k, hE[:, lv % 2], ALU.mult).then_inc(s["qk"], 1)
                    add(lv)
                dve.wait_ge(s["E"], h * NL + NL)
                dve.wait_ge(s["qk"], h * (NL + 1) + NL)
                diff(NL + 1)
                dve.wait_ge(s["ex"], 3 * h + 3)
                dve.wait_ge(s["s"], (h + 1) * (NL + 1))
                dchain(dve, dve.tensor_tensor(hqe[:, 1], q, hE[:, 0], ALU.mult))
                dve.tensor_tensor(hke[:, 1], k, hE[:, 1], ALU.mult).then_inc(s["qk"], 1)
                dve.wait_ge(s["kv"], h + 1)
                for n in range(1, NC):
                    kv = hgrn_kv(n - 1)
                    if n == 1:
                        dchain(dve, dve.tensor_copy(hst[:, 1], kv))
                    else:
                        dchain(dve, dve.scalar_tensor_tensor(hst[:, n], hst[:, n - 1], hdec[:, n - 1:n], kv, ALU.mult, ALU.add))
                dve.sem_inc(s["state"], 1)
                dve.wait_ge(s["ss"], h + 1)
                dchain(dve, dve.reciprocal(hrs[:, :], hrs[:, :]))
                for c in range(ST):
                    t = tok[:, c, h * P:h * P + P]
                    dve.scalar_tensor_tensor(t, bank[3][:, c * P:c * P + P], hrs[:, c:c + 1], t, ALU.mult, ALU.mult)\
                       .then_inc(s["out"], 1)
                    dve.wait_ge(s["out"], 4 * h + c + 1)
            for g, w in enumerate(POOLS):
                u = hu[:, g]
                if g == 0:
                    dve.wait_ge(s["o"], 4)
                dchain(dve, dve.tensor_tensor_scan(pc, ones[:, 0:1].broadcast_to([P, SEQ]), u, 0.0, ALU.mult, ALU.add))
                o = pp_[:, g % 2]
                if g >= 2:
                    dve.wait_ge(s["po"], g - 1)
                dchain(dve, dve.tensor_tensor(o[:, w:], pc[:, w:], pc[:, :SEQ - w], ALU.subtract))
                dchain(dve, dve.tensor_tensor(o[:, 0:w], pc[:, 0:w], rcnt[:, 0:w], ALU.mult))
                dchain(dve, dve.tensor_tensor(o[:, 0:w], o[:, 0:w], u[:, 0:w], ALU.subtract))
                dve.scalar_tensor_tensor(o[:, w:], o[:, w:], 1.0 / w, u[:, w:], ALU.mult, ALU.subtract).then_inc(s["pool"], 1)
                dve.wait_ge(s["pool"], g + 1)
            for g in range(4):
                dve.wait_ge(s["po"], g + 1)
                for c in range(ST):
                    t = tok[:, c, COLS + g * P:COLS + g * P + P]
                    dve.tensor_tensor(t, bank[6 + g % 2][:, c * P:c * P + P], t, ALU.mult).then_inc(s["pout"], 1)
            dve.wait_ge(s["pout"], 16)
            dve.sem_inc(TS["mid_even_out"]["tok_ready"], 1)

        block = ctx.enter_context(nc.Block())

        @block.sync
        def _(sp):
            sp.dma_start(vrow[:, :, :], T["vec_rows"].rearrange("(t p) n -> p t n", p=P)).then_inc(vec_ld, 16)
            for k in range(KT):
                if k == RING:
                    sp.dma_start(x[:, :, :], T["x"][0].rearrange("(s p) d -> p s d", p=P)).then_inc(x_ld, 16)
                if k >= RING:
                    sp.wait_ge(ada0_used, k - RING + 1)
                sp.dma_start(ring_s[:, k % RING], ADA[0][:, k, 0:2 * D]).then_inc(ada0_ld[k % RING], 16)
            for h in range(2):
                sp_half(sp, h, h, W["gla_in"][:, HK * h:HK * h + HK, 0:COLS], peel=True)
            sp.dma_start(w16[:, :, :], W["gla_in"][:, :, 6 * COLS:6 * COLS + GLA_R]).then_inc(w16_ld, 16)
            sp.dma_start(wgk2[:, :], T["gla_w_gk2"][0]).then_inc(gk2_ld, 16)
            for r, (gate, piece) in enumerate([(gate1, 2), (gate2, 5)]):
                sp.dma_start(gate[:, :], T["b_ada"][0, piece * D:piece * D + D].partition_broadcast(P)).then_inc(gate_ld, 16)
            w = W["gla_in"]

            def ada0_tile(g):
                sp.wait_ge(ada0_used, KT + g - RING + 1)
                at = 2 * D + g // KT * COLS
                sp.dma_start(ring0[:, g % RING], ADA[0][:, g % KT, at:at + COLS]).then_inc(ada0_ld[g % RING], 16)
            for g in range(2):
                ada0_tile(g)
            for j in range(2, 12):
                p, h = divmod(j, 2)
                sp_half(sp, j, h, w[:, HK * h:HK * h + HK, p * COLS:p * COLS + COLS])
                for g in range(6 * j - 10, 6 * j - 4 if j < 11 else 8 * KT):
                    ada0_tile(g)
            sp_panels(sp, "gla_out", 2)
            sp.wait_ge(TS["mid_gla_out"]["xT_ready"], TS["mid_gla_out"]["k0"] + KT)
            sp_lnrow(sp, 0, 0)
            sp_ff(sp, 0, ADA[1].unsqueeze(2), [T["b_ada"][1, i * D:i * D + D] for i in (2, 5)])
            sp.wait_ge(x_new, 1)
            sp_lnrow(sp, 0, 1)
            sp_panels(sp, "att_in", 6)
            sp_panels(sp, "att_out", 2)
            sp.wait_ge(TS["mid_att_out"]["xT_ready"], TS["mid_att_out"]["k0"] + KT)
            sp_lnrow(sp, 1, 0)
            sp_ff(sp, 1, T["ada_w_2"].rearrange("l (k p) n -> p k l n", p=P),
                  [T["ada_b_2"][l, 2 * D:3 * D] for l in range(DEPTH)])
            sp.wait_ge(x_new, 3)
            sp_lnrow(sp, 1, 1)
            sp_panels(sp, "even_in", 6)
            sp.wait_ge(x_new, 4)
            sp.dma_start(pw[:, :, :], T["pool_w_2"][0].rearrange("g c d -> c g d")).then_inc(h_sem["pw"], 16)
            sp_panels(sp, "even_out", 2)
            sp.wait_ge(TS["mid_even_out"]["xT_ready"], TS["mid_even_out"]["k0"] + KT)
            sp.dma_start(fbf[:, :], T["fox_b_f_2"][0].unsqueeze(1)).then_inc(f_sem["bf"], 16)
            sp.dma_start(w16[:, :, :], W["odd_in"][:, :, 4 * D:4 * D + HEADS]).then_inc(w16_ld, 16)
            sp_panels(sp, "odd_in", 8)
            sp_panels(sp, "odd_out", 2)
            for t in range(ST):
                sp.wait_ge(out_ready, t + 1)
                sp.dma_start(out[0, t * P:t * P + P], x[:, t]).then_inc(st_out, 16)
            sp.wait_ge(st_out, 16 * ST)

        @block.gpsimd
        def _(pool):
            def made(ins):
                ins.then_inc(const_made, 1)
            for buf, v in [(ones, 1.0), (ident, 0.0)]:
                made(pool.memset(buf[:, :], v))
            pool.wait_ge(const_made, 2)
            made(pool.affine_select(out=ident[:, :], in_=ident[:, :], compare_op=ALU.not_equal, fill=1.0, base=0,
                                    pattern=[[-1, P]], channel_multiplier=1))
            for buf, v in [(gmask, 1.0), (cmask, 0.0), (rev, 0.0), (bones, 0.0)]:
                made(pool.memset(buf[:, :], v))
            made(pool.memset(lmask[:, :, :], 0.0))
            for i in range(max(POOLS)):
                made(pool.memset(rcnt[:, i:i + 1], 1.0 / (i + 1)))
            pool.wait_ge(const_made, 8 + max(POOLS))
            made(pool.affine_select(out=gmask[:, :], in_=gmask[:, :], compare_op=ALU.is_gt, fill=0.0, base=0,
                                    pattern=[[-1, P]], channel_multiplier=1))
            made(pool.affine_select(out=cmask[:, :], in_=cmask[:, :], compare_op=ALU.is_ge, fill=NEG, base=0,
                                    pattern=[[-1, P]], channel_multiplier=1))
            made(pool.affine_select(out=rev[:, :], in_=rev[:, :], compare_op=ALU.not_equal, fill=1.0, base=1 - P,
                                    pattern=[[1, P]], channel_multiplier=1))
            for n, r in enumerate((slice(0, HD), slice(HD, P))):
                pool.wait_ge(const_made, 11 + max(POOLS) + n)
                made(pool.memset(bones[r, r], 1.0))
            halves = [lmask[:, i, :].rearrange("p (n two h) -> p n two h", two=2, h=h)[:, :, 1, :] for i, h in enumerate(LEVELS)]
            pool.wait_ge(const_made, 13 + max(POOLS))
            for v in halves:
                made(pool.memset(v, 1.0))
            n = 13 + max(POOLS)
            for i, (h, v) in enumerate(zip(LEVELS, halves)):
                pool.wait_ge(const_made, n + len(LEVELS))
                made(pool.affine_select(out=v, in_=v, compare_op=ALU.is_ge, fill=0.0, base=0,
                                        pattern=[[-2 * h, P // (2 * h)], [0, h]], channel_multiplier=1))
            pool.wait_ge(const_made, n + 2 * len(LEVELS))
            for i, (h, v) in enumerate(zip(LEVELS, halves)):
                made(pool.affine_select(out=v, in_=v, compare_op=ALU.is_ge, fill=0.0, base=h - 1,
                                        pattern=[[2 * h, P // (2 * h)], [0, h]], channel_multiplier=-1))

            def low(i, slot):
                pool.wait_ge(hi_made, 2 * i + slot + 1)
                pool.tensor_tensor(wsp[:, slot, 1], raw[:, slot], wsp[:, slot, 0].bitcast(F32), ALU.subtract)\
                    .then_inc(lo_made, 1)
            with pool.Fori(0, J // 2) as i:
                for slot in range(2):
                    low(i, slot)

        scale_at = lambda k: scol[:, k:k + 1]
        bias_at = lambda k: bcol[:, k:k + 1]

        @block.scalar
        def _(act):
            act.wait_ge(vtr_done, 1)
            act.activation(cols[:, :], bank[0][:, 0:NV * P], ACT.Copy).then_inc(cols_made, 1)
            act.wait_ge(cols_made, 1)
            act.activation(ctmp[:, :], col("c", 0, 16), ACT.Exp, scale=-1.0).then_inc(esil_done, 1)
            for slot in range(2):
                act_high(act, 0, slot, peel=True)
            act.wait_ge(mod_made, 1)
            act_transposed(act, "in_gla_in", scale_at, bias_at)
            for i in range(3):
                def fn(b, t, ps):
                    if i == 0:
                        return act.activation((gq, gk)[b][:, t], ps[:, :], ACT.Copy)
                    return act.activation((gv, gg)[i - 1][:, t, b * COLS:b * COLS + COLS], ps[:, :],
                                          (ACT.Copy, ACT.Silu)[i - 1])
                act_evac(act, "gla_in", "in_gla_in", i, fn)
            gla_act(act)
            act_transposed(act, "mid_gla_out", lambda k: col("gla_g_norm", k), None)
            act_out(act, "gla_out")
            act_sd(act, "gla_out")
            act_transposed(act, "hid_ff0", scale_at, bias_at)
            act_ff(act, 0)
            act_sd(act, "ff0")
            act_transposed(act, "in_att_in", scale_at, bias_at)
            act.wait_ge(x_new, 2)
            for h in range(2):
                att_bias_load(act, h)
            for i in range(3):
                def fn(b, t, ps):
                    f = 4 * b + t
                    if i == 0:
                        return act.activation(aq[:, f], ps[:, :], ACT.Identity, scale=HD ** -0.5, bias=bq8[:, f:f + 1])
                    if i == 1:
                        return act.activation(ak[:, f], ps[:, :], ACT.Identity, bias=col("att_b_in", KT + f))
                    return act.activation(av[:, t, b * COLS:b * COLS + COLS], ps[:, :], ACT.Copy)
                act_evac(act, "att_in", "in_att_in", i, fn)
            att_act(act)
            act_transposed(act, "mid_att_out", None, lambda k: col("att_b_in", 2 * KT + k))
            act_out(act, "att_out")
            act_sd(act, "att_out")
            act_transposed(act, "hid_ff1", scale_at, bias_at)
            act_ff(act, 1)
            for t in range(ST):
                act_sd(act, "ff1", t, t + 1)
                act_rms(act, "even_in", t)
            act_transposed(act, "in_even_in", scale_at, bias_at)
            act.wait_ge(x_new, 4)
            for i in range(3):
                def fn(b, t, ps):
                    if i == 0:
                        return act.activation((hq, hf)[b][:, t], ps[:, :], (ACT.Copy, ACT.Sigmoid)[b])
                    if b == 0:
                        return act.activation((hv, hu)[i - 1][:, t], ps[:, :], ACT.Copy)
                    return act.activation(tok[:, t, (i - 1) * COLS:i * COLS], ps[:, :], ACT.Silu)
                act_evac(act, "even_in", "in_even_in", i, fn)
            hgrn_act(act)
            act_transposed(act, "mid_even_out", lambda k: col("hgrn_onorm_g_2", k) if k < 4 else col("pool_scale_2", k - 4), None)
            act_out(act, "even_out")
            for t in range(ST):
                act_rms(act, "odd_in", t)
            act_transposed(act, "in_odd_in", scale_at, bias_at)
            for i in range(4):
                def fn(b, t, ps):
                    if i < 2:
                        return act.activation((fq, fk)[i][:, 4 * b + t], ps[:, :], ACT.Copy)
                    c = slice(b * COLS, b * COLS + COLS)
                    if i == 2:
                        return act.activation(fv[:, t, c], ps[:, :], ACT.Copy)
                    return act.activation(tok[:, t, c], ps[:, :], ACT.Silu)
                act_evac(act, "odd_in", "in_odd_in", i, fn)
            fox_act(act)
            act_transposed(act, "mid_odd_out", None, None)
            act_out(act, "odd_out")

        @block.tensor
        def _(pe):
            pe.wait_ge(vec_ld, 16)
            pe.wait_ge(const_made, 3)
            for t in range(NV):
                mm = pe.transpose(bank[0][:, t * P:t * P + P], vrow[:, t, :], ident[:, :])
            mm.then_inc(vtr_done, 1)
            pe.wait_ge(x_ld, 16)
            pe.wait_ge(cols_made, 1)

            def first_columns():
                pe.wait_ge(ada0_used, KT)
                pe_modcols(pe, acc0, range(16), KT - 1, mod_done)
                pe.wait_ge(mod_made, 1)
            pe_transposes(pe, "in_gla_in", x, None, first_columns)
            pe_panels(pe, "gla_in", "in_gla_in", [("TT", 1), ("NN", 2)])
            gla_pe(pe)
            pe_transposes(pe, "mid_gla_out", tok, 1)
            pe_panels(pe, "gla_out", "mid_gla_out", [("NN", 1)])
            pe_transposes(pe, "hid_ff0", tok, ST + 1)
            pe_ff(pe, 0)
            pe.wait_ge(const_made, NCONST)
            pe.wait_ge(mod_made, 8)
            pe_transposes(pe, "in_att_in", tok, ST)
            pe_panels(pe, "att_in", "in_att_in", [("TT", 2), ("NN", 1)])
            pe.wait_ge(TS["in_att_in"]["bank_free"], 8 + 24)
            att_pe(pe)
            pe_transposes(pe, "mid_att_out", tok, 1)
            pe_panels(pe, "att_out", "mid_att_out", [("NN", 1)])
            pe_transposes(pe, "hid_ff1", tok, ST + 1)
            pe_ff(pe, 1)
            pe.wait_ge(mod_made, 12)
            pe_transposes(pe, "in_even_in", tok, ST)
            pe_panels(pe, "even_in", "in_even_in", [("TT", 1), ("NN", 1), ("TN", 1)])
            pe.wait_ge(TS["in_even_in"]["bank_free"], 8 + 24)
            hgrn_pe(pe)
            pe_transposes(pe, "mid_even_out", tok, 1)
            pe_panels(pe, "even_out", "mid_even_out", [("NN", 1)])
            pe_transposes(pe, "in_odd_in", tok, ST)
            pe_panels(pe, "odd_in", "in_odd_in", [("TT", 2), ("NN", 2)])
            fox_pe(pe)
            pe_transposes(pe, "mid_odd_out", tok, 1)
            pe_panels(pe, "odd_out", "mid_odd_out", [("NN", 1)])

        @block.vector
        def _(dve):
            dve.wait_ge(esil_done, 1)
            dchain(dve, dve.tensor_scalar(ctmp[:, :], ctmp[:, :], 1.0, None, ALU.add))
            dchain(dve, dve.reciprocal(ctmp[:, :], ctmp[:, :]))
            dchain(dve, dve.tensor_tensor(csil[:, :], ctmp[:, :], col("c", 0, 16), ALU.mult))
            for k in range(KT):
                dve_mod_tile(dve, acc0[:, 0:2 * D], ring_s[:, k % RING], k, csil[:, k:k + 1], ada0_ld[k % RING],
                             16 * (k // RING + 1), ada0_used, k)
            dve.wait_ge(mod_done, 1)
            dchain(dve, dve.tensor_tensor(modcol[:, 0:16], bank[KT - 1][:, 0:16], col("b_ada", 0, 16), ALU.add))
            dchain(dve, dve.tensor_copy(bcol[:, :], modcol[:, 0:8]))
            dchain(dve, dve.tensor_scalar(scol[:, :], modcol[:, 8:16], 1.0, None, ALU.add))
            dve.sem_inc(mod_made, 1)
            dve.wait_ge(w16_ld, 16)
            dve_w16_split(dve, lohi, lohi_made)
            dve_transposed(dve, "in_gla_in")
            for g in range(8 * KT):
                at = (2 * D + g // KT * COLS) % (ST * D)
                dve_mod_tile(dve, acc0[:, at:at + COLS], ring0[:, g % RING], g % KT, csil[:, g % KT:g % KT + 1], ada0_ld[g % RING],
                             16 * ((KT + g) // RING + 1), ada0_used, KT + g)
            dve.wait_ge(mod_done, 4)
            dve.wait_ge(gate_ld, 32)
            dve.tensor_tensor(modcol[:, 24:40], bank[1][:, 24:40], col("b_ada", 24, 16), ALU.add).then_inc(mod_made, 1)
            dve_modrow(dve, gate1, 2)
            dve.sem_inc(mod_made, 1)
            dve_modrow(dve, gate2, 4)
            dve.sem_inc(mod_made, 1)
            gla_dve(dve)
            dve_transposed(dve, "mid_gla_out")

            def y_and_norm(name, ready, gate):
                for n in range(2):
                    for t in range(ST):
                        wait_tile(dve, name, n, t)
                        dchain(dve, dve.tensor_copy(tok[:, t, n * COLS:n * COLS + COLS], bank[4 * n + t][:, :]))
                        if n == 1:
                            dve_norm(dve, t, gate, ready, name)

            def next_modulation(l, bias, plus_one):
                m = 4 + 4 * l
                one = 1.0 if plus_one else 0.0
                dve.wait_ge(mod_done, m + 3)
                dve.wait_ge(brow_ld, 32 * l + 32)
                dchain(dve, dve.tensor_tensor(modcol[:, :], bank[0][:, 0:48], bias, ALU.add))
                dve.sem_inc(mod_made, 1)
                for n in range(2):
                    g = brow[l][:, 0, n * COLS:n * COLS + COLS]
                    dchain(dve, dve.scalar_tensor_tensor(g, bank[1 + n][:, :], one, g, ALU.add, ALU.add))
                dve.sem_inc(mod_made, 1)
                g = brow[l][:, 1, 0:COLS]
                dchain(dve, dve.scalar_tensor_tensor(g, bank[3][:, :], one, g, ALU.add, ALU.add))
                dve.sem_inc(mod_made, 1)

            def next_gates(l, plus_one):
                dve.wait_ge(mod_done, 4 + 4 * l + 4)
                g = brow[l][:, 1, COLS:D]
                dchain(dve, dve.scalar_tensor_tensor(g, bank[1][:, :], 1.0 if plus_one else 0.0, g, ALU.add, ALU.add))
                dve.sem_inc(mod_made, 1)
                for r, gate in enumerate((gate1, gate2)):
                    dchain(dve, dve.tensor_copy(gate[:, :], brow[l][:, r]))

            def rms_fold(l):
                dchain(dve, dve.tensor_scalar(ctmp[:, 0:8], modcol[:, 24 * l + 8:24 * l + 16], 1.0, None, ALU.add))
                dchain(dve, dve.tensor_tensor(scol[:, :], col("norm_g_2", KT * l, KT), ctmp[:, 0:8], ALU.mult))
                dchain(dve, dve.tensor_copy(bcol[:, :], modcol[:, 24 * l:24 * l + 8]))

            def rms_scaled(name, t):
                dve.wait_ge(RS[name]["rms"], t + 1)
                dchain(dve, dve.reciprocal(rstd[:, t:t + 1], rms[:, t:t + 1]))
                dve.tensor_scalar(tok[:, t], x[:, t], rstd[:, t:t + 1], None, ALU.mult)\
                   .then_inc(TS["in_" + name]["tok_ready"], 1)

            ready = TS["hid_ff0"]["tok_ready"]
            dve_fold(dve, 0, 0, 24, 32)
            dve.sem_inc(ready, 1)
            y_and_norm("gla_out", ready, gate1)
            dve.wait_ge(ready, ST + 1)
            dve_transposed(dve, "hid_ff0")
            dve.wait_ge(ln_ld, 32)
            dve_residual(dve, 0, x_new)
            ready = TS["in_att_in"]["tok_ready"]

            def before_last0():
                next_modulation(0, col("b_ada", 48, 48), True)
                dve_fold(dve, 0, 1, 0, 8)
            dve_ff(dve, 0, 0, 1, before_last0,
                   lambda t: dve_norm(dve, t, gate2, ready, "ff0"))
            dve.wait_ge(ready, ST)
            next_gates(0, True)
            dve_transposed(dve, "in_att_in")
            dve.wait_ge(ln_ld, 64)
            dchain(dve, dve.tensor_scalar(bq8[:, :], col("att_b_in", 0, KT), HD ** -0.5, None, ALU.mult))
            dve_residual(dve, 0, x_new)
            att_dve(dve)
            dve_transposed(dve, "mid_att_out")
            ready = TS["hid_ff1"]["tok_ready"]
            dve_fold(dve, 1, 0, 24, 32)
            dve.sem_inc(ready, 1)
            y_and_norm("att_out", ready, gate1)
            dve.wait_ge(ready, ST + 1)
            dve_transposed(dve, "hid_ff1")
            dve.wait_ge(ln_ld, 96)
            dve_residual(dve, 1, x_new)

            def before_last1():
                next_modulation(1, col("ada_b_2", 0, 48), False)
                rms_fold(0)
                dve.wait_ge(ln_ld, 128)

            def finish1(t):
                dve_norm(dve, t, gate2, normed, "ff1")
                dve.wait_ge(normed, t + 1)
                dchain(dve, dve.tensor_tensor(tok[:, t], tok[:, t], lnrow[1][:, 0], ALU.mult))
                ins = dve.tensor_tensor(x[:, t], tok[:, t], lnrow[1][:, 1], ALU.add)
                ins.then_inc(RS["even_in"]["x"], 1)
                dve.wait_ge(RS["even_in"]["x"], t + 1)
                if t:
                    rms_scaled("even_in", t - 1)
            dve_ff(dve, 1, KT, DEPTH, before_last1, finish1)
            rms_scaled("even_in", ST - 1)
            next_gates(1, False)
            dve.sem_inc(x_new, 1)
            dve_transposed(dve, "in_even_in")
            hgrn_dve(dve)
            dve_transposed(dve, "mid_even_out")
            rms_fold(1)

            def gated(name, gate, new):
                for n in range(2):
                    for t in range(ST):
                        c = slice(n * COLS, n * COLS + COLS)
                        wait_tile(dve, name, n, t)
                        dchain(dve, dve.tensor_tensor(tok[:, t, c], bank[4 * n + t][:, :], gate[:, c], ALU.mult))
                        if n == 1:
                            dve.tensor_tensor(x[:, t], x[:, t], tok[:, t], ALU.add).then_inc(new, 1)
                            dve.wait_ge(new, t + 1)
                            if t and name == "even_out":
                                rms_scaled("odd_in", t - 1)
            gated("even_out", gate1, RS["odd_in"]["x"])
            dve.sem_inc(x_new, 1)
            rms_scaled("odd_in", ST - 1)
            dve.wait_ge(w16_ld, 32)
            dve_w16_split(dve, flohi, f_sem["lohi"])
            dve_transposed(dve, "in_odd_in")
            fox_dve(dve)
            dve_transposed(dve, "mid_odd_out")
            gated("odd_out", gate2, out_ready)

    return nc


_NAMES = ["x", "c", "w_ada", "b_ada", "ln_g", "ln_b", "gla_w_in", "gla_w_gk2", "gla_b_gk", "gla_g_norm", "gla_w_out",
          "att_w_in", "att_b_in", "att_rel_bias", "att_w_out", "ff_w1", "ff_w2", "c_2", "norm_g_2", "ada_w_2", "ada_b_2",
          "hgrn_lb_2", "even_w_in_2", "hgrn_onorm_g_2", "pool_w_2", "pool_scale_2", "even_w_out_2", "odd_w_in_2",
          "fox_b_f_2", "fox_qnorm_g_2", "fox_knorm_g_2", "odd_w_out_2"]


def kernel(**inputs):
    import numpy as np
    import concourse.bacc as bacc
    from concourse.bass_utils import run_bass_kernel_spmd

    nc = bacc.Bacc("TRN2", target_bir_lowering=False, num_devices=1)
    rows = []
    for name in ROWS:
        a = np.ascontiguousarray(inputs[name]).reshape(-1)
        if a.size < P:
            a = np.concatenate([a] * (P // a.size))
        rows.append(a.reshape(-1, P))
    rows = np.concatenate(rows)
    rows = np.concatenate([rows, np.zeros((NV * P - len(rows), P), rows.dtype)])
    rel = np.asarray(inputs["att_rel_bias"])[0]
    rel = rel[:, np.clip(np.arange(SEQ - 1, SEQ - 1 - REL, -1), -MAX_REL, MAX_REL) + MAX_REL]
    arrays, aps = {}, {}
    for name, a in [(n, inputs[n]) for n in _NAMES if n != "att_rel_bias"] + [("vec_rows", rows), ("rel_rows", rel)]:
        a = np.ascontiguousarray(a)
        arrays["in_" + name] = a
        aps[name] = nc.dram_tensor("in_" + name, a.shape, mybir.dt.from_np(a.dtype), kind="ExternalInput").ap()
    out = nc.dram_tensor("out_0", (1, SEQ, D), F32, kind="ExternalOutput").ap()
    build(nc, aps, out)
    r = run_bass_kernel_spmd(nc, [arrays], core_ids=[0])
    return r.results[0]["out_0"]
```

```python
from contextlib import ExitStack

import concourse.bass as bass
from concourse import mybir

F32 = mybir.dt.float32
F32R = mybir.dt.float32r
U32 = mybir.dt.uint32
ALU = mybir.AluOpType
ACT = mybir.ActivationFunctionType
AX = mybir.AxisListType.X

P = 128
SEQ = 512
D = 1024
ST = SEQ // P
KT = D // P
COLS = 512
HK = 4
FF = 4 * D
FB = FF // COLS
CH = 64
NC = SEQ // CH
DEPTH = 2
ALPHA = (2.0 * DEPTH) ** 0.25
LN_EPS = 1e-5
RMS_EPS = 1e-6
GLA_H, GLA_DK, GLA_DV, GLA_R, GLA_TAU = 4, 128, 256, 16, 16.0
HEADS, HD = 16, 64
POOLS = (2, 4, 8, 16)
LEVELS = (32, 16, 8, 4, 2, 1)
REL = SEQ + P - 1
MAX_REL = 128
NEG = -1e30
AW = 6 * D // FB
RING = 4

ROWS = {}
_n = 0
for _name, _rows in [("b_ada", DEPTH * 48), ("ln_g", 32), ("ln_b", 32), ("gla_b_gk", 4), ("gla_g_norm", 8),
                     ("att_b_in", 24), ("norm_g_2", 16), ("ada_b_2", 48), ("hgrn_lb_2", 12), ("hgrn_onorm_g_2", 4),
                     ("pool_scale_2", 4), ("fox_qnorm_g_2", 1), ("fox_knorm_g_2", 1), ("c", 8), ("c_2", 8)]:
    ROWS[_name] = _n
    _n += _rows
NV = (_n + P - 1) // P


def build(nc, T, out):
    ctx = ExitStack()

    def sb(name, shape, dt=F32, where=None):
        return (where or ctx).enter_context(nc.sbuf_tensor(name, shape, dt))

    def sem(name):
        return ctx.enter_context(nc.semaphore(name))

    with ctx:
        bank = [ctx.enter_context(nc.psum_tensor(f"bank{i}", [P, COLS], F32)) for i in range(8)]

        raw = sb("raw", [P, 2, HK, COLS])
        wsp = sb("wsp", [P, 2, 2, HK, COLS], F32R)
        x_ctx = ExitStack()
        xT = sb("xT", [P, 2, KT, SEQ], F32R, where=x_ctx)
        x_ctx.close()
        spare = sb("spare", [P, 2 * KT, SEQ])
        x = sb("x", [P, ST, D])
        tok = sb("tok", [P, ST, D])
        u32 = sb("u32", [P, 2, SEQ])
        vrow = u32[:, :, :].rearrange("p a b -> p (a b)")[:, 0:NV * P].rearrange("p (t n) -> p t n", n=P)
        cols = sb("cols", [P, NV * P])
        ident = sb("ident", [P, P])
        ones = sb("ones", [P, P])
        gmask = sb("gmask", [P, P])
        cmask = sb("cmask", [P, P])
        lmask = sb("lmask", [P, len(LEVELS), P])
        rcnt = sb("rcnt", [P, max(POOLS)])
        rev = sb("rev", [P, P])
        bones = sb("bones", [P, P])
        csil = sb("csil", [P, 16])
        ctmp = sb("ctmp", [P, 16])
        modcol = sb("modcol", [P, 48])
        scol = sb("scol", [P, KT])
        bcol = sb("bcol", [P, KT])
        stats = sb("stats", [P, ST, 2, 6])
        mv = sb("mv", [P, ST, 2])
        rstd = sb("rstd", [P, ST])
        sd = sb("sd", [P, ST])
        negmean = sb("negmean", [P, ST])
        shift = sb("shift", [P, ST])
        ssq = sb("ssq", [P, ST])
        rms = sb("rms", [P, ST])
        w16 = sb("w16", [P, KT, GLA_R])

        first = ctx.enter_context(ExitStack())
        gate1 = sb("gate1", [P, D], where=first)
        gate2 = sb("gate2", [P, D], where=first)
        vec_ld = sem("vec_ld")

        def col(name, k=0, n=1):
            return cols[:, ROWS[name] + k:ROWS[name] + k + n]

        base, J = {}, 0
        PANELS = [("gla_in", 6), ("gla_out", 2), ("ff0", None), ("att_in", 6), ("att_out", 2), ("ff1", None),
                  ("even_in", 6), ("even_out", 2), ("odd_in", 8), ("odd_out", 2)]
        PANELS_N = dict(PANELS)
        for n, c in PANELS:
            base[n] = J
            J += 2 * c if c else 4 * FB
        kview = lambda w: w.rearrange("(k p) n -> p k n", p=P)
        W = {"gla_in": kview(T["gla_w_in"][0]), "gla_out": kview(T["gla_w_out"][0]),
             "att_in": kview(T["att_w_in"][0]), "att_out": kview(T["att_w_out"][0]),
             "even_in": kview(T["even_w_in_2"][0]), "even_out": kview(T["even_w_out_2"][0]),
             "odd_in": kview(T["odd_w_in_2"][0]), "odd_out": kview(T["odd_w_out_2"][0])}
        W1 = [kview(T["ff_w1"][l]) for l in range(DEPTH)]
        W2 = [kview(T["ff_w2"][l]) for l in range(DEPTH)]
        ADA = [kview(T["w_ada"][l]) for l in range(DEPTH)]

        raw_ld = [sem("raw_ld0"), sem("raw_ld1")]
        hi_made = sem("hi_made")
        lo_made = sem("lo_made")
        w_used = sem("w_used")
        dve_step = sem("dve_step")
        act_step = sem("act_step")
        const_made = sem("const_made")

        def sems(stage, *names):
            return [sem(f"{n}_{stage}") for n in names]

        shared = {n: sem(n) for n in ("tr_done", "u_made", "xT_ready")}
        TS = {}
        for n, _ in PANELS:
            s = {"in": "in_", "out": "mid_"}.get(n.split("_")[-1], "hid_") + n
            TS[s] = {"k0": KT * len(TS), "tok_ready": sem("tok_ready_" + s), "bank_free": sem("bank_free_" + s), **shared}
        tile_done, tile0, var_made, sd_made = sem("tile_done"), {}, sem("var_made"), sem("sd_made")
        for n, c in PANELS:
            if c:
                tile0[n] = 3 * sum(PANELS_N[m] for m in tile0)
        norm0 = {n: ST * i for i, n in enumerate(("gla_out", "ff0", "att_out", "ff1"))}
        FS = {}
        for n in ("ff0", "ff1"):
            names = ("ff1_tile", "relu_done", "sq_done", "hhi_done", "hT_ready", "ff2_tile", "acc_done", "ada_used")
            FS[n] = dict(zip(names, sems(n, *names)))
            FS[n]["ada_ld"] = sems(n, *[f"ada_ld{i}" for i in range(RING)])

        def sp_half(sp, j, slot, src, peel=False):
            if not peel:
                sp.wait_ge(lo_made, j - 1)
            sp.dma_start(raw[:, slot], src).then_inc(raw_ld[slot], 16)

        def sp_panels(sp, name, n, extra=None):
            w = W[name]
            b = base[name]
            peel = 1 if b == 0 else 0
            if peel:
                for h in range(2):
                    sp_half(sp, h, h, w[:, HK * h:HK * h + HK, 0:COLS], peel=True)
            with sp.Fori(peel, n) as i:
                for h in range(2):
                    sp_half(sp, b + 2 * i + h, h, w[:, HK * h:HK * h + HK, bass.ds(i * COLS, COLS)])

        def act_high(act, q, slot, peel=False):
            act.wait_ge(raw_ld[slot], 16 * q + 16)
            if not peel:
                act.wait_ge(w_used, 2 * q + slot - 1)
            act.activation(wsp[:, slot, 0], raw[:, slot], ACT.Copy).then_inc(hi_made, 1)

        def act_ahead(act, name, panel, half):
            q = base[name] // 2 + panel + 1
            if not isinstance(q, int) or q < J // 2:
                act_high(act, q, half)

        def pe_tile(pe, out_ap, slot, k, kk, t, kind, start, stop):
            for n, (a, b) in enumerate([(0, 0), (0, 1), (1, 0)]):
                w = wsp[:, slot, b, k, :]
                if kind == "T":
                    l, r = wsp[:, slot, b, k, t * P:t * P + P], xT[:, a, kk, :]
                else:
                    l, r = xT[:, a, kk, t * P:t * P + P], w
                mm = pe.matmul(out_ap, l, r, start=(start and n == 0), stop=(stop and n == 2))
            return mm

        def pe_panel(pe, j, bk, kind, free, free_at, ts):
            for h in range(2):
                pe.wait_ge(lo_made, j + h + 1)
                if h == 0:
                    for t in range(4):
                        pe.wait_ge(free, free_at + t + 1)
                        for k in range(HK):
                            if t == 0 and bk == 0:
                                pe.wait_ge(ts["xT_ready"], ts["k0"] + k + 1)
                            mm = pe_tile(pe, bank[bk + t][:, :], 0, k, k, t, kind, k == 0, False)
                    mm.then_inc(w_used, 1)
                else:
                    for t in range(4):
                        for k in range(HK):
                            if t == 0 and bk == 0:
                                pe.wait_ge(ts["xT_ready"], ts["k0"] + HK + k + 1)
                            mm = pe_tile(pe, bank[bk + t][:, :], 1, k, HK + k, t, kind, False, k == HK - 1)
                        mm.then_inc(tile_done if t < 3 else w_used, 1)

        def pe_panels(pe, name, ts, runs):
            s = TS[ts]
            i0 = 0
            for kind, pairs in runs:
                def pair(i):
                    for b in range(2):
                        pe_panel(pe, base[name] + 4 * i + 2 * b, 4 * b, kind[b], s["bank_free"], 8 * i + 4 * b, s)
                if pairs > 1:
                    with pe.Fori(i0, i0 + pairs) as i:
                        pair(i)
                else:
                    pair(i0)
                i0 += pairs

        def wait_tile(eng, name, panel, t):
            if t < 3:
                eng.wait_ge(tile_done, tile0[name] + 3 * panel + t + 1)
            else:
                eng.wait_ge(w_used, base[name] + 2 * panel + 2)

        def act_evac(act, name, ts, i, fn):
            for b in range(2):
                act_ahead(act, name, 2 * i + b, 0)
                for t in range(4):
                    if t == 3:
                        act_ahead(act, name, 2 * i + b, 1)
                    wait_tile(act, name, 2 * i + b, t)
                    fn(b, t, bank[4 * b + t]).then_inc(TS[ts]["bank_free"], 1)

        def pe_transposes(pe, ts, src, need=None, tile_need=None, before_last=None):
            s = TS[ts]
            if tile_need:
                for t in range(ST):
                    pe.wait_ge(s["tok_ready"], tile_need + t)
                    for k in range(KT):
                        mm = pe.transpose(bank[k][:, t * P:t * P + P], src[:, t, k * P:k * P + P], ident[:, :])
                        if t == ST - 1:
                            mm.then_inc(s["tr_done"], 1)
                return
            if need:
                pe.wait_ge(s["tok_ready"], need)
            for k in range(KT):
                if before_last and k == KT - 1:
                    before_last()
                for t in range(ST):
                    mm = pe.transpose(bank[k][:, t * P:t * P + P], src[:, t, k * P:k * P + P], ident[:, :])
                mm.then_inc(s["tr_done"], 1)

        def act_transposed(act, ts, scale, bias):
            s = TS[ts]
            for k in range(KT):
                act.wait_ge(s["tr_done"], s["k0"] + k + 1)
                if k >= 2:
                    act.wait_ge(s["xT_ready"], s["k0"] + k - 1)
                kw = {}
                if scale is not None:
                    kw["scale"] = scale(k)
                if bias is not None:
                    kw["bias"] = bias(k)
                act.activation(u32[:, k % 2], bank[k][:, :], ACT.Identity, **kw).then_inc(s["u_made"], 1)
                act.activation(xT[:, 0, k], bank[k][:, :], ACT.Identity, **kw).then_inc(s["bank_free"], 1)

        def dve_transposed(dve, ts):
            s = TS[ts]
            for k in range(KT):
                dve.wait_ge(s["u_made"], s["k0"] + k + 1)
                dve.wait_ge(s["bank_free"], k + 1)
                dve.tensor_tensor(xT[:, 1, k], u32[:, k % 2], xT[:, 0, k].bitcast(F32), ALU.subtract)\
                   .then_inc(s["xT_ready"], 1)

        dcount, acount = [0], [0]

        def dchain(dve, ins):
            ins.then_inc(dve_step, 1)
            dcount[0] += 1
            dve.wait_ge(dve_step, dcount[0])

        def achain(act, ins):
            ins.then_inc(act_step, 1)
            acount[0] += 1
            act.wait_ge(act_step, acount[0])

        def sp_ff(sp, l, ada, rows):
            s, hid = FS[f"ff{l}"], TS[f"hid_ff{l}"]
            b = base[f"ff{l}"]
            w = AW // ada.shape[2]

            def ada_tiles(m, ks, peel=False):
                for k in ks:
                    if not (peel and k < RING):
                        sp.wait_ge(s["ada_used"], KT * m + k - RING + 1)
                    if peel and k == RING - 1:
                        sp.wait_ge(hid["xT_ready"], hid["k0"] + KT)
                    sp.dma_start(ada_slot(l, k % RING).rearrange("p (l n) -> p l n", n=w), ada[:, k, :, bass.ds(m * w, w)])\
                      .then_inc(s["ada_ld"][k % RING], 16)

            for h in range(2):
                sp_half(sp, b + h, h, W1[l][:, HK * h:HK * h + HK, 0:COLS])
            for r, row in enumerate(rows):
                sp.dma_start(brow[l][:, r], row.partition_broadcast(P)).then_inc(brow_ld, 16)
            ada_tiles(0, range(KT), True)
            with sp.Fori(0, FB - 1) as i:
                for h in range(2):
                    sp_half(sp, b + 2 + 4 * i + h, h, W1[l][:, HK * h:HK * h + HK, bass.ds((i + 1) * COLS, COLS)])
                    ada_tiles(i + 1, range(2 * h, 2 * h + 2))
                for n in range(2):
                    sp_half(sp, b + 4 + 4 * i + n, n, W2[l][:, bass.ds(i * HK, HK), n * COLS:n * COLS + COLS])
                    ada_tiles(i + 1, range(4 + 2 * n, 6 + 2 * n))
            for n in range(2):
                sp_half(sp, b + 4 * FB - 2 + n, n, W2[l][:, (FB - 1) * HK:FB * HK, n * COLS:n * COLS + COLS])

        def pe_ff(pe, l):
            s = FS[f"ff{l}"]
            b = base[f"ff{l}"]
            ts = TS[f"hid_ff{l}"]

            def up(m, peel=False):
                j = b if peel else b + 4 * m - 2
                for h in range(2):
                    pe.wait_ge(lo_made, j + h + 1)
                    for t in range(4):
                        if h == 0 and peel:
                            pe.wait_ge(ts["bank_free"], t + 1)
                        elif h == 0:
                            pe.wait_ge(s["relu_done"], 4 * m - 4 + t + 1)
                        for k in range(HK):
                            if peel and t == 0:
                                pe.wait_ge(ts["xT_ready"], ts["k0"] + HK * h + k + 1)
                            mm = pe_tile(pe, bank[t][:, :], h, k, HK * h + k, t, "T", h == 0 and k == 0,
                                         h == 1 and k == HK - 1)
                        if h == 1 and t < 3:
                            mm.then_inc(s["ff1_tile"], 1)
                    mm.then_inc(w_used, 1)

            def down(i, peel=False, last=False):
                j = b + 4 * i + (4 if not last else 2)
                pe.wait_ge(s["hT_ready"], 4 * i + 4)
                for n in range(2):
                    pe.wait_ge(lo_made, j + n + 1)
                    for t in range(ST):
                        if not (peel and n == 0):
                            pe.wait_ge(s["acc_done"], 8 * i + 4 * n - 4 + t + 1)
                        for k in range(HK):
                            for q, (a, c) in enumerate([(0, 0), (0, 1), (1, 0)]):
                                mm = pe.matmul(bank[4 + t][:, :], hT[l][:, a, k, t * P:t * P + P], wsp[:, n, c, k, :],
                                               start=(k == 0 and q == 0), stop=(k == HK - 1 and q == 2))
                        mm.then_inc(s["ff2_tile"] if t < 3 else w_used, 1)

            up(0, peel=True)
            up(1)
            down(0, peel=True)
            with pe.Fori(1, FB - 1) as i:
                up(i + 1)
                down(i)
            acc = modacc[l]
            pe.wait_ge(s["ada_used"], KT * FB)
            pe.wait_ge(s["relu_done"], 4 * FB)
            pe_modcols(pe, acc, range(48), 0, mod_done)
            r1, r2 = mod_rows[l]
            pe_modrow(pe, acc, r1, 1, mod_done)
            pe.matmul(bank[3][:, :], ones[:, :], acc[:, r2:r2 + COLS], start=True, stop=True).then_inc(mod_done, 1)
            pe.wait_ge(mod_made, 4 + 4 * l + 1)
            pe.matmul(bank[0][:, :], ones[:, :], acc[:, r2 + COLS:r2 + D], start=True, stop=True).then_inc(mod_done, 1)
            down(FB - 1, last=True)

        def act_ff(act, l):
            s = FS[f"ff{l}"]
            b = base[f"ff{l}"]

            def relu(m, t, peel=False):
                if t < 3:
                    act.wait_ge(s["ff1_tile"], 3 * m + t + 1)
                else:
                    act.wait_ge(w_used, b + (2 if peel else 4 * m))
                if not peel:
                    act.wait_ge(s["hT_ready"], 4 * m - 4 + t + 1)
                act.activation(h32[l][:, t], bank[t][:, :], ACT.Relu).then_inc(s["relu_done"], 1)

            def high(m):
                for t in range(4):
                    act.wait_ge(s["sq_done"], 4 * m + t + 1)
                    act.activation(hT[l][:, 0, t], h32[l][:, t], ACT.Copy).then_inc(s["hhi_done"], 1)

            act_high(act, b // 2 + 1, 0)
            for t in range(3):
                relu(0, t, True)
            relu(0, 3, True)
            act_high(act, b // 2 + 1, 1)
            high(0)

            def step(m):
                q = b // 2 + 2 * m
                act_high(act, q, 0)
                for t in range(3):
                    relu(m, t)
                relu(m, 3)
                act_high(act, q, 1)
                act_high(act, q + 1, 0)
                act_high(act, q + 1, 1)
                high(m)
            with act.Fori(1, FB) as m:
                step(m)
            if b // 2 + 2 * FB < J // 2:
                for slot in range(2):
                    act_high(act, b // 2 + 2 * FB, slot)

        def ada_slot(l, i):
            return ada_ring[l][:, i] if i < RING - 1 else u32[:, :, :].rearrange("p a b -> p (a b)")[:, 0:AW]

        def dve_ff(dve, l, cb, layers, gate, residual, before_last, finish):
            s = FS[f"ff{l}"]
            w = AW // layers

            def square(m):
                for t in range(4):
                    dve.wait_ge(s["relu_done"], 4 * m + t + 1)
                    dve.tensor_tensor(h32[l][:, t], h32[l][:, t], h32[l][:, t], ALU.mult).then_inc(s["sq_done"], 1)

            def low(m):
                for t in range(4):
                    dve.wait_ge(s["hhi_done"], 4 * m + t + 1)
                    dve.tensor_tensor(hT[l][:, 1, t], h32[l][:, t], hT[l][:, 0, t].bitcast(F32), ALU.subtract)\
                       .then_inc(s["hT_ready"], 1)

            def add(i, n, peel=False):
                for t in range(ST):
                    y = tok[:, t, n * COLS:n * COLS + COLS]
                    if t < 3:
                        dve.wait_ge(s["ff2_tile"], 6 * i + 3 * n + t + 1)
                    else:
                        dve.wait_ge(w_used, base[f"ff{l}"] + 4 * i + 4 + n + 1)
                    if peel:
                        ins = dve.tensor_copy(y, bank[4 + t][:, :])
                    else:
                        dve.wait_ge(s["acc_done"], 8 * i - 8 + 4 * n + t + 1)
                        ins = dve.tensor_tensor(y, y, bank[4 + t][:, :], ALU.add)
                    ins.then_inc(s["acc_done"], 1)

            def gated_sum():
                dve.wait_ge(s["acc_done"], 8 * (FB - 1))
                for t in range(ST):
                    dchain(dve, dve.tensor_tensor(tok[:, t], tok[:, t], gate[:, :], ALU.mult))
                    dchain(dve, dve.scalar_tensor_tensor(tok[:, t], x[:, t], ALPHA, tok[:, t], ALU.mult, ALU.add))

            def add_last(n):
                i = FB - 1
                c = slice(n * COLS, n * COLS + COLS)
                for t in range(ST):
                    if t < 3:
                        dve.wait_ge(s["ff2_tile"], 6 * i + 3 * n + t + 1)
                    else:
                        dve.wait_ge(w_used, base[f"ff{l}"] + 4 * i + 2 + n + 1)
                    dve.tensor_tensor(h32[l][:, t], bank[4 + t][:, :], gate[:, c], ALU.mult).then_inc(s["acc_done"], 1)
                    dve.wait_ge(s["acc_done"], 8 * i + 4 * n + t + 1)
                    dchain(dve, dve.tensor_tensor(tok[:, t, c], tok[:, t, c], h32[l][:, t], ALU.add))
                    dve_statistics(dve, t, n)
                    finish(t, n)

            def ada(m, ks):
                acc = modacc[l][:, :].rearrange("p (l n) -> p l n", l=layers)[:, :, bass.ds(m * w, w)]
                for k in ks:
                    t = ada_slot(l, k % RING).rearrange("p (l n) -> p l n", n=w)
                    dve_mod_tile(dve, acc, t, k, csil[:, cb + k:cb + k + 1], s["ada_ld"][k % RING],
                                 16 * (KT // RING * m + k // RING + 1), s["ada_used"], KT * m + k)

            def step(i, peel=False):
                ada(i + 1, range(0, 4))
                square(i + 1)
                ada(i + 1, range(4, 6))
                add(i, 0, peel)
                ada(i + 1, range(6, 8))
                add(i, 1, peel)
                low(i + 1)

            ada(0, range(KT))
            residual()
            square(0)
            low(0)
            step(0, True)
            with dve.Fori(1, FB - 1) as i:
                step(i)
            before_last()
            gated_sum()
            for n in range(2):
                add_last(n)

        def dve_mod_tile(dve, acc, w, k, c, ld, ld_at, used, done):
            dve.wait_ge(ld, ld_at)
            if k == 0:
                ins = dve.tensor_scalar(acc, w, c, None, ALU.mult)
            else:
                dve.wait_ge(used, done)
                ins = dve.scalar_tensor_tensor(acc, w, c, acc, ALU.mult, ALU.add)
            ins.then_inc(used, 1)

        def pe_modcols(pe, acc, blocks, bk, done, wrap=6 * KT):
            for b in blocks:
                a = b % wrap * P
                mm = pe.matmul(bank[bk][:, b:b + 1], acc[:, a:a + P], ones[:, 0:1], start=True, stop=True)
            mm.then_inc(done, 1)

        def pe_modrow(pe, acc, off, bk, done):
            for n in range(2):
                mm = pe.matmul(bank[bk + n][:, :], ones[:, :], acc[:, off + n * COLS:off + n * COLS + COLS],
                               start=True, stop=True)
            mm.then_inc(done, 1)

        def dve_modrow(dve, gate, bk):
            for n in range(2):
                g = gate[:, n * COLS:n * COLS + COLS]
                dchain(dve, dve.scalar_tensor_tensor(g, bank[bk + n][:, :], 1.0, g, ALU.add, ALU.add))

        def act_inverse_root(act, out_ap, in_ap, tmp, scale, eps):
            achain(act, act.activation(tmp, in_ap, ACT.Ln, scale=scale, bias=eps))
            return act.activation(out_ap, tmp, ACT.Exp, scale=-0.5)

        def act_normalised(act, name, t, ready):
            act.wait_ge(var_made, norm0[name] + t + 1)
            achain(act, act_inverse_root(act, rstd[:, t:t + 1], mv[:, t, 1:2], sd[:, t:t + 1], 1.0, LN_EPS))
            achain(act, act.activation(shift[:, t:t + 1], negmean[:, t:t + 1], ACT.Identity, scale=rstd[:, t:t + 1]))
            act.activation(tok[:, t], tok[:, t], ACT.Identity, scale=rstd[:, t:t + 1], bias=shift[:, t:t + 1]).then_inc(ready, 1)

        def dve_mix(dve, t, n, y, gate):
            c = slice(n * COLS, n * COLS + COLS)
            z = tok[:, t, c]
            dchain(dve, dve.tensor_tensor(z, y, gate[:, c], ALU.mult))
            dchain(dve, dve.scalar_tensor_tensor(z, x[:, t, c], ALPHA, z, ALU.mult, ALU.add))
            dve_statistics(dve, t, n)

        def dve_statistics(dve, t, n):
            dchain(dve, dve.bn_stats(stats[:, t, n], tok[:, t, n * COLS:n * COLS + COLS]))
            if n == 1:
                dchain(dve, dve.bn_aggr(mv[:, t], stats[:, t]))
                dve.tensor_scalar(negmean[:, t:t + 1], mv[:, t, 0:1], -1.0, None, ALU.mult).then_inc(var_made, 1)

        def dve_fold(dve, l, i, sh, sc):
            g, b = col("ln_g", (2 * l + i) * 8, 8), col("ln_b", (2 * l + i) * 8, 8)
            dchain(dve, dve.tensor_scalar(ctmp[:, 0:8], modcol[:, sc:sc + 8], 1.0, None, ALU.add))
            dchain(dve, dve.tensor_tensor(scol[:, :], g, ctmp[:, 0:8], ALU.mult))
            dchain(dve, dve.tensor_tensor(ctmp[:, 8:16], b, ctmp[:, 0:8], ALU.mult))
            dchain(dve, dve.tensor_tensor(bcol[:, :], ctmp[:, 8:16], modcol[:, sh:sh + 8], ALU.add))

        def act_rms(act, name, t):
            act.wait_ge(RS[name]["x"], t + 1)
            achain(act, act.activation(u32[:, :, :].rearrange("p a b -> p (a b)"), x[:, t], ACT.Square, accum_out=ssq[:, t:t + 1]))
            achain(act, act_inverse_root(act, rms[:, t:t + 1], ssq[:, t:t + 1], sd[:, t:t + 1], 1.0 / D, RMS_EPS))
            act.activation(tok[:, t], x[:, t], ACT.Copy, scale=rms[:, t:t + 1]).then_inc(TS["in_" + name]["tok_ready"], 1)

        def act_out(act, name):
            for p in range(2):
                for h in range(2):
                    act_ahead(act, name, p, h)

        def dve_w16_split(dve, pad, done):
            dchain(dve, dve.memset(pad[:, :, :, :].bitcast(F32), 0.0))
            dchain(dve, dve.tensor_copy(pad[:, 0, :, 0:GLA_R], w16[:, :, :]))
            dve.sem_inc(done, 1)
            dve.tensor_tensor(pad[:, 1, :, 0:GLA_R], w16[:, :, :], pad[:, 0, :, 0:GLA_R].bitcast(F32), ALU.subtract)\
               .then_inc(done, 1)

        def dve_residual(dve, l, ready_done):
            for t in range(ST):
                dchain(dve, dve.tensor_tensor(x[:, t], tok[:, t], lnrow[l][:, 0], ALU.mult))
                ins = dve.tensor_tensor(x[:, t], x[:, t], lnrow[l][:, 1], ALU.add)
                dchain(dve, ins)
            dve.sem_inc(ready_done, 1)

        def sp_lnrow(sp, l, i):
            for r, n in enumerate(("ln_g", "ln_b")):
                sp.dma_start(lnrow[l][:, r], T[n][l, i, :].partition_broadcast(P)).then_inc(ln_ld, 16)

        ada_ring, modacc, hT, h32, lnrow, brow = {}, {}, {}, {}, {}, {}
        s_ctx = ExitStack()
        ring_s = sb("ring_s", [P, RING, 2 * D], where=s_ctx)
        s_ctx.close()
        g_ctx = ExitStack()
        gq = sb("gq", [P, GLA_H, SEQ], where=g_ctx)
        gk = sb("gk", [P, GLA_H, SEQ], where=g_ctx)
        gv = sb("gv", [P, ST, D], where=g_ctx)
        gg = sb("gg", [P, ST, D], where=g_ctx)
        gkT = sb("gkT", [P, SEQ], where=g_ctx)
        wgk2 = sb("wgk2", [GLA_R, GLA_H * GLA_DK], where=g_ctx)
        a_ctx = ExitStack()
        ring0 = sb("ring0", [P, RING, COLS], where=a_ctx)
        acc0 = tok[:, :, :].rearrange("p s d -> p (s d)")
        lohi = sb("lohi", [P, 2, KT, P], F32R, where=a_ctx)
        a_ctx.close()
        r_ctx = ExitStack()
        gt = sb("gt", [P, 2, SEQ], where=r_ctx)
        gcum = sb("gcum", [P, 2, SEQ], where=r_ctx)
        gAT = sb("gAT", [P, 2, ST, P], where=r_ctx)
        gst = sb("gst", [P, NC, GLA_DV], where=r_ctx)
        gdec = sb("gdec", [P, GLA_H, NC], where=r_ctx)
        gss = sb("gss", [P, ST], where=r_ctx)
        grs = sb("grs", [P, ST], where=r_ctx)
        gjunk, greset = u32[:, 0, 0:GLA_DV], u32[:, 1]
        r_ctx.close()
        g_ctx.close()
        for l in range(DEPTH):
            f_ctx = ExitStack()
            lnrow[l] = sb(f"lnrow{l}", [P, 2, D], where=f_ctx)
            brow[l] = sb(f"brow{l}", [P, 2, D], where=f_ctx)
            ada_ring[l] = sb(f"ada_ring{l}", [P, RING - 1, AW], where=f_ctx)
            modacc[l] = sb(f"modacc{l}", [P, 6 * D], where=f_ctx)
            hT[l] = sb(f"hT{l}", [P, 2, 4, SEQ], F32R, where=f_ctx)
            h32[l] = sb(f"h32_{l}", [P, 4, SEQ], where=f_ctx)
            f_ctx.close()

        t_ctx = ExitStack()
        q_ctx = ExitStack()
        aq = sb("aq", [P, KT, SEQ], where=t_ctx)
        ak = sb("ak", [P, KT, SEQ], where=q_ctx)
        q_ctx.close()
        akl = sb("akl", [P, KT, SEQ], F32R, where=t_ctx)
        av = sb("av", [P, ST, D], where=t_ctx)
        aP = sb("aP", [P, 4, SEQ], where=t_ctx)
        aPT = u32
        abt = sb("abt", [P, 2, SEQ], where=t_ctx)
        abt_parts = sb("abt_parts", [P, 2, 2, SEQ], F32R, where=t_ctx)
        revr = sb("revr", [P, P], F32R, where=t_ctx)
        bq8 = sb("bq8", [P, KT], where=t_ctx)
        a_max = sb("a_max", [P, HEADS * ST], where=t_ctx)
        a_sum = sb("a_sum", [P, HEADS * ST], where=t_ctx)
        a_rec = sb("a_rec", [P, HEADS * ST], where=t_ctx)
        t_ctx.close()
        e_ctx = ExitStack()
        hq = sb("hq", [P, 4, SEQ], where=e_ctx)
        hf = sb("hf", [P, 4, SEQ], where=e_ctx)
        hk = sb("hk", [P, 4, SEQ], where=e_ctx)
        hv = sb("hv", [P, ST, COLS], where=e_ctx)
        hu = sb("hu", [P, 4, SEQ], where=e_ctx)
        hAT = sb("hAT", [P, 4, ST, P], where=e_ctx)
        hst = sb("hst", [P, 2, NC, P], where=e_ctx)
        hreset = sb("hreset", [P, SEQ], where=e_ctx)
        hdec = sb("hdec", [P, 4, NC], where=e_ctx)
        hss = sb("hss", [P, 4, ST], where=e_ctx)
        hrs = sb("hrs", [P, 4, ST], where=e_ctx)
        hjunk = sb("hjunk", [P, P], where=e_ctx)
        lb = sb("lb", [P, 4], where=e_ctx)
        omlb = sb("omlb", [P, 4], where=e_ctx)
        lbe = sb("lbe", [P, 3, 4], where=e_ctx)
        lbm = sb("lbm", [P, 4], where=e_ctx)
        pw = sb("pw", [P, 4, P], where=e_ctx)

        def xt_slot(i):
            return spare[:, i]

        hE = lambda i: xt_slot(i)
        hX = lambda i: xt_slot(KT + i)
        hqe = lambda i: xt_slot(3 + i)
        hke = lambda i: xt_slot(5 + i)
        hEq = lambda i: xt_slot((7, KT + 3)[i])
        hEk = lambda i: xt_slot(12 + i)
        hkeT = lambda i: xt_slot(14 + i)
        pool_sum = xt_slot(0)
        pools = lambda g: xt_slot((1, 2, KT, KT + 1)[g])
        e_ctx.close()
        o_ctx = ExitStack()
        q_ctx = ExitStack()
        fq = sb("fq", [P, KT, SEQ], where=o_ctx)
        fk = sb("fk", [P, KT, SEQ], where=q_ctx)
        q_ctx.close()
        fkl = sb("fkl", [P, KT, SEQ], F32R, where=o_ctx)
        fv = sb("fv", [P, ST, D], where=o_ctx)
        fP = sb("fP", [P, 4, SEQ], where=o_ctx)
        fPT = u32
        flohi = sb("flohi", [P, 2, KT, P], F32R, where=o_ctx)
        fcum = sb("fcum", [HEADS, SEQ], where=o_ctx)
        fncum = sb("fncum", [P, SEQ], F32R, where=o_ctx)
        fsel = sb("fsel", [P, HEADS], F32R, where=o_ctx)
        eyer = sb("eyer", [P, P], F32R, where=o_ctx)
        cmaskr = sb("cmaskr", [P, P], F32R, where=o_ctx)
        ft = sb("ft", [HEADS, SEQ], where=o_ctx)
        fbf = sb("fbf", [HEADS, 1], where=o_ctx)
        f_max = sb("f_max", [P, HEADS * ST], where=o_ctx)
        f_sum = sb("f_sum", [P, HEADS * ST], where=o_ctx)
        f_rec = sb("f_rec", [P, HEADS * ST], where=o_ctx)
        qg8 = sb("qg8", [P, 1], where=o_ctx)
        o_ctx.close()

        x_ld, w16_ld, gk2_ld, gate_ld, ln_ld = (sem(n) for n in ("x_ld", "w16_ld", "gk2_ld", "gate_ld", "ln_ld"))
        vtr_done, cols_made, esil_done = (sem(n) for n in ("vtr_done", "cols_made", "esil_done"))
        ada0_ld = [sem(f"ada0_ld{i}") for i in range(RING)]
        ada0_used = sem("ada0_used")
        mod_done, mod_made, lohi_made, gkT_done = sem("mod_done"), sem("mod_made"), sem("lohi_made"), sem("gkT_done")
        x_new = sem("x_new")
        brow_ld = sem("brow_ld")
        normed = sem("normed")
        out_ready = sem("out_ready")
        RS = {n: {"x": sem(f"x_made_{n}")} for n in ("even_in", "odd_in")}
        st_out = sem("st_out")
        g_sem = {n: sem("gla_" + n) for n in ("gkT", "pre", "la", "softplus", "cum", "exps", "dl", "edl", "qk", "ke", "a",
                                              "keT", "keTs", "at", "kv", "state", "o", "ss", "out", "reset")}
        N0 = 9 * KT

        mod_rows = [(2 * D, 5 * D), (2 * D, 5 * D)]
        NCONST = 13 + max(POOLS) + 3 * len(LEVELS)
        gqb = lambda h: spare[:, 4 * h]
        gkb = lambda h: spare[:, 4 * h + 1]
        gkf = lambda h: spare[:, 4 * h + 2]
        gke = lambda h: spare[:, 4 * h + 3]

        def gla_kv(n):
            at = n // 2 % 2 * GLA_DV
            return bank[4 + 2 * (n % 2) + n // 4][:, at:at + GLA_DV]

        def gla_o(c):
            return bank[1 + c // 2][:, (c % 2) * GLA_DV:(c % 2) * GLA_DV + GLA_DV]

        def gla_pe(pe):
            s = g_sem
            pe.wait_ge(lohi_made, 2)
            pe.wait_ge(TS["in_gla_in"]["bank_free"], 8 + 20)
            for k in range(KT):
                for q, (a, b) in enumerate([(0, 0), (0, 1), (1, 0)]):
                    mm = pe.matmul(bank[0][:, :], lohi[:, b, k, :], xT[:, a, k, :], start=(k == 0 and q == 0),
                                   stop=(k == KT - 1 and q == 2))
            mm.then_inc(gkT_done, 1)
            pe.wait_ge(gk2_ld, 16)
            pe.wait_ge(s["gkT"], 1)
            pe.wait_ge(TS["in_gla_in"]["bank_free"], 8 + 24)
            for h in range(GLA_H):
                pe.matmul(bank[4 + h][:, :], wgk2[:, h * P:h * P + P], gkT[0:GLA_R, :], start=True, stop=True)\
                  .then_inc(s["pre"], 1)
            pe.wait_ge(ada0_used, N0)
            pe_modcols(pe, acc0, range(24, 40), 1, mod_done, ST * KT)
            pe_modrow(pe, acc0, 2 * D, 2, mod_done)
            pe.wait_ge(mod_made, 3)
            pe_modrow(pe, acc0, D, 2, mod_done)
            pe.wait_ge(mod_made, 4)

            def turned(h):
                pe.wait_ge(s["ke"], h + 1)
                if h:
                    pe.wait_ge(s["at"], h)
                for c in range(ST):
                    mm = pe.transpose(bank[0][:, c * P:c * P + P], gke(h)[:, c * P:c * P + P], ident[:, :])
                mm.then_inc(s["keT"], 1)

            def scores(h):
                pe.wait_ge(s["qk"], 4 * h + 4)
                pe.wait_ge(s["keTs"], h + 1)
                for c in range(ST):
                    cc = slice(c * P, c * P + P)
                    pe.matmul(bank[0][:, cc], gkf(h)[:, cc], gq[:, h, cc], start=True, stop=True)
                    mm = pe.matmul(bank[3][:, cc], gkb(h)[:, cc], gqb(h)[:, cc], start=True, stop=True)
                mm.then_inc(s["a"], 1)

            def chunk_states(h):
                if h:
                    pe.wait_ge(s["state"], h)
                else:
                    pe.wait_ge(s["la"], GLA_H)
                for n in range(NC - 1):
                    pp = slice((n % 2) * CH, (n % 2) * CH + CH)
                    mm = pe.matmul(gla_kv(n), gke(h)[pp, n // 2 * P:n // 2 * P + P], gv[pp, n // 2, h * GLA_DV:h * GLA_DV + GLA_DV],
                                   start=True, stop=True)
                mm.then_inc(s["kv"], 1)

            def output(h):
                pe.wait_ge(s["at"], h + 1)
                pe.wait_ge(s["state"], h + 1)
                if h:
                    pe.wait_ge(s["out"], 4 * h)
                for c in range(ST):
                    mm = pe.matmul(gla_o(c), gAT[:, h % 2, c, :], gv[:, c, h * GLA_DV:h * GLA_DV + GLA_DV], start=True, stop=False,
                                   skip_group_check=True)
                    for n in (2 * c, 2 * c + 1):
                        if n == 0:
                            continue
                        r = slice((n % 2) * CH, (n % 2) * CH + CH)
                        mm = pe.matmul(gla_o(c)[r, :], gq[:, h, n * CH:n * CH + CH], gst[:, n, :], start=False,
                                       stop=True, skip_group_check=True)
                mm.then_inc(s["o"], 1)

            turned(0)
            scores(0)
            turned(1)
            scores(1)
            chunk_states(0)
            for h in range(2, GLA_H):
                turned(h)
                scores(h)
                chunk_states(h - 1)
                output(h - 2)
            chunk_states(GLA_H - 1)
            output(GLA_H - 2)
            output(GLA_H - 1)

        def gla_act(act):
            s = g_sem
            act.wait_ge(gkT_done, 1)
            act.activation(gkT[:, :], bank[0][:, :], ACT.Copy).then_inc(s["gkT"], 1)

            def softplus(h):
                t = gt[:, h % 2]
                act.wait_ge(s["pre"], h + 1)
                if h >= 2:
                    act.wait_ge(s["la"], h - 1)
                achain(act, act.activation(t, bank[4 + h][:, :], ACT.Abs, bias=col("gla_b_gk", h)))
                achain(act, act.activation(t, t, ACT.Exp, scale=-1.0))
                act.activation(t, t, ACT.Ln, bias=1.0).then_inc(s["softplus"], 1)

            def exps(h):
                c = gcum[:, h % 2]
                act.wait_ge(s["cum"], h + 1)
                act.activation(gkf(h), c, ACT.Exp, scale=-1 / GLA_TAU).then_inc(s["exps"], 1)
                act.activation(gkb(h), c, ACT.Exp, scale=1 / GLA_TAU).then_inc(s["exps"], 1)
                act.activation(gdec[:, h], c[:, CH - 1::CH], ACT.Exp, scale=1 / GLA_TAU).then_inc(s["exps"], 1)
                act.wait_ge(s["dl"], h + 1)
                act.activation(gke(h), gke(h), ACT.Exp, scale=1 / GLA_TAU).then_inc(s["edl"], 1)

            def keys(h):
                act.wait_ge(s["keT"], h + 1)
                act.activation(gke(h), bank[0][:, :], ACT.Copy).then_inc(s["keTs"], 1)

            def squares(h):
                act.wait_ge(s["o"], h + 1)
                for c in range(ST):
                    if h:
                        act.wait_ge(s["out"], 4 * h)
                    achain(act, act.activation(gjunk, gla_o(c), ACT.Square, accum_out=gss[:, c:c + 1]))
                act_inverse_root(act, grs[:, :], gss[:, :], sd[:, :], 1.0 / GLA_DV, RMS_EPS).then_inc(s["ss"], 1)

            act.wait_ge(ada0_used, N0)
            softplus(0)
            softplus(1)
            exps(0)
            softplus(2)
            exps(1)
            keys(0)
            softplus(3)
            exps(2)
            keys(1)
            exps(3)
            keys(2)
            squares(0)
            keys(3)
            for h in range(1, GLA_H):
                squares(h)

        def gla_dve(dve, rest_of_modulation):
            s = g_sem
            dve.wait_ge(const_made, NCONST)
            dchain(dve, dve.memset(greset, 1.0))
            dchain(dve, dve.memset(greset[:, 0::CH], 0.0))
            dve.wait_ge(gkT_done, 1)
            dchain(dve, dve.memset(gAT[:, :, :, :], 0.0))

            def gates(h):
                c = gcum[:, h % 2]
                dve.wait_ge(s["softplus"], h + 1)
                if h >= 2:
                    dve.wait_ge(s["exps"], 3 * h - 3)
                dchain(dve, dve.tensor_scalar(c, bank[4 + h][:, :], col("gla_b_gk", h), 0.0, ALU.add, ALU.min))
                dve.tensor_tensor(c, c, gt[:, h % 2], ALU.subtract).then_inc(s["la"], 1)
                dve.wait_ge(s["la"], h + 1)
                dve.tensor_tensor_scan(c, greset, c, 0.0, ALU.mult, ALU.add).then_inc(s["cum"], 1)
                dve.wait_ge(s["cum"], h + 1)
                c3 = c.rearrange("p (n c) -> p n c", c=CH)
                dve.tensor_tensor(gke(h).rearrange("p (n c) -> p n c", c=CH),
                                  c3[:, :, CH - 1:CH].broadcast_to([P, NC, CH]), c3, ALU.subtract).then_inc(s["dl"], 1)

            def scaled(h):
                sc = GLA_DK ** -0.5
                q, k = gq[:, h], gk[:, h]
                dve.wait_ge(s["edl"], h + 1)
                dve.tensor_tensor(gke(h), k, gke(h), ALU.mult).then_inc(s["ke"], 1)
                dve.wait_ge(s["exps"], 3 * h + 3)
                dve.scalar_tensor_tensor(gqb(h), q, sc, gkf(h), ALU.mult, ALU.mult).then_inc(s["qk"], 1)
                dve.wait_ge(s["qk"], 4 * h + 1)
                dve.scalar_tensor_tensor(q, q, sc, gkb(h), ALU.mult, ALU.mult).then_inc(s["qk"], 1)
                dve.tensor_tensor(gkf(h), k, gkf(h), ALU.mult).then_inc(s["qk"], 1)
                dve.wait_ge(s["qk"], 4 * h + 2)
                dve.tensor_tensor(gkb(h), k, gkb(h), ALU.mult).then_inc(s["qk"], 1)

            def taken(h):
                dve.wait_ge(s["a"], h + 1)
                if h >= 2:
                    dve.wait_ge(s["o"], h - 1)
                for r in range(2):
                    pp = slice(r * CH, r * CH + CH)
                    fw = bank[0][pp, :].rearrange("p (c t) -> p c t", c=ST)[:, :, pp]
                    dchain(dve, dve.tensor_copy(gAT[pp, h % 2, :, pp], fw))
                for r in range(2):
                    pp = slice(r * CH, r * CH + CH)
                    bw = bank[3][pp, :].rearrange("p (c t) -> p c t", c=ST)[:, :, pp]
                    m = gmask[pp, pp].bitcast(U32).unsqueeze(1).broadcast_to([CH, ST, CH])
                    dchain(dve, dve.copy_predicated(gAT[pp, h % 2, :, pp], m, bw))
                dve.sem_inc(s["at"], 1)

            def states(h):
                dve.wait_ge(s["kv"], h + 1)
                if h:
                    dve.wait_ge(s["o"], h)
                for n in range(1, NC):
                    kv = gla_kv(n - 1)
                    if n == 1:
                        dchain(dve, dve.tensor_copy(gst[:, 1], kv))
                    else:
                        dchain(dve, dve.scalar_tensor_tensor(gst[:, n], gst[:, n - 1], gdec[:, h, n - 1:n], kv, ALU.mult, ALU.add))
                dve.sem_inc(s["state"], 1)

            def written(h):
                dve.wait_ge(s["ss"], h + 1)
                for c in range(ST):
                    hv_ = slice(h * GLA_DV, h * GLA_DV + GLA_DV)
                    dve.scalar_tensor_tensor(tok[:, c, hv_], gla_o(c), grs[:, c:c + 1], gg[:, c, hv_], ALU.mult, ALU.mult)\
                       .then_inc(s["out"], 1)

            gates(0)
            gates(1)
            rest_of_modulation()
            scaled(0)
            gates(2)
            scaled(1)
            taken(0)
            gates(3)
            scaled(2)
            taken(1)
            states(0)
            scaled(3)
            taken(2)
            states(1)
            written(0)
            taken(3)
            states(2)
            written(1)
            states(3)
            written(2)
            written(3)
            dve.wait_ge(s["out"], 4 * GLA_H)
            dve.sem_inc(TS["mid_gla_out"]["tok_ready"], 1)

        UNITS = [(h, qt) for h in range(HEADS) for qt in range(ST)]
        NU = len(UNITS)
        LAG = 3
        S_BANK = (0, 1, 6, 7)
        both = {n: sem("att_" + n) for n in ("s", "max", "exp", "tr", "pt", "pv", "out")}
        a_sem = {"bt": sem("att_bt"), "split": sem("att_split"), "qsplit": sem("att_qsplit"), "u0": 0, **both}
        bt_ld = [sem("bt_ld0"), sem("bt_ld1")]
        f_sem = {n: sem("fox_" + n) for n in ("normed", "sq", "ms", "ln", "rs", "qk", "fl", "z",
                                              "sp", "la", "cum", "lohi", "bf")}
        f_sem.update(both, u0=NU, qsplit=sem("fox_qsplit"))

        PASSES = ((0, 0), (0, 1), (1, 0))

        def dve_split(dve, hi, lo, src, done):
            dchain(dve, dve.tensor_copy(hi, src))
            dve.tensor_tensor(lo, src, hi.bitcast(F32), ALU.subtract).then_inc(done, 1)

        q_part = lambda h, a: xT[:, a, h % 2]
        k_high = lambda f: xT[:, f % 2, 2 + f // 2]

        def dve_zeros(dve):
            for h in range(2):
                other = slice((1 - h) * HD, (1 - h) * HD + HD)
                dchain(dve, dve.memset(xT[other, :, h].bitcast(F32), 0.0))

        def dve_split_q(dve, s, q, h):
            hp = slice(h % 2 * HD, h % 2 * HD + HD)
            if h >= 2:
                dve.wait_ge(s["s"], s["u0"] + ST * (h - 1))
            dve_split(dve, q_part(h, 0)[hp], q_part(h, 1)[hp], q[hp, h // 2], s["qsplit"])

        def pe_attention(pe, s, k_low, v, pr, pt, ready, add):
            for u in range(NU + LAG + 2):
                if u < NU:
                    h, qt = UNITS[u]
                    n = qt * P + P
                    if u >= 4:
                        pe.wait_ge(s["exp"], s["u0"] + u - 3)
                    S = bank[S_BANK[u % 4]]
                    if qt == 0:
                        ready(h)
                    for a, b in PASSES:
                        k = (k_high(h // 2), k_low[:, h // 2])[b]
                        pe.matmul(S[:, 0:n], q_part(h, a)[:, qt * P:qt * P + P], k[:, 0:n],
                                  start=(a + b == 0), stop=False, skip_group_check=True)
                    add(h, qt, n, S).then_inc(s["s"], 1)
                if LAG <= u < NU + LAG:
                    w = u - LAG
                    pe.wait_ge(s["exp"], s["u0"] + w + 1)
                    if w >= 2:
                        pe.wait_ge(s["pt"], s["u0"] + w - 1)
                    for kt in range(UNITS[w][1] + 1):
                        mm = pe.transpose(bank[2 + w % 2][:, kt * P:kt * P + P], pr[:, w % 4, kt * P:kt * P + P], ident[:, :])
                    mm.then_inc(s["tr"], 1)
                if u >= LAG + 2:
                    w = u - LAG - 2
                    h, qt = UNITS[w]
                    pe.wait_ge(s["pt"], s["u0"] + w + 1)
                    if w >= 2:
                        pe.wait_ge(s["out"], s["u0"] + w - 1)
                    for kt in range(qt + 1):
                        mm = pe.matmul(bank[4 + w % 2][:, 0:HD], pt[:, w % 2, kt * P:kt * P + P], v[:, kt, h * HD:h * HD + HD],
                                       start=(kt == 0), stop=(kt == qt))
                    mm.then_inc(s["pv"], 1)

        def act_attention(act, s, pr, pt, mx, sm, after=None):
            for u in range(NU + LAG):
                if u < NU:
                    n = UNITS[u][1] * P + P
                    act.wait_ge(s["max"], s["u0"] + u + 1)
                    if u >= 4:
                        act.wait_ge(s["tr"], s["u0"] + u - 3)
                    act.activation(pr[:, u % 4, 0:n], bank[S_BANK[u % 4]][:, 0:n], ACT.Exp, bias=mx[:, u:u + 1],
                                   accum_out=sm[:, u:u + 1]).then_inc(s["exp"], 1)
                    if after:
                        after(u)
                if u >= LAG:
                    w = u - LAG
                    n = UNITS[w][1] * P + P
                    act.wait_ge(s["tr"], s["u0"] + w + 1)
                    if w >= 2:
                        act.wait_ge(s["pv"], s["u0"] + w - 1)
                    act.activation(pt[:, w % 2, 0:n], bank[2 + w % 2][:, 0:n], ACT.Copy).then_inc(s["pt"], 1)

        def dve_attention(dve, s, mx, sm, rec, write, after=None):
            for u in range(NU + LAG + 3):
                if u < NU:
                    n = UNITS[u][1] * P + P
                    dve.wait_ge(s["s"], s["u0"] + u + 1)
                    dve.tensor_reduce(mx[:, u:u + 1], bank[S_BANK[u % 4]][:, 0:n], AX, ALU.max, negate=True).then_inc(s["max"], 1)
                if u >= LAG + 3:
                    w = u - LAG - 3
                    h, qt = UNITS[w]
                    dve.wait_ge(s["pv"], s["u0"] + w + 1)
                    dchain(dve, dve.reciprocal(rec[:, w:w + 1], sm[:, w:w + 1]))
                    write(w, h, qt, bank[4 + w % 2][:, 0:HD], rec[:, w:w + 1]).then_inc(s["out"], 1)
                if u < NU and after:
                    after(u)
            dve.wait_ge(s["out"], s["u0"] + NU)

        def att_bias_load(act, h):
            src = T["rel_rows"]
            ap = bass.AP(src.tensor, h * REL, [[1, P], [1, SEQ]])
            act.dma_start(abt[:, h % 2], ap).then_inc(bt_ld[h % 2], 16)

        def att_pe(pe):
            def ready(h):
                pe.wait_ge(a_sem["bt"], h + 1)
                pe.wait_ge(a_sem["qsplit"], h + 1)
                pe.wait_ge(a_sem["split"], h // 2 + 1)

            def add(h, qt, n, S):
                if h == 0 and qt == 1:
                    pe.wait_ge(TS["in_att_in"]["bank_free"], 8 + 24)
                for part in range(2):
                    mm = pe.matmul(S[:, 0:n], revr[:, :], abt_parts[:, h % 2, part, SEQ - n:SEQ], start=False, stop=(part == 1),
                                   skip_group_check=True)
                return mm
            pe_attention(pe, a_sem, akl, av, aP, aPT, ready, add)

        def att_act(act):
            def after(u):
                h, qt = UNITS[u]
                if qt == ST - 1 and h + 2 < HEADS:
                    act.wait_ge(a_sem["bt"], h + 1)
                    att_bias_load(act, h + 2)
            act_attention(act, a_sem, aP, aPT, a_max, a_sum, after)

        def att_dve(dve):
            def bt(h):
                dve.wait_ge(bt_ld[h % 2], 16 * (h // 2) + 16)
                dchain(dve, dve.memset(abt[CH:P, h % 2, SEQ - CH:SEQ], NEG))
                if h >= 2:
                    dve.wait_ge(a_sem["s"], 4 * (h - 1))
                dve_split(dve, abt_parts[:, h % 2, 0], abt_parts[:, h % 2, 1], abt[:, h % 2], a_sem["bt"])

            def split_k(i):
                dve_split(dve, k_high(i), akl[:, i], ak[:, i], a_sem["split"])

            dchain(dve, dve.tensor_copy(revr[:, :], rev[:, :]))
            bt(0)
            dve.wait_ge(TS["in_att_in"]["bank_free"], 8 + 16)
            dve.wait_ge(w_used, base["att_in"] + 2 * 6 - 1)
            dve_zeros(dve)
            dve_split_q(dve, a_sem, aq, 0)
            split_k(0)
            split_k(1)
            dve.wait_ge(TS["in_att_in"]["bank_free"], 8 + 24)

            def after(u):
                h, qt = UNITS[u]
                if qt == 0 and h + 1 < HEADS:
                    dve_split_q(dve, a_sem, aq, h + 1)
                if qt == 1 and h + 1 < HEADS:
                    bt(h + 1)
                if qt == 2 and h % 2 == 0 and h // 2 + 2 < KT:
                    split_k(h // 2 + 2)

            def write(w, h, qt, o, r):
                return dve.tensor_scalar(tok[:, qt, h * HD:h * HD + HD], o, r, None, ALU.mult)
            dve_attention(dve, a_sem, a_max, a_sum, a_rec, write, after)
            dve.sem_inc(TS["mid_att_out"]["tok_ready"], 1)

        def fox_gate_pe(pe):
            pe.wait_ge(f_sem["lohi"], 2)
            for k in range(KT):
                for q, (a, b) in enumerate([(0, 0), (0, 1), (1, 0)]):
                    mm = pe.matmul(bank[0][:, :], flohi[:, b, k, :], xT[:, a, k, :], start=(k == 0 and q == 0),
                                   stop=(k == KT - 1 and q == 2))
            mm.then_inc(f_sem["fl"], 1)

        def fox_pe(pe):
            s = f_sem
            pe.wait_ge(TS["in_odd_in"]["bank_free"], 8 + 28)
            fox_gate_pe(pe)
            for i in range(2 * KT):
                pe.wait_ge(s["sq"], i + 1)
                if i >= 2:
                    pe.wait_ge(s["rs"], i - 1)
                pe.matmul(bank[2 + i % 2][:, :], bones[:, :], fPT[:, i % 2], start=True, stop=True).then_inc(s["ms"], 1)
            pe.wait_ge(s["cum"], 2)
            pe.wait_ge(TS["in_odd_in"]["bank_free"], 8 + 32)
            def add(h, qt, n, S):
                pe.matmul(S[:, 0:n], fsel[:, h:h + 1].broadcast_to([P, P]), fncum[:, 0:n], start=False, stop=False,
                          skip_group_check=True)
                return pe.matmul(S[:, n - P:n], eyer[:, :], cmaskr[:, :], start=False, stop=True, skip_group_check=True)
            def ready(h):
                pe.wait_ge(s["qsplit"], h + 1)
                pe.wait_ge(s["qk"], h // 2 + 1)
            pe_attention(pe, s, fkl, fv, fP, fPT, ready, add)

        def fox_act(act):
            s = f_sem
            def squares(i):
                act.activation(fPT[:, i % 2], (fq, fk)[i % 2][:, i // 2], ACT.Square).then_inc(s["sq"], 1)

            def gates():
                act.wait_ge(s["fl"], 1)
                act.wait_ge(s["bf"], 16)
                z = bank[0][0:HEADS, :]
                act.activation(fcum[:, :], z, ACT.Identity, bias=fbf[:, 0:1]).then_inc(s["z"], 1)
                achain(act, act.activation(ft[:, :], z, ACT.Abs, bias=fbf[:, 0:1]))
                achain(act, act.activation(ft[:, :], ft[:, :], ACT.Exp, scale=-1.0))
                act.activation(ft[:, :], ft[:, :], ACT.Ln, bias=1.0).then_inc(s["sp"], 1)

            squares(0)
            squares(1)
            gates()
            for i in range(2 * KT):
                act.wait_ge(s["ms"], i + 1)
                if i >= 4:
                    act.wait_ge(s["normed"], i - 3)
                act.activation(fP[:, i % 4], bank[2 + i % 2][:, :], ACT.Ln, scale=1.0 / HD, bias=RMS_EPS).then_inc(s["ln"], 1)
                if i + 2 < 2 * KT:
                    squares(i + 2)
                act.wait_ge(s["ln"], i + 1)
                act.activation(fP[:, i % 4], fP[:, i % 4], ACT.Exp, scale=-0.5).then_inc(s["rs"], 1)
            act_attention(act, s, fP, fPT, f_max, f_sum)

        def fox_dve(dve):
            s = f_sem
            dve.wait_ge(s["z"], 1)
            dchain(dve, dve.tensor_scalar(fcum[:, :], fcum[:, :], 0.0, None, ALU.min))
            dve.wait_ge(s["sp"], 1)
            dve.tensor_tensor(ft[:, :], fcum[:, :], ft[:, :], ALU.subtract).then_inc(s["la"], 1)
            dve.wait_ge(s["la"], 1)
            dve.tensor_tensor_scan(fcum[:, :], ones[0:HEADS, 0:1].broadcast_to([HEADS, SEQ]), ft[:, :], 0.0, ALU.mult, ALU.add)\
               .then_inc(s["cum"], 1)
            dve.wait_ge(s["cum"], 1)
            hi, lo = slice(0, HEADS), slice(32, 32 + HEADS)
            dchain(dve, dve.memset(fncum[:, :].bitcast(F32), 0.0))
            dchain(dve, dve.tensor_scalar(fncum[hi, :], fcum[:, :], -1.0, None, ALU.mult))
            dchain(dve, dve.scalar_tensor_tensor(fncum[lo, :], fcum[:, :], -1.0, fncum[hi, :].bitcast(F32), ALU.mult, ALU.subtract))
            dchain(dve, dve.tensor_tensor(fsel[:, :], ident[:, hi], ident[:, lo], ALU.add))
            dchain(dve, dve.tensor_copy(eyer[:, :], ident[:, :]))
            dve.tensor_copy(cmaskr[:, :], cmask[:, :]).then_inc(s["cum"], 1)
            dchain(dve, dve.tensor_scalar(qg8[:, :], col("fox_qnorm_g_2"), HD ** -0.5, None, ALU.mult))
            dve.wait_ge(s["fl"], 1)
            dve_zeros(dve)
            for i in range(2 * KT):
                f = i // 2
                t = (fq, fk)[i % 2][:, f]
                g = (qg8[:, 0:1], col("fox_knorm_g_2"))[i % 2]
                dve.wait_ge(s["rs"], i + 1)
                dve.scalar_tensor_tensor(t, t, g, fP[:, i % 4], ALU.mult, ALU.mult).then_inc(s["normed"], 1)
                dve.wait_ge(s["normed"], i + 1)
                if i == 0:
                    dve_split_q(dve, s, fq, 0)
                if i % 2:
                    dve_split(dve, k_high(f), fkl[:, f], t, s["qk"])

            def after(u):
                h, qt = UNITS[u]
                if qt == 0 and h + 1 < HEADS:
                    dve_split_q(dve, s, fq, h + 1)

            def write(w, h, qt, o, r):
                t = tok[:, qt, h * HD:h * HD + HD]
                return dve.scalar_tensor_tensor(t, o, r, t, ALU.mult, ALU.mult)
            dve_attention(dve, s, f_max, f_sum, f_rec, write, after)
            dve.sem_inc(TS["mid_odd_out"]["tok_ready"], 1)

        h_sem = {n: sem("hgrn_" + n) for n in ("lb", "lbe", "f", "logf", "cum", "zero", "diff", "E", "qk", "s", "at", "end", "ex",
                                               "qke", "keT", "keTs", "kv", "state", "o", "ss", "out", "pool", "po", "pout", "pw")}
        NL = len(LEVELS)
        ITEMS = [(h, lv) for h in range(4) for lv in range(NL + 1)]
        PO_BANK = (2, 3, 4, 5)

        def hgrn_kv(h, n):
            at = n // 2 * P
            return bank[4 + 2 * (h % 2) + n % 2][:, at:at + P]

        def level_of(it):
            return ITEMS[it][0] * NL + ITEMS[it][1] - 1

        def halves_of(ap, lv):
            v = ap.rearrange("p (n two h) -> p n two h", two=2, h=LEVELS[lv - 1])
            return v[:, :, 0, :], v[:, :, 1, :]

        def hgrn_pe(pe):
            s = h_sem
            for it, (h, lv) in enumerate(ITEMS):
                if lv == 0:
                    pe.wait_ge(s["f"], h + 1)
                    kk, qq = hk[:, h], hq[:, h]
                else:
                    j = level_of(it)
                    pe.wait_ge(s["qk"], 2 * j + 2)
                    kk = qq = hX(j % 3)
                if it >= 3:
                    pe.wait_ge(s["at"], it - 2)
                for c in range(ST):
                    cc = slice(c * P, c * P + P)
                    mm = pe.matmul(bank[it % 3][:, cc], kk[:, cc], qq[:, cc], start=True, stop=True)
                mm.then_inc(s["s"], 1)

            def turned(h):
                pe.wait_ge(s["qke"], 2 * h + 2)
                if h:
                    pe.wait_ge(s["keTs"], h)
                for c in range(ST):
                    mm = pe.transpose(bank[3][:, c * P:c * P + P], hke(h % 2)[:, c * P:c * P + P], ident[:, :])
                mm.then_inc(s["keT"], 1)

            def chunk_states(h):
                pe.wait_ge(s["keTs"], h + 1)
                if h >= 2:
                    pe.wait_ge(s["state"], h - 1)
                for n in range(NC - 1):
                    r = slice((n % 2) * CH, (n % 2) * CH + CH)
                    mm = pe.matmul(hgrn_kv(h, n), hkeT(h % 2)[r, n // 2 * P:n // 2 * P + P], hv[r, n // 2, h * P:h * P + P],
                                   start=True, stop=True)
                mm.then_inc(s["kv"], 1)

            def output(h):
                if h == 0:
                    pe.wait_ge(s["at"], len(ITEMS))
                pe.wait_ge(s["state"], h + 1)
                if h >= 2:
                    pe.wait_ge(s["out"], 4 * (h - 1))
                for c in range(ST):
                    o = bank[h % 2][:, c * P:c * P + P]
                    mm = pe.matmul(o, hAT[:, h, c, :], hv[:, c, h * P:h * P + P], start=True, stop=False, skip_group_check=True)
                    for n in (2 * c, 2 * c + 1):
                        if n == 0:
                            continue
                        r = slice((n % 2) * CH, (n % 2) * CH + CH)
                        mm = pe.matmul(o[r, :], hqe(h % 2)[:, n * CH:n * CH + CH], hst[:, h % 2, n, :], start=False, stop=True,
                                       skip_group_check=True)
                mm.then_inc(s["o"], 1)

            def pooled(g):
                pe.wait_ge(s["pool"], g + 1)
                for t in range(ST):
                    mm = pe.matmul(bank[PO_BANK[g]][:, t * P:t * P + P], pools(g)[:, t * P:t * P + P], pw[:, g, :],
                                   start=True, stop=True)
                mm.then_inc(s["po"], 1)

            turned(0)
            chunk_states(0)
            for h in range(1, 4):
                turned(h)
                chunk_states(h)
                output(h - 1)
            pe.wait_ge(s["pw"], 16)
            for g in range(4):
                pooled(g)
            output(3)

        def hgrn_act_gates(act):
            s = h_sem
            act.wait_ge(s["lb"], 1)
            act.activation(lbe[:, :, :], lbe[:, :, :], ACT.Exp).then_inc(s["lbe"], 1)
            for h in range(4):
                act.wait_ge(s["f"], h + 1)
                act.activation(hf[:, h], hf[:, h], ACT.Ln).then_inc(s["logf"], 1)

        def hgrn_act(act):
            s = h_sem
            for j in range(4 * NL):
                act.wait_ge(s["diff"], 2 * j + 2)
                act.activation(hE(j % 3), hE(j % 3), ACT.Exp).then_inc(s["E"], 1)

            def exps(h):
                act.wait_ge(s["end"], h + 1)
                act.activation(hEk(h % 2), hEk(h % 2), ACT.Exp).then_inc(s["ex"], 1)
                act.activation(hEq(h % 2), hf[:, h], ACT.Exp).then_inc(s["ex"], 1)
                act.activation(hdec[:, h], hf[:, h, CH - 1::CH], ACT.Exp).then_inc(s["ex"], 1)

            def keys(h):
                act.wait_ge(s["keT"], h + 1)
                if h >= 2:
                    act.wait_ge(s["kv"], h - 1)
                act.activation(hkeT(h % 2), bank[3][:, :], ACT.Copy).then_inc(s["keTs"], 1)

            def squares(h):
                act.wait_ge(s["o"], h + 1)
                for c in range(ST):
                    achain(act, act.activation(hjunk[:, :], bank[h % 2][:, c * P:c * P + P], ACT.Square,
                                               accum_out=hss[:, h, c:c + 1]))
                act_inverse_root(act, hrs[:, h], hss[:, h], sd[:, :], 1.0 / P, RMS_EPS).then_inc(s["ss"], 1)

            exps(0)
            exps(1)
            keys(0)
            exps(2)
            keys(1)
            squares(0)
            exps(3)
            keys(2)
            squares(1)
            keys(3)
            squares(2)
            squares(3)

        def hgrn_dve(dve):
            s = h_sem
            r = [col("hgrn_lb_2", 4 * i, 4) for i in range(3)]
            dchain(dve, dve.tensor_tensor(lbm[:, :], r[0], r[1], ALU.max))
            dchain(dve, dve.tensor_tensor(lbm[:, :], lbm[:, :], r[2], ALU.max))
            for i in range(3):
                dchain(dve, dve.tensor_tensor(lbe[:, i], r[i], lbm[:, :], ALU.subtract))
            dve.sem_inc(s["lb"], 1)
            dve.wait_ge(s["lbe"], 1)
            dchain(dve, dve.tensor_tensor(lbm[:, :], lbe[:, 0], lbe[:, 1], ALU.add))
            dchain(dve, dve.tensor_tensor(lbm[:, :], lbm[:, :], lbe[:, 2], ALU.add))
            dchain(dve, dve.reciprocal(lbm[:, :], lbm[:, :]))
            dchain(dve, dve.tensor_tensor(lb[:, :], lbe[:, 0], lbm[:, :], ALU.mult))
            dchain(dve, dve.tensor_scalar(omlb[:, :], lb[:, :], -1.0, 1.0, ALU.mult, ALU.add))
            dve.wait_ge(TS["in_even_in"]["bank_free"], 8 + 8)
            for h in range(4):
                dchain(dve, dve.tensor_scalar(hf[:, h], hf[:, h], omlb[:, h:h + 1], lb[:, h:h + 1], ALU.mult, ALU.add))
                dve.tensor_scalar(hk[:, h], hf[:, h], -1.0, 1.0, ALU.mult, ALU.add).then_inc(s["f"], 1)
            dchain(dve, dve.memset(hreset[:, :], 1.0))
            dchain(dve, dve.memset(hreset[:, 0::CH], 0.0))
            dve.memset(hAT[:, :, :, :], 0.0).then_inc(s["zero"], 1)
            for h in range(4):
                dve.wait_ge(s["logf"], h + 1)
                dve.tensor_tensor_scan(hf[:, h], hreset[:, :], hf[:, h], 0.0, ALU.mult, ALU.add).then_inc(s["cum"], 1)
            dve.wait_ge(s["zero"], 1)
            dve.wait_ge(s["cum"], 4)
            dve.wait_ge(w_used, base["even_in"] + 2 * 6 - 1)

            def diff(it):
                h, lv = ITEMS[it]
                j = level_of(it)
                first, second = halves_of(hf[:, h], lv)
                m = first[:, :, LEVELS[lv - 1] - 1:].broadcast_to(list(first.shape))
                e1, e2 = halves_of(hE(j % 3), lv)
                if j >= 3:
                    dve.wait_ge(s["qk"], 2 * j - 4)
                dve.tensor_tensor(e1, m, first, ALU.subtract).then_inc(s["diff"], 1)
                dve.tensor_tensor(e2, second, m, ALU.subtract).then_inc(s["diff"], 1)

            def scaled(it):
                h, lv = ITEMS[it]
                j = level_of(it)
                dve.wait_ge(s["E"], j + 1)
                if j >= 3:
                    dve.wait_ge(s["s"], [i for i, x in enumerate(ITEMS) if x[1] and level_of(i) == j - 3][0] + 1)
                (k1, _), (_, q2), (e1, e2), (x1, x2) = (halves_of(a, lv) for a in (hk[:, h], hq[:, h], hE(j % 3), hX(j % 3)))
                dve.tensor_tensor(x1, k1, e1, ALU.mult).then_inc(s["qk"], 1)
                dve.tensor_tensor(x2, q2, e2, ALU.mult).then_inc(s["qk"], 1)

            def take(it):
                h, lv = ITEMS[it]
                dve.wait_ge(s["s"], it + 1)
                if it:
                    dve.wait_ge(s["at"], it)
                m = ident[:, :] if lv == 0 else lmask[:, lv - 1, :]
                m = m.bitcast(U32).unsqueeze(1).broadcast_to([P, ST, P])
                dve.copy_predicated(hAT[:, h], m, bank[it % 3][:, :].rearrange("p (c t) -> p c t", c=ST)).then_inc(s["at"], 1)

            for t in range(len(ITEMS) + 3):
                if t < len(ITEMS) and ITEMS[t][1]:
                    diff(t)
                if t >= 3:
                    take(t - 3)
                if 1 <= t <= len(ITEMS) and ITEMS[t - 1][1]:
                    scaled(t - 1)

            def end(h):
                c3 = hf[:, h].rearrange("p (n c) -> p n c", c=CH)
                if h >= 2:
                    dve.wait_ge(s["qke"], 2 * h - 2)
                dve.tensor_tensor(hEk(h % 2).rearrange("p (n c) -> p n c", c=CH), c3[:, :, CH - 1:].broadcast_to([P, NC, CH]),
                                  c3, ALU.subtract).then_inc(s["end"], 1)

            def ends(h):
                dve.wait_ge(s["ex"], 3 * h + 3)
                if h >= 2:
                    dve.wait_ge(s["o"], h - 1)
                    dve.wait_ge(s["keT"], h - 1)
                dve.tensor_tensor(hke(h % 2), hk[:, h], hEk(h % 2), ALU.mult).then_inc(s["qke"], 1)
                dve.tensor_tensor(hqe(h % 2), hq[:, h], hEq(h % 2), ALU.mult).then_inc(s["qke"], 1)

            def states(h):
                dve.wait_ge(s["kv"], h + 1)
                for n in range(1, NC):
                    kv = hgrn_kv(h, n - 1)
                    if n == 1:
                        dchain(dve, dve.tensor_copy(hst[:, h % 2, 1], kv))
                    else:
                        dchain(dve, dve.scalar_tensor_tensor(hst[:, h % 2, n], hst[:, h % 2, n - 1], hdec[:, h, n - 1:n], kv,
                                                             ALU.mult, ALU.add))
                dve.sem_inc(s["state"], 1)

            def written(h):
                dve.wait_ge(s["ss"], h + 1)
                for c in range(ST):
                    t = tok[:, c, h * P:h * P + P]
                    dve.scalar_tensor_tensor(t, bank[h % 2][:, c * P:c * P + P], hrs[:, h, c:c + 1], t, ALU.mult, ALU.mult)\
                       .then_inc(s["out"], 1)

            def pool(g):
                u, w, o = hu[:, g], POOLS[g], pools(g)
                dchain(dve, dve.tensor_tensor_scan(pool_sum, ones[:, 0:1].broadcast_to([P, SEQ]), u, 0.0, ALU.mult, ALU.add))
                dchain(dve, dve.tensor_tensor(o[:, w:], pool_sum[:, w:], pool_sum[:, :SEQ - w], ALU.subtract))
                dchain(dve, dve.tensor_tensor(o[:, 0:w], pool_sum[:, 0:w], rcnt[:, 0:w], ALU.mult))
                dchain(dve, dve.tensor_tensor(o[:, 0:w], o[:, 0:w], u[:, 0:w], ALU.subtract))
                dve.scalar_tensor_tensor(o[:, w:], o[:, w:], 1.0 / w, u[:, w:], ALU.mult, ALU.subtract).then_inc(s["pool"], 1)
                dve.wait_ge(s["pool"], g + 1)

            def pool_written(g):
                dve.wait_ge(s["po"], g + 1)
                for c in range(ST):
                    t = tok[:, c, COLS + g * P:COLS + g * P + P]
                    dve.tensor_tensor(t, bank[PO_BANK[g]][:, c * P:c * P + P], t, ALU.mult).then_inc(s["pout"], 1)

            dve.wait_ge(TS["in_even_in"]["bank_free"], 8 + 24)
            end(0)
            end(1)
            ends(0)
            pool(0)
            ends(1)
            end(2)
            states(0)
            pool(1)
            ends(2)
            end(3)
            states(1)
            written(0)
            pool(2)
            ends(3)
            states(2)
            written(1)
            pool(3)
            states(3)
            written(2)
            for g in range(4):
                pool_written(g)
            written(3)
            dve.wait_ge(s["out"], 16)
            dve.wait_ge(s["pout"], 16)
            dve.sem_inc(TS["mid_even_out"]["tok_ready"], 1)

        block = ctx.enter_context(nc.Block())

        @block.sync
        def _(sp):
            sp.dma_start(vrow[:, :, :], T["vec_rows"].rearrange("(t p) n -> p t n", p=P)).then_inc(vec_ld, 16)
            for k in range(KT):
                if k == RING:
                    sp.dma_start(x[:, :, :], T["x"][0].rearrange("(s p) d -> p s d", p=P)).then_inc(x_ld, 16)
                if k >= RING:
                    sp.wait_ge(ada0_used, k - RING + 1)
                sp.dma_start(ring_s[:, k % RING], ADA[0][:, k, 0:2 * D]).then_inc(ada0_ld[k % RING], 16)
            for h in range(2):
                sp_half(sp, h, h, W["gla_in"][:, HK * h:HK * h + HK, 0:COLS], peel=True)
            sp.dma_start(w16[:, :, :], W["gla_in"][:, :, 6 * COLS:6 * COLS + GLA_R]).then_inc(w16_ld, 16)
            sp.dma_start(wgk2[:, :], T["gla_w_gk2"][0]).then_inc(gk2_ld, 16)
            for r, (gate, piece) in enumerate([(gate1, 2), (gate2, 5)]):
                sp.dma_start(gate[:, :], T["b_ada"][0, piece * D:piece * D + D].partition_broadcast(P)).then_inc(gate_ld, 16)
            w = W["gla_in"]

            def ada0_tile(g):
                sp.wait_ge(ada0_used, KT + g - RING + 1)
                at = 2 * D + g // KT * COLS
                sp.dma_start(ring0[:, g % RING], ADA[0][:, g % KT, at:at + COLS]).then_inc(ada0_ld[g % RING], 16)
            for g in range(2):
                ada0_tile(g)
            for j in range(2, 12):
                p, h = divmod(j, 2)
                sp_half(sp, j, h, w[:, HK * h:HK * h + HK, p * COLS:p * COLS + COLS])
                for g in range(6 * j - 10, 6 * j - 4 if j < 11 else 8 * KT):
                    ada0_tile(g)
            sp_panels(sp, "gla_out", 2)
            sp.wait_ge(TS["mid_gla_out"]["xT_ready"], TS["mid_gla_out"]["k0"] + KT)
            sp_lnrow(sp, 0, 0)
            sp_ff(sp, 0, ADA[1].unsqueeze(2), [T["b_ada"][1, i * D:i * D + D] for i in (2, 5)])
            sp.wait_ge(x_new, 1)
            sp_lnrow(sp, 0, 1)
            sp_panels(sp, "att_in", 6)
            sp_panels(sp, "att_out", 2)
            sp.wait_ge(TS["mid_att_out"]["xT_ready"], TS["mid_att_out"]["k0"] + KT)
            sp_lnrow(sp, 1, 0)
            sp_ff(sp, 1, T["ada_w_2"].rearrange("l (k p) n -> p k l n", p=P),
                  [T["ada_b_2"][l, 2 * D:3 * D] for l in range(DEPTH)])
            sp.wait_ge(x_new, 3)
            sp_lnrow(sp, 1, 1)
            sp_panels(sp, "even_in", 6)
            sp.wait_ge(x_new, 4)
            sp.dma_start(pw[:, :, :], T["pool_w_2"][0].rearrange("g c d -> c g d")).then_inc(h_sem["pw"], 16)
            sp_panels(sp, "even_out", 2)
            sp.wait_ge(TS["mid_even_out"]["xT_ready"], TS["mid_even_out"]["k0"] + KT)
            sp.dma_start(fbf[:, :], T["fox_b_f_2"][0].unsqueeze(1)).then_inc(f_sem["bf"], 16)
            sp.dma_start(w16[:, :, :], W["odd_in"][:, :, 4 * D:4 * D + HEADS]).then_inc(w16_ld, 16)
            sp_panels(sp, "odd_in", 8)
            sp_panels(sp, "odd_out", 2)
            for t in range(ST):
                sp.wait_ge(out_ready, t + 1)
                sp.dma_start(out[0, t * P:t * P + P], x[:, t]).then_inc(st_out, 16)
            sp.wait_ge(st_out, 16 * ST)

        @block.gpsimd
        def _(pool):
            def made(ins):
                ins.then_inc(const_made, 1)
            for buf, v in [(ones, 1.0), (ident, 0.0)]:
                made(pool.memset(buf[:, :], v))
            pool.wait_ge(const_made, 2)
            made(pool.affine_select(out=ident[:, :], in_=ident[:, :], compare_op=ALU.not_equal, fill=1.0, base=0,
                                    pattern=[[-1, P]], channel_multiplier=1))
            for buf, v in [(gmask, 1.0), (cmask, 0.0), (rev, 0.0), (bones, 0.0)]:
                made(pool.memset(buf[:, :], v))
            made(pool.memset(lmask[:, :, :], 0.0))
            for i in range(max(POOLS)):
                made(pool.memset(rcnt[:, i:i + 1], 1.0 / (i + 1)))
            pool.wait_ge(const_made, 8 + max(POOLS))
            made(pool.affine_select(out=gmask[:, :], in_=gmask[:, :], compare_op=ALU.is_gt, fill=0.0, base=0,
                                    pattern=[[-1, P]], channel_multiplier=1))
            made(pool.affine_select(out=cmask[:, :], in_=cmask[:, :], compare_op=ALU.is_ge, fill=NEG, base=0,
                                    pattern=[[-1, P]], channel_multiplier=1))
            made(pool.affine_select(out=rev[:, :], in_=rev[:, :], compare_op=ALU.not_equal, fill=1.0, base=1 - P,
                                    pattern=[[1, P]], channel_multiplier=1))
            for n, r in enumerate((slice(0, HD), slice(HD, P))):
                pool.wait_ge(const_made, 11 + max(POOLS) + n)
                made(pool.memset(bones[r, r], 1.0))
            halves = [lmask[:, i, :].rearrange("p (n two h) -> p n two h", two=2, h=h)[:, :, 1, :] for i, h in enumerate(LEVELS)]
            pool.wait_ge(const_made, 13 + max(POOLS))
            for v in halves:
                made(pool.memset(v, 1.0))
            n = 13 + max(POOLS)
            for i, (h, v) in enumerate(zip(LEVELS, halves)):
                pool.wait_ge(const_made, n + len(LEVELS))
                made(pool.affine_select(out=v, in_=v, compare_op=ALU.is_ge, fill=0.0, base=0,
                                        pattern=[[-2 * h, P // (2 * h)], [0, h]], channel_multiplier=1))
            pool.wait_ge(const_made, n + 2 * len(LEVELS))
            for i, (h, v) in enumerate(zip(LEVELS, halves)):
                made(pool.affine_select(out=v, in_=v, compare_op=ALU.is_ge, fill=0.0, base=h - 1,
                                        pattern=[[2 * h, P // (2 * h)], [0, h]], channel_multiplier=-1))

            def low(i, slot):
                pool.wait_ge(hi_made, 2 * i + slot + 1)
                pool.tensor_tensor(wsp[:, slot, 1], raw[:, slot], wsp[:, slot, 0].bitcast(F32), ALU.subtract)\
                    .then_inc(lo_made, 1)
            with pool.Fori(0, J // 2) as i:
                for slot in range(2):
                    low(i, slot)

        LN_EXP = "natural_log_exp_and_others"
        scale_at = lambda k: scol[:, k:k + 1]
        bias_at = lambda k: bcol[:, k:k + 1]

        @block.scalar
        def _(act):
            act.preload_act_table_set(LN_EXP)
            act.wait_ge(vtr_done, 1)
            act.activation(cols[:, :], bank[0][:, 0:NV * P], ACT.Copy).then_inc(cols_made, 1)
            act.wait_ge(cols_made, 1)
            act.activation(ctmp[:, :], col("c", 0, 16), ACT.Exp, scale=-1.0).then_inc(esil_done, 1)
            for slot in range(2):
                act_high(act, 0, slot, peel=True)
            act.wait_ge(mod_made, 1)
            act_transposed(act, "in_gla_in", scale_at, bias_at)
            for i in range(3):
                def fn(b, t, ps):
                    if i == 0:
                        return act.activation((gq, gk)[b][:, t], ps[:, :], ACT.Copy)
                    return act.activation((gv, gg)[i - 1][:, t, b * COLS:b * COLS + COLS], ps[:, :],
                                          (ACT.Copy, ACT.Silu)[i - 1])
                act_evac(act, "gla_in", "in_gla_in", i, fn)
            act.preload_act_table_set(LN_EXP)
            gla_act(act)
            act_transposed(act, "mid_gla_out", lambda k: col("gla_g_norm", k), None)
            act_out(act, "gla_out")
            for t in range(ST):
                act_normalised(act, "gla_out", t, TS["hid_ff0"]["tok_ready"])
            act_transposed(act, "hid_ff0", scale_at, bias_at)
            act_ff(act, 0)
            for t in range(ST):
                act_normalised(act, "ff0", t, TS["in_att_in"]["tok_ready"])
            act_transposed(act, "in_att_in", scale_at, bias_at)
            act.wait_ge(x_new, 2)
            for h in range(2):
                att_bias_load(act, h)
            for i in range(3):
                def fn(b, t, ps):
                    f = 4 * b + t
                    if i == 0:
                        return act.activation(aq[:, f], ps[:, :], ACT.Identity, scale=HD ** -0.5, bias=bq8[:, f:f + 1])
                    if i == 1:
                        return act.activation(ak[:, f], ps[:, :], ACT.Identity, bias=col("att_b_in", KT + f))
                    return act.activation(av[:, t, b * COLS:b * COLS + COLS], ps[:, :], ACT.Copy)
                act_evac(act, "att_in", "in_att_in", i, fn)
            att_act(act)
            act_transposed(act, "mid_att_out", None, lambda k: col("att_b_in", 2 * KT + k))
            act_out(act, "att_out")
            for t in range(ST):
                act_normalised(act, "att_out", t, TS["hid_ff1"]["tok_ready"])
            act_transposed(act, "hid_ff1", scale_at, bias_at)
            act_ff(act, 1)
            for t in range(ST):
                act_normalised(act, "ff1", t, normed)
                if t:
                    act_rms(act, "even_in", t - 1)
            act_rms(act, "even_in", ST - 1)
            act_transposed(act, "in_even_in", scale_at, bias_at)
            act.wait_ge(x_new, 4)
            for i in range(3):
                def fn(b, t, ps):
                    if i == 0:
                        return act.activation((hq, hf)[b][:, t], ps[:, :], (ACT.Copy, ACT.Sigmoid)[b])
                    if b == 0:
                        return act.activation((hv, hu)[i - 1][:, t], ps[:, :], ACT.Copy)
                    return act.activation(tok[:, t, (i - 1) * COLS:i * COLS], ps[:, :], ACT.Silu)
                act_evac(act, "even_in", "in_even_in", i, fn)
                if i == 1:
                    act.preload_act_table_set(LN_EXP)
                    hgrn_act_gates(act)
            act.preload_act_table_set(LN_EXP)
            hgrn_act(act)
            act_transposed(act, "mid_even_out", lambda k: col("hgrn_onorm_g_2", k) if k < 4 else col("pool_scale_2", k - 4), None)
            act_out(act, "even_out")
            for t in range(ST):
                act_rms(act, "odd_in", t)
            act_transposed(act, "in_odd_in", scale_at, bias_at)
            for i in range(4):
                def fn(b, t, ps):
                    if i < 2:
                        return act.activation((fq, fk)[i][:, 4 * b + t], ps[:, :], ACT.Copy)
                    c = slice(b * COLS, b * COLS + COLS)
                    if i == 2:
                        return act.activation(fv[:, t, c], ps[:, :], ACT.Copy)
                    return act.activation(tok[:, t, c], ps[:, :], ACT.Silu)
                act_evac(act, "odd_in", "in_odd_in", i, fn)
            act.preload_act_table_set(LN_EXP)
            fox_act(act)
            act_transposed(act, "mid_odd_out", None, None)
            act_out(act, "odd_out")

        @block.tensor
        def _(pe):
            pe.wait_ge(vec_ld, 16)
            pe.wait_ge(const_made, 3)
            for t in range(NV):
                mm = pe.transpose(bank[0][:, t * P:t * P + P], vrow[:, t, :], ident[:, :])
            mm.then_inc(vtr_done, 1)
            pe.wait_ge(x_ld, 16)
            pe.wait_ge(cols_made, 1)

            def first_columns():
                pe.wait_ge(ada0_used, KT)
                pe_modcols(pe, acc0, range(16), KT - 1, mod_done)
                pe.wait_ge(mod_made, 1)
            pe_transposes(pe, "in_gla_in", x, before_last=first_columns)
            pe_panels(pe, "gla_in", "in_gla_in", [("TT", 1), ("NN", 2)])
            gla_pe(pe)
            pe_transposes(pe, "mid_gla_out", tok, 1)
            pe_panels(pe, "gla_out", "mid_gla_out", [("NN", 1)])
            pe.wait_ge(var_made, norm0["gla_out"] + ST)
            pe_transposes(pe, "hid_ff0", tok, tile_need=2)
            pe_ff(pe, 0)
            pe.wait_ge(const_made, NCONST)
            pe.wait_ge(mod_made, 8)
            pe.wait_ge(var_made, norm0["ff0"] + ST)
            pe_transposes(pe, "in_att_in", tok, tile_need=1)
            pe_panels(pe, "att_in", "in_att_in", [("TT", 2), ("NN", 1)])
            pe.wait_ge(TS["in_att_in"]["bank_free"], 8 + 20)
            att_pe(pe)
            pe_transposes(pe, "mid_att_out", tok, 1)
            pe_panels(pe, "att_out", "mid_att_out", [("NN", 1)])
            pe.wait_ge(var_made, norm0["att_out"] + ST)
            pe_transposes(pe, "hid_ff1", tok, tile_need=2)
            pe_ff(pe, 1)
            pe.wait_ge(mod_made, 12)
            pe.wait_ge(var_made, norm0["ff1"] + ST)
            pe_transposes(pe, "in_even_in", tok, tile_need=1)
            pe_panels(pe, "even_in", "in_even_in", [("TT", 1), ("NN", 1), ("TN", 1)])
            pe.wait_ge(TS["in_even_in"]["bank_free"], 8 + 20)
            hgrn_pe(pe)
            pe_transposes(pe, "mid_even_out", tok, 1)
            pe_panels(pe, "even_out", "mid_even_out", [("NN", 1)])
            pe.wait_ge(RS["odd_in"]["x"], ST)
            pe_transposes(pe, "in_odd_in", tok, tile_need=1)
            pe_panels(pe, "odd_in", "in_odd_in", [("TT", 2), ("NN", 2)])
            fox_pe(pe)
            pe_transposes(pe, "mid_odd_out", tok, 1)
            pe_panels(pe, "odd_out", "mid_odd_out", [("NN", 1)])

        @block.vector
        def _(dve):
            dve.wait_ge(esil_done, 1)
            dchain(dve, dve.tensor_scalar(ctmp[:, :], ctmp[:, :], 1.0, None, ALU.add))
            dchain(dve, dve.reciprocal(ctmp[:, :], ctmp[:, :]))
            dchain(dve, dve.tensor_tensor(csil[:, :], ctmp[:, :], col("c", 0, 16), ALU.mult))
            for k in range(KT):
                dve_mod_tile(dve, acc0[:, 0:2 * D], ring_s[:, k % RING], k, csil[:, k:k + 1], ada0_ld[k % RING],
                             16 * (k // RING + 1), ada0_used, k)
            dve.wait_ge(mod_done, 1)
            dchain(dve, dve.tensor_tensor(modcol[:, 0:16], bank[KT - 1][:, 0:16], col("b_ada", 0, 16), ALU.add))
            dchain(dve, dve.tensor_copy(bcol[:, :], modcol[:, 0:8]))
            dchain(dve, dve.tensor_scalar(scol[:, :], modcol[:, 8:16], 1.0, None, ALU.add))
            dve.sem_inc(mod_made, 1)
            dve_transposed(dve, "in_gla_in")
            dve.wait_ge(w16_ld, 16)
            dve_w16_split(dve, lohi, lohi_made)
            for g in range(8 * KT):
                at = (2 * D + g // KT * COLS) % (ST * D)
                dve_mod_tile(dve, acc0[:, at:at + COLS], ring0[:, g % RING], g % KT, csil[:, g % KT:g % KT + 1], ada0_ld[g % RING],
                             16 * ((KT + g) // RING + 1), ada0_used, KT + g)

            def rest_of_modulation():
                dve.wait_ge(mod_done, 2)
                dve.tensor_tensor(modcol[:, 24:40], bank[1][:, 24:40], col("b_ada", 24, 16), ALU.add).then_inc(mod_made, 1)
                dve.wait_ge(gate_ld, 32)
                for r, gate in enumerate((gate1, gate2)):
                    dve.wait_ge(mod_done, 3 + r)
                    dve_modrow(dve, gate, 2)
                    dve.sem_inc(mod_made, 1)
            gla_dve(dve, rest_of_modulation)
            dve_transposed(dve, "mid_gla_out")

            def y_and_statistics(name, gate):
                for n in range(2):
                    for t in range(ST):
                        wait_tile(dve, name, n, t)
                        dve_mix(dve, t, n, bank[4 * n + t][:, :], gate)

            def next_modulation(l, bias, plus_one):
                m = 4 + 4 * l
                one = 1.0 if plus_one else 0.0
                dve.wait_ge(mod_done, m + 1)
                dchain(dve, dve.tensor_tensor(modcol[:, :], bank[0][:, 0:48], bias, ALU.add))
                dve.sem_inc(mod_made, 1)
                dve.wait_ge(brow_ld, 32 * l + 32)
                for done, row, halves in ((2, 0, ((0, 1), (1, 2))), (3, 1, ((0, 3),)), (4, 1, ((1, 0),))):
                    dve.wait_ge(mod_done, m + done)
                    for n, bk in halves:
                        g = brow[l][:, row, n * COLS:n * COLS + COLS]
                        dchain(dve, dve.scalar_tensor_tensor(g, bank[bk][:, :], one, g, ALU.add, ALU.add))
                    dve.sem_inc(mod_made, 1)

            def next_gates(l):
                for r, gate in enumerate((gate1, gate2)):
                    dchain(dve, dve.tensor_copy(gate[:, :], brow[l][:, r]))

            def rms_fold(l):
                dchain(dve, dve.tensor_scalar(ctmp[:, 0:8], modcol[:, 24 * l + 8:24 * l + 16], 1.0, None, ALU.add))
                dchain(dve, dve.tensor_tensor(scol[:, :], col("norm_g_2", KT * l, KT), ctmp[:, 0:8], ALU.mult))
                dchain(dve, dve.tensor_copy(bcol[:, :], modcol[:, 24 * l:24 * l + 8]))

            ready = TS["hid_ff0"]["tok_ready"]
            dve_fold(dve, 0, 0, 24, 32)
            dve.sem_inc(ready, 1)
            y_and_statistics("gla_out", gate1)
            dve.wait_ge(ready, ST + 1)
            dve_transposed(dve, "hid_ff0")

            def residual0():
                dve.wait_ge(ln_ld, 32)
                dve_residual(dve, 0, x_new)
            ready = TS["in_att_in"]["tok_ready"]

            def before_last0():
                next_modulation(0, col("b_ada", 48, 48), True)
                dve_fold(dve, 0, 1, 0, 8)
            dve_ff(dve, 0, 0, 1, gate2, residual0, before_last0, lambda t, n: None)
            next_gates(0)
            dve_transposed(dve, "in_att_in")
            dve.wait_ge(ln_ld, 64)
            dchain(dve, dve.tensor_scalar(bq8[:, :], col("att_b_in", 0, KT), HD ** -0.5, None, ALU.mult))
            dve_residual(dve, 0, x_new)
            att_dve(dve)
            dve_transposed(dve, "mid_att_out")
            ready = TS["hid_ff1"]["tok_ready"]
            dve_fold(dve, 1, 0, 24, 32)
            dve.sem_inc(ready, 1)
            y_and_statistics("att_out", gate1)
            dve.wait_ge(ready, ST + 1)
            dve_transposed(dve, "hid_ff1")

            def residual1():
                dve.wait_ge(ln_ld, 96)
                dve_residual(dve, 1, x_new)

            def before_last1():
                next_modulation(1, col("ada_b_2", 0, 48), False)
                rms_fold(0)
                dve.wait_ge(ln_ld, 128)

            def affine1(t):
                dve.wait_ge(normed, t + 1)
                dchain(dve, dve.tensor_tensor(tok[:, t], tok[:, t], lnrow[1][:, 0], ALU.mult))
                dve.tensor_tensor(x[:, t], tok[:, t], lnrow[1][:, 1], ALU.add).then_inc(RS["even_in"]["x"], 1)

            def finish1(t, n):
                if n == 1 and t:
                    affine1(t - 1)
            dve_ff(dve, 1, KT, DEPTH, gate2, residual1, before_last1, finish1)
            affine1(ST - 1)
            next_gates(1)
            dve.sem_inc(x_new, 1)
            dve_transposed(dve, "in_even_in")
            hgrn_dve(dve)
            dve_transposed(dve, "mid_even_out")
            rms_fold(1)

            def gated(name, gate, new):
                for n in range(2):
                    for t in range(ST):
                        c = slice(n * COLS, n * COLS + COLS)
                        wait_tile(dve, name, n, t)
                        dchain(dve, dve.tensor_tensor(tok[:, t, c], bank[4 * n + t][:, :], gate[:, c], ALU.mult))
                        if n == 1:
                            dve.tensor_tensor(x[:, t], x[:, t], tok[:, t], ALU.add).then_inc(new, 1)
                            dve.wait_ge(new, t + 1)
            gated("even_out", gate1, RS["odd_in"]["x"])
            dve.sem_inc(x_new, 1)
            dve_transposed(dve, "in_odd_in")
            dve.wait_ge(w16_ld, 32)
            dve_w16_split(dve, flohi, f_sem["lohi"])
            fox_dve(dve)
            dve_transposed(dve, "mid_odd_out")
            gated("odd_out", gate2, out_ready)

    return nc


_NAMES = ["x", "c", "w_ada", "b_ada", "ln_g", "ln_b", "gla_w_in", "gla_w_gk2", "gla_b_gk", "gla_g_norm", "gla_w_out",
          "att_w_in", "att_b_in", "att_rel_bias", "att_w_out", "ff_w1", "ff_w2", "c_2", "norm_g_2", "ada_w_2", "ada_b_2",
          "hgrn_lb_2", "even_w_in_2", "hgrn_onorm_g_2", "pool_w_2", "pool_scale_2", "even_w_out_2", "odd_w_in_2",
          "fox_b_f_2", "fox_qnorm_g_2", "fox_knorm_g_2", "odd_w_out_2"]


def kernel(**inputs):
    import numpy as np
    import concourse.bacc as bacc
    from concourse.bass_utils import run_bass_kernel_spmd

    nc = bacc.Bacc("TRN2", target_bir_lowering=False, num_devices=1)
    rows = []
    for name in ROWS:
        a = np.ascontiguousarray(inputs[name]).reshape(-1)
        if a.size < P:
            a = np.concatenate([a] * (P // a.size))
        rows.append(a.reshape(-1, P))
    rows = np.concatenate(rows)
    rows = np.concatenate([rows, np.zeros((NV * P - len(rows), P), rows.dtype)])
    rel = np.asarray(inputs["att_rel_bias"])[0]
    rel = rel[:, np.clip(np.arange(SEQ - 1, SEQ - 1 - REL, -1), -MAX_REL, MAX_REL) + MAX_REL]
    arrays, aps = {}, {}
    for name, a in [(n, inputs[n]) for n in _NAMES if n != "att_rel_bias"] + [("vec_rows", rows), ("rel_rows", rel)]:
        a = np.ascontiguousarray(a)
        arrays["in_" + name] = a
        aps[name] = nc.dram_tensor("in_" + name, a.shape, mybir.dt.from_np(a.dtype), kind="ExternalInput").ap()
    out = nc.dram_tensor("out_0", (1, SEQ, D), F32, kind="ExternalOutput").ap()
    build(nc, aps, out)
    r = run_bass_kernel_spmd(nc, [arrays], core_ids=[0])
    return r.results[0]["out_0"]
```
